# Optimizing a Trainium2 kernel written in Bass

```python
import math
import jax, jax.numpy as jnp
from jax import lax
import numpy as np

D_MODEL = 2048
BATCH = 1
SEQ = 256
DEPTH = 2

CHUNK = 64
N_MIXERS = 2
N_RET_LAYERS = (DEPTH + 1) // 2
N_SSD_LAYERS = DEPTH // 2
RMS_EPS = 1e-6

RET_HEAD_DK = 256
RET_HEADS = D_MODEL // RET_HEAD_DK
RET_QK = RET_HEADS * RET_HEAD_DK
RET_HEAD_DV = 2 * RET_HEAD_DK
RET_V = RET_HEADS * RET_HEAD_DV
RET_IN = 2 * RET_QK + 2 * RET_V
ROPE_BASE = 10000.0
GN_EPS = 1e-5

SSD_EXPAND = 2
SSD_D_INNER = SSD_EXPAND * D_MODEL
SSD_HEADDIM = 64
SSD_HEADS = SSD_D_INNER // SSD_HEADDIM
SSD_GROUPS = 8
SSD_HEADS_PER_GROUP = SSD_HEADS // SSD_GROUPS
SSD_STATE = 128
SSD_CONV_W = 4
SSD_CONV_DIM = SSD_D_INNER + 2 * SSD_GROUPS * SSD_STATE
SSD_IN = SSD_D_INNER + SSD_CONV_DIM + SSD_HEADS
SSD_NORM_GROUPS = SSD_GROUPS

D_FF = 4 * D_MODEL

kernel_name = "hybrid_retention_ssd_sandwich_trunk"

def rms_norm(x, w):
    xf = x.astype(jnp.float32)
    y = xf * lax.rsqrt(jnp.mean(xf * xf, axis=-1, keepdims=True) + RMS_EPS)
    return (y * w.astype(jnp.float32)).astype(x.dtype)

def to_chunks(t):
    b, s = t.shape[:2]
    return jnp.moveaxis(t.reshape(b, s // CHUNK, CHUNK, *t.shape[2:]), 1, 0)

def from_chunks(t):
    t = jnp.moveaxis(t, 0, 1)
    return t.reshape(t.shape[0], t.shape[1] * t.shape[2], *t.shape[3:])

def rotary(t, pos):
    half = t.shape[-1] // 2
    inv_freq = ROPE_BASE ** (-jnp.arange(half, dtype=jnp.float32) / half)
    ang = pos.astype(jnp.float32)[:, None] * inv_freq[None, :]
    cos = jnp.cos(ang)[None, :, None, :]
    sin = jnp.sin(ang)[None, :, None, :]
    t1, t2 = t[..., :half], t[..., half:]
    return jnp.concatenate([t1 * cos - t2 * sin, t1 * sin + t2 * cos], axis=-1)

def retention_mixer(u, w_in, gn_w, w_out):
    b, s, _ = u.shape
    f32 = jnp.float32
    proj = u @ w_in
    q, k, v, g = jnp.split(proj, [RET_QK, 2 * RET_QK, 2 * RET_QK + RET_V], axis=-1)
    pos = jnp.arange(s)
    q = rotary(q.astype(f32).reshape(b, s, RET_HEADS, RET_HEAD_DK), pos)
    k = rotary(k.astype(f32).reshape(b, s, RET_HEADS, RET_HEAD_DK), pos) * (RET_HEAD_DK ** -0.5)
    v = v.astype(f32).reshape(b, s, RET_HEADS, RET_HEAD_DV)

    log_gamma = jnp.log1p(-jnp.exp2(-5.0 - jnp.arange(RET_HEADS, dtype=f32)))
    idx = jnp.arange(CHUNK, dtype=f32)
    dist = jnp.abs(idx[:, None] - idx[None, :])
    dmat = jnp.exp(dist[None] * log_gamma[:, None, None])
    xi = jnp.exp((idx[:, None] + 1.0) * log_gamma[None, :])
    zeta = jnp.exp((CHUNK - 1.0 - idx)[:, None] * log_gamma[None, :])
    chunk_decay = jnp.exp(CHUNK * log_gamma)

    def step(state, inp):
        qc, kc, vc = inp
        scores = jnp.einsum('blhd,bmhd->bhlm', qc, kc) * dmat[None]
        inner = jnp.einsum('bhlm,bmhv->blhv', scores, vc)
        cross = jnp.einsum('blhd,bhdv->blhv', qc, state) * xi[None, :, :, None]
        state = state * chunk_decay[None, :, None, None] + jnp.einsum(
            'bmhd,bmhv->bhdv', kc * zeta[None, :, :, None], vc)
        return state, inner + cross

    state0 = jnp.zeros((b, RET_HEADS, RET_HEAD_DK, RET_HEAD_DV), f32)
    _, o = lax.scan(step, state0, (to_chunks(q), to_chunks(k), to_chunks(v)))
    o = from_chunks(o)
    mu = jnp.mean(o, axis=-1, keepdims=True)
    var = jnp.mean(jnp.square(o - mu), axis=-1, keepdims=True)
    o = ((o - mu) * lax.rsqrt(var + GN_EPS)).reshape(b, s, RET_V) * gn_w.astype(f32)
    y = jax.nn.silu(g.astype(f32)) * o
    return y.astype(u.dtype) @ w_out

def causal_depthwise_conv(t, w, bias):
    s = t.shape[1]
    width = w.shape[0]
    tp = jnp.pad(t, ((0, 0), (width - 1, 0), (0, 0)))
    out = bias[None, None, :]
    for tap in range(width):
        out = out + tp[:, tap:tap + s, :] * w[tap][None, None, :]
    return out

def ssd_mixer(u, w_in, conv_w, conv_b, dt_bias, a_log, d_skip, norm_w, w_out):
    b, s, _ = u.shape
    f32 = jnp.float32
    G, R, P, N = SSD_GROUPS, SSD_HEADS_PER_GROUP, SSD_HEADDIM, SSD_STATE
    proj = u @ w_in
    z, xbc, dt = jnp.split(proj, [SSD_D_INNER, SSD_D_INNER + SSD_CONV_DIM], axis=-1)
    xbc = jax.nn.silu(causal_depthwise_conv(xbc, conv_w, conv_b))
    xs, bm, cm = jnp.split(xbc, [SSD_D_INNER, SSD_D_INNER + G * N], axis=-1)
    xs = xs.astype(f32).reshape(b, s, G, R, P)
    bm = bm.astype(f32).reshape(b, s, G, N)
    cm = cm.astype(f32).reshape(b, s, G, N)
    dt = jax.nn.softplus(dt.astype(f32) + dt_bias.astype(f32)).reshape(b, s, G, R)
    a = -jnp.exp(a_log.astype(f32)).reshape(G, R)
    da = dt * a[None, None]
    xdt = xs * dt[..., None]
    tril = jnp.tril(jnp.ones((CHUNK, CHUNK), dtype=bool))

    def step(state, inp):
        xc, ac, bc, cc = inp
        acum = jnp.cumsum(ac, axis=1)
        seg = acum[:, :, None] - acum[:, None, :]
        lmat = jnp.exp(jnp.where(tril[None, :, :, None, None], seg, -jnp.inf))
        cb = jnp.einsum('blgn,bsgn->blsg', cc, bc)
        y_diag = jnp.einsum('blsgr,bsgrp->blgrp', cb[..., None] * lmat, xc)
        y_off = jnp.einsum('blgn,bgrpn->blgrp', cc, state) * jnp.exp(acum)[..., None]
        decay_to_end = jnp.exp(acum[:, -1:] - acum)
        state = state * jnp.exp(acum[:, -1])[..., None, None] + jnp.einsum(
            'bsgn,bsgrp->bgrpn', bc, xc * decay_to_end[..., None])
        return state, y_diag + y_off

    state0 = jnp.zeros((b, G, R, P, N), f32)
    _, ys = lax.scan(step, state0, (to_chunks(xdt), to_chunks(da), to_chunks(bm), to_chunks(cm)))
    y = from_chunks(ys) + d_skip.astype(f32).reshape(G, R)[None, None, :, :, None] * xs
    y = y.reshape(b, s, SSD_D_INNER) * jax.nn.silu(z.astype(f32))
    yg = y.reshape(b, s, SSD_NORM_GROUPS, SSD_D_INNER // SSD_NORM_GROUPS)
    yg = yg * lax.rsqrt(jnp.mean(yg * yg, axis=-1, keepdims=True) + RMS_EPS)
    y = yg.reshape(b, s, SSD_D_INNER) * norm_w.astype(f32)
    return y.astype(u.dtype) @ w_out

def sq_relu_mlp(u, w_up, w_down):
    h = jax.nn.relu(u @ w_up)
    return (h * h) @ w_down

def setup_inputs(seed: int = 0) -> dict:
    key = jax.random.key(seed)
    ks = jax.random.split(key, 20)
    f32 = jnp.float32

    def nrm(k, shape, scale):
        return jax.random.normal(k, shape, f32) * scale

    def gain(k, shape):
        return 1.0 + 0.05 * jax.random.normal(k, shape, f32)

    x = jax.random.normal(ks[0], (BATCH, SEQ, D_MODEL), f32)
    norm_mix_pre = gain(ks[1], (DEPTH, D_MODEL))
    norm_mix_post = gain(ks[2], (DEPTH, D_MODEL))
    norm_ffn_pre = gain(ks[3], (DEPTH, D_MODEL))
    norm_ffn_post = gain(ks[4], (DEPTH, D_MODEL))

    ret_w_in = nrm(ks[5], (N_RET_LAYERS, D_MODEL, RET_IN), D_MODEL ** -0.5)
    ret_gn_w = gain(ks[6], (N_RET_LAYERS, RET_V))
    ret_w_out = nrm(ks[7], (N_RET_LAYERS, RET_V, D_MODEL), RET_V ** -0.5)

    ssd_w_in = nrm(ks[8], (N_SSD_LAYERS, D_MODEL, SSD_IN), D_MODEL ** -0.5)
    ssd_conv_w = nrm(ks[9], (N_SSD_LAYERS, SSD_CONV_W, SSD_CONV_DIM), SSD_CONV_W ** -0.5)
    ssd_conv_b = nrm(ks[10], (N_SSD_LAYERS, SSD_CONV_DIM), 0.02)
    dt0 = jnp.exp(jax.random.uniform(ks[11], (N_SSD_LAYERS, SSD_HEADS), f32,
                                     math.log(1e-3), math.log(1e-1)))
    ssd_dt_bias = dt0 + jnp.log(-jnp.expm1(-dt0))
    ssd_a_log = jnp.log(jax.random.uniform(ks[12], (N_SSD_LAYERS, SSD_HEADS), f32, 1.0, 16.0))
    ssd_d = gain(ks[13], (N_SSD_LAYERS, SSD_HEADS))
    ssd_norm_w = gain(ks[14], (N_SSD_LAYERS, SSD_D_INNER))
    ssd_w_out = nrm(ks[15], (N_SSD_LAYERS, SSD_D_INNER, D_MODEL), SSD_D_INNER ** -0.5)

    mlp_w_up = nrm(ks[16], (DEPTH, D_MODEL, D_FF), D_MODEL ** -0.5)
    mlp_w_down = nrm(ks[17], (DEPTH, D_FF, D_MODEL), D_FF ** -0.5)

    return {"x": x,
            "norm_mix_pre": norm_mix_pre, "norm_mix_post": norm_mix_post,
            "norm_ffn_pre": norm_ffn_pre, "norm_ffn_post": norm_ffn_post,
            "ret_w_in": ret_w_in, "ret_gn_w": ret_gn_w, "ret_w_out": ret_w_out,
            "ssd_w_in": ssd_w_in, "ssd_conv_w": ssd_conv_w, "ssd_conv_b": ssd_conv_b,
            "ssd_dt_bias": ssd_dt_bias, "ssd_a_log": ssd_a_log, "ssd_d": ssd_d,
            "ssd_norm_w": ssd_norm_w, "ssd_w_out": ssd_w_out,
            "mlp_w_up": mlp_w_up, "mlp_w_down": mlp_w_down}

def reference(x, norm_mix_pre, norm_mix_post, norm_ffn_pre, norm_ffn_post,
              ret_w_in, ret_gn_w, ret_w_out,
              ssd_w_in, ssd_conv_w, ssd_conv_b, ssd_dt_bias, ssd_a_log, ssd_d,
              ssd_norm_w, ssd_w_out, mlp_w_up, mlp_w_down):
    h = x
    for i in range(DEPTH):
        j = i // N_MIXERS
        u = rms_norm(h, norm_mix_pre[i])
        if i % N_MIXERS == 0:
            m = retention_mixer(u, ret_w_in[j], ret_gn_w[j], ret_w_out[j])
        else:
            m = ssd_mixer(u, ssd_w_in[j], ssd_conv_w[j], ssd_conv_b[j], ssd_dt_bias[j],
                          ssd_a_log[j], ssd_d[j], ssd_norm_w[j], ssd_w_out[j])
        h = h + rms_norm(m, norm_mix_post[i])
        u = rms_norm(h, norm_ffn_pre[i])
        h = h + rms_norm(sq_relu_mlp(u, mlp_w_up[i], mlp_w_down[i]), norm_ffn_post[i])
    return h


_drawn_inputs = setup_inputs


def setup_inputs(seed=0):
    import zlib

    import numpy as np

    out = dict(_drawn_inputs(seed))
    spreads = {}
    factors = {'ssd_conv_b': 4.194, 'ssd_d': 3.108}
    for name, (base, spread) in spreads.items():
        noise = np.random.default_rng([zlib.crc32(name.encode()), seed]).standard_normal(out[name].shape)
        drawn = base * np.exp(spread * noise) if base else spread * noise
        out[name] = __import__('jax').numpy.asarray(drawn.astype(out[name].dtype))
    for name, factor in factors.items():
        out[name] = (out[name] * factor).astype(out[name].dtype)
    return out
```

```python
from contextlib import ExitStack

import numpy as np

import concourse.bass as bass
from concourse import mybir

ALU = mybir.AluOpType
ACT = mybir.ActivationFunctionType
AX_X = mybir.AxisListType.X
F32 = mybir.dt.float32
F32R = mybir.dt.float32r
BF16 = mybir.dt.bfloat16

P = 128
SEQ = 256
T = SEQ // P
D = 2048
KT = D // P
NB = 512
CH = 8
CK = KT // CH
RAW = 4
SPLIT = 4
LEAD = 3
NBANK = 4
DECAY_CHUNK = 64

HEADS = 8
DK = 256
DV = 512
PAIRS = HEADS // 2
INNER = 4096
GROUPS = 8
SHEADS = 64
HPG = SHEADS // GROUPS
HD = 64
TAPS = 4
CONV_KT = 48
FF_GROUPS = 4
RMS_EPS = 1e-6
GN_EPS = 1e-5

U_RET, U_RET_OUT, U_MLP0, U_SSD, U_SSD_OUT, U_MLP1, U_END = 0, 24, 32, 64, 84, 92, 124
B_RET, B_RET_OUT, B_MLP0, B_SSD, B_SSD_OUT, B_MLP1 = 0, 12, 14, 30, 40, 42
F_COLS, F_PHASE0, F_RET, F_PHASE1, F_MLP0, F_PHASE2 = 0, 1, 9, 73, 81, 113
F_DT, F_BC0, F_DECAY, F_BC1, F_BC2, F_BC3, F_G0, F_G1 = 121, 122, 124, 125, 127, 129, 131, 142
F_GTAIL, F_PHASE3, F_MLP1 = 254, 259, 267
F_PHASE = (F_PHASE0, F_PHASE1, F_PHASE2, F_PHASE3)

COL_PRE = (0, 32, 16, 48)
COL_GN = 64
COL_SN = 96
COL_CONV = 128
NCOLS = COL_CONV + (TAPS + 1) * CONV_KT


class Fill:

    def __init__(self, static, turns=0):
        self.bank = static % NBANK
        self.full = turns * NBANK + (static + 1)
        self.turn = turns + static // NBANK
        self.static, self.turns = static, turns

    def __add__(self, n):
        return Fill(self.static + n, self.turns)


def squares_before(k):
    return 8 * k + (2 * GROUPS if k > 4 else 0)


class Steps:

    def __init__(self):
        self.base, self.n = 0, 0

    def next(self):
        self.n += 1
        return self.base + self.n

    def loop(self, i, per):
        self.start, self.per = self.base + self.n, per
        self.base, self.n = i * per + self.start, 0

    def end(self, times):
        assert self.n == self.per, (self.n, self.per)
        self.base, self.n = self.start + times * self.per, 0


def hybrid_trunk(nc, x, norm_mix_pre, norm_mix_post, norm_ffn_pre, norm_ffn_post, ret_w_in, ret_gn_w,
                 ret_w_out, ssd_w_in, ssd_conv_w, ssd_conv_b, ssd_dt_bias, ssd_a_log, ssd_d, ssd_norm_w,
                 ssd_w_out, mlp_w_up, mlp_w_down, rot_cos, rot_sin, ret_decay, masks, out):
    with ExitStack() as ctx:
        def sb(name, shape, dt=F32):
            return ctx.enter_context(nc.sbuf_tensor(name, shape, dt))

        def sem(name):
            return ctx.enter_context(nc.semaphore(name))

        h = sb("h", [P, T, D])
        ut_hi = sb("ut_hi", [P, KT, SEQ], F32R)
        ut_lo = sb("ut_lo", [P, KT, SEQ], F32R)
        yt_hi = sb("yt_hi", [P, 2 * KT, SEQ], F32R)
        yt_lo = sb("yt_lo", [P, 2 * KT, SEQ], F32R)
        w_raw = sb("w_raw", [P, RAW, CK, NB])
        w_hi = sb("w_hi", [P, SPLIT, CK, NB], F32R)
        w_lo = sb("w_lo", [P, SPLIT, CK, NB], F32R)
        cols = sb("cols", [P, NCOLS])
        mask = sb("mask", [P, 3, P])
        ident, upto, after = mask[:, 0, :], mask[:, 1, :], mask[:, 2, :]
        ssq = sb("ssq", [P, 8, T, 4])
        var = sb("var", [P, 8, T])
        std = sb("std", [P, 8, T])
        rstd = sb("rstd", [P, 8, T])
        bn = sb("bn", [P, 4, 6])
        mv = sb("mv", [P, 4, 2])
        waited = sb("waited", [P, 1])
        head_var = sb("head_var", [P, 4])
        head_std = sb("head_std", [P, 4])
        head_rstd = sb("head_rstd", [P, 4])
        group_ssq = sb("group_ssq", [P, T])
        group_var = sb("group_var", [P, T])
        group_std = sb("group_std", [P, T])
        group_rstd = sb("group_rstd", [P, T])
        junk = sb("junk", [P, T, NB], BF16)

        arena = sb("arena", [P, 13568])

        def part(at, *shape):
            n = int(np.prod(shape))
            v = arena[:, at:at + n]
            if len(shape) == 2:
                v = v.rearrange("p (a b) -> p a b", a=shape[0])
            if len(shape) == 3:
                v = v.rearrange("p (a b c) -> p a b c", a=shape[0], b=shape[1])
            return v

        cos2 = part(0, T, DK)
        sin2 = part(512, T, DK)
        rot_a = part(1024, T, NB)
        rot_b = part(2048, T, NB)
        qt = part(3072, 2, 2, SEQ)
        kt_ = part(4096, 2, 2, SEQ)
        vv = part(5120, 2, T, DV)
        sg = part(7168, 2, T, DV)
        sd = part(9216, 2, 384)
        decay = part(9984, 2, 384)
        rows = part(10752, 4, P)
        acc = part(0, T, D)
        mw = part(4096, T, D)
        zt = part(8192, 2, T, NB)
        wpost = part(10240, D)
        bt = part(0, GROUPS, SEQ)
        ct = part(2048, GROUPS, SEQ)
        nat = part(4096, T, NB)
        conv = part(5120, 4, SEQ)
        yoff = part(5120, NB)
        yy = part(6144, T, NB)
        xdt = part(7168, T, NB)
        xoff = part(8192, NB)
        sz = part(8704, T, NB)
        mm = part(9728, 4, NB)
        cb = part(11776, 3, P)
        bcg = part(12160, 2, SEQ)
        dt_raw = part(12288, KT, SHEADS)
        dt = part(12672, T, SHEADS)
        da = part(12800, T, SHEADS)
        edge = part(12928, 2, SHEADS)
        woff = part(13056, SHEADS)
        d_bc = part(13312, SHEADS)
        a_bc = part(13376, SHEADS)
        dtb_bc = part(13440, SHEADS)
        gcol = part(13504, TAPS + 1, 4)
        dx, de, ds_, ds2, dp = (part(6144 + 128 * i, T, SHEADS) for i in range(5))

        gemm = ctx.enter_context(nc.psum_tensor("gemm", [P, 2, T, NB], F32))
        banks = ctx.enter_context(nc.psum_tensor("banks", [P, NBANK, NB], F32))

        raw_full = [sem(f"raw_full{i}") for i in range(RAW)]
        hi_ready, lo_ready, chunk_done = sem("hi_ready"), sem("lo_ready"), sem("chunk_done")
        drained = [sem(f"drained{i}") for i in range(2)]
        bank_full = sem("bank_full")
        consumed = [sem(f"consumed{i}") for i in range(NBANK)]
        x_full = [sem(f"x_full{i}") for i in range(4)]
        const_full, rot_full, ssdc_full = sem("const_full"), sem("rot_full"), sem("ssdc_full")
        decay_full, wpost_full, dtw_full = sem("decay_full"), sem("wpost_full"), sem("dtw_full")
        ut_hi_ready, yt_hi_ready, ht_hi_ready = sem("ut_hi_ready"), sem("yt_hi_ready"), sem("ht_hi_ready")
        h_ready, squares_done = sem("h_ready"), sem("squares_done")
        var_ready, std_ready, rstd_ready = sem("var_ready"), sem("std_ready"), sem("rstd_ready")
        dve_step, pool_step = sem("dve_step"), sem("pool_step")
        rot_done, head_var_ready, head_std_ready = sem("rot_done"), sem("head_var_ready"), sem("head_std_ready")
        head_rstd_ready, y_scaled = sem("head_rstd_ready"), sem("y_scaled")
        squared, acc_zero, mw_ready = sem("squared"), sem("acc_zero"), sem("mw_ready")
        dtw_hi_ready, dtw_lo_ready = sem("dtw_hi_ready"), sem("dtw_lo_ready")
        dt_abs, dt_exp, a_exp, da_ready = sem("dt_abs"), sem("dt_exp"), sem("a_exp"), sem("da_ready")
        woff_ready, conv_silu, bcg_ready = sem("woff_ready"), sem("conv_silu"), sem("bcg_ready")
        da_masked, m_done, x_ready, gated = sem("da_masked"), sem("m_done"), sem("x_ready"), sem("gated")
        group_var_ready = sem("group_var_ready")
        group_std_ready, group_rstd_ready = sem("group_std_ready"), sem("group_rstd_ready")
        group_scaled, out_done = sem("group_scaled"), sem("out_done")

        w_in_v = ret_w_in[0].rearrange("(k p) n -> p k n", p=P)
        w_ro_v = ret_w_out[0].rearrange("(k p) n -> p k n", p=P)
        w_si_v = ssd_w_in[0].rearrange("(k p) n -> p k n", p=P)
        w_so_v = ssd_w_out[0].rearrange("(k p) n -> p k n", p=P)
        w_up_v = [mlp_w_up[i].rearrange("(k p) n -> p k n", p=P) for i in range(2)]
        w_dn_v = [mlp_w_down[i].rearrange("(k p) n -> p k n", p=P) for i in range(2)]

        block = ctx.enter_context(nc.Block())

        @block.sync
        def _(sp):
            def load_unit(u, w, kt0, col):
                for c in range(CH):
                    free = u * CH + (c - RAW + 1)
                    if not isinstance(free, int) or free > 0:
                        sp.wait_ge(lo_ready, free)
                    sp.dma_start(w_raw[:, c % RAW, :, :],
                                 w[:, bass.ds(kt0 + CK * c, CK), bass.ds(col, NB)]
                                 ).then_inc(raw_full[c % RAW], 16)

            def load_pair(p):
                u = p * 6 + U_RET
                load_unit(u, w_in_v, 0, p * 512)
                if not isinstance(p, int):
                    f = Fill(F_RET + 7, (p - 1) * 4)
                    sp.wait_ge(consumed[f.bank], f.turn + 1)
                sp.dma_start(decay, ret_decay[:, bass.ds(p * 768, 768)].rearrange("p (a b) -> p a b", a=2)
                             ).then_inc(decay_full, 16)
                load_unit(u + 1, w_in_v, 0, p * 512 + 2048)
                for i in range(2):
                    load_unit(u + (2 + i), w_in_v, 0, p * 1024 + (4096 + 512 * i))
                for i in range(2):
                    load_unit(u + (4 + i), w_in_v, 0, p * 1024 + (8192 + 512 * i))

            def load_out(u0, w):
                for b in range(4):
                    for half in range(2):
                        load_unit(u0 + 2 * b + half, w, KT * half, NB * b)

            def load_mlp(u0, layer):
                with sp.Fori(0, FF_GROUPS) as g:
                    for j in range(4):
                        load_unit(g * 8 + (u0 + j), w_up_v[layer], 0, g * 2048 + NB * j)
                    for j in range(4):
                        load_unit(g * 8 + (u0 + 4 + j), w_dn_v[layer], g * KT, NB * j)

            for i in range(4):
                sp.dma_start(h[:, :, NB * i:NB * (i + 1)],
                             x[0].rearrange("(t p) d -> p t d", p=P)[:, :, NB * i:NB * (i + 1)]
                             ).then_inc(x_full[i], 16)
            load_pair(0)
            with sp.Fori(1, PAIRS) as p:
                load_pair(p)
            load_out(U_RET_OUT, w_ro_v)
            load_mlp(U_MLP0, 0)
            for k, col in enumerate((8192, 8704, 9216, 9728)):
                load_unit(U_SSD + k, w_si_v, 0, col)
            with sp.Fori(1, GROUPS + 1) as g1:
                load_unit(g1 * 2 + (U_SSD + 2), w_si_v, 0, g1 * NB + (INNER - NB))
                load_unit(g1 * 2 + (U_SSD + 3), w_si_v, 0, g1 * NB + (-NB))
            load_out(U_SSD_OUT, w_so_v)
            load_mlp(U_MLP1, 1)
            for i in range(4):
                sp.wait_ge(h_ready, 24 + 2 * (i + 1))
                sp.dma_start(out[0].rearrange("(t p) d -> p t d", p=P)[:, :, NB * i:NB * (i + 1)],
                             h[:, :, NB * i:NB * (i + 1)]).then_inc(out_done, 16)
            sp.wait_ge(out_done, 64)

        @block.tensor
        def _(pe):
            def chunk(u, c, hi, lo, kt0, par, start, stop):
                pe.wait_ge(lo_ready, u * CH + (c + 1))
                s = c % SPLIT
                for kk in range(CK):
                    k = kt0 + CK * c + kk
                    first = start and c == 0 and kk == 0
                    last = stop and c == CH - 1 and kk == CK - 1
                    for t in range(T):
                        o = gemm[:, par, t, :]
                        a_hi, a_lo = hi[:, k, P * t:P * (t + 1)], lo[:, k, P * t:P * (t + 1)]
                        pe.matmul(o, a_hi, w_hi[:, s, kk, :], start=first, stop=False)
                        pe.matmul(o, a_hi, w_lo[:, s, kk, :], start=False, stop=False)
                        mm_ = pe.matmul(o, a_lo, w_hi[:, s, kk, :], start=False, stop=last)
                mm_.then_inc(chunk_done, 1)

            def unit(u, par, turn, hi=ut_hi, lo=ut_lo, kt0=0, start=True, stop=True, before={}, after_={}):
                if start and (not isinstance(turn, int) or turn > 0):
                    pe.wait_ge(drained[par], turn * 4)
                for c in range(CH):
                    for f in before.get(c, ()):
                        f()
                    chunk(u, c, hi, lo, kt0, par, start, stop)
                    for f in after_.get(c, ()):
                        f()

            def free(f):
                if not isinstance(f.turn, int) or f.turn > 0:
                    pe.wait_ge(consumed[f.bank], f.turn)

            def turn_to_channels(f, src):
                free(f)
                for kk in range(2):
                    for t in range(T):
                        at = SEQ * kk + P * t
                        tr = pe.transpose(banks[:, f.bank, at:at + P], src(t, kk), ident)
                tr.then_inc(bank_full, 1)

            def norm_fill(phase, j):
                if phase == 0:
                    pe.wait_ge(x_full[j // 2], 16)
                else:
                    pe.wait_ge(h_ready, 8 * (phase - 1) + 2 * (j // 2) + 2)
                turn_to_channels(Fill(F_PHASE[phase] + j),
                                 lambda t, kk: h[:, t, P * (2 * j + kk):P * (2 * j + kk + 1)])

            def ut_ready(phase, j):
                f = Fill(F_PHASE[phase] + j)
                pe.wait_ge(consumed[f.bank], f.turn + 1)

            def first_unit(phase, u, turn, more={}):
                for j in range(3):
                    norm_fill(phase, j)
                aft = {c: [lambda c=c: norm_fill(phase, c + 3)] for c in range(5)}
                for c, fs in more.items():
                    aft[c] = aft.get(c, []) + list(fs)
                unit(u, 0, turn, before={c: [lambda c=c: ut_ready(phase, c)] for c in range(CH)}, after_=aft)

            pe.wait_ge(const_full, 16 * 10)
            at = 0
            for i, n in enumerate((128, 96, 96, 48)):
                tr = pe.transpose(banks[:, 0, at:at + n], rows[0:n, i, :], ident[0:n, 0:n])
                at += n
            tr.then_inc(bank_full, 1)

            def heads_to_channels(f, p, done, hh):
                pe.wait_ge(rot_done, p * 4 + done)
                turn_to_channels(f + hh, lambda t, kk: rot_a[:, t, DK * hh + P * kk:DK * hh + P * (kk + 1)])

            def scores(f, hh):
                for g in (f + (hh - 4), f + (hh - 2)):
                    pe.wait_ge(consumed[g.bank], g.turn + 1)
                for mt in range(T):
                    g = f + (2 * hh + mt)
                    free(g)
                    w = SEQ - P * mt
                    for k in range(2):
                        s_ = pe.matmul(banks[:, g.bank, 0:w], kt_[:, hh, k, P * mt:P * (mt + 1)],
                                       qt[:, hh, k, P * mt:SEQ], start=(k == 0), stop=(k == 1))
                    s_.then_inc(bank_full, 1)

            def values(p, fs, f, hh):
                for mt in range(T):
                    g = fs + (2 * hh + mt)
                    pe.wait_ge(consumed[g.bank], g.turn + 1)
                pe.wait_ge(drained[hh], (p * 3 + (B_RET + 1)) * 4 + 4)
                for t in range(T):
                    g = f + (2 * hh + t)
                    free(g)
                    o = banks[:, g.bank, :]
                    v_ = pe.matmul(o, sd[:, hh, P * t:P * (t + 1)], vv[:, hh, 0, :], start=True, stop=(t == 0))
                    if t == 1:
                        v_ = pe.matmul(o, sd[:, hh, 256:384], vv[:, hh, 1, :], start=False, stop=True)
                    v_.then_inc(bank_full, 1)

            def heads_out(f, p, hh):
                pe.wait_ge(y_scaled, p * 4 + 2 * (hh + 1))
                for j in range(2):
                    turn_to_channels(f + (2 * hh + j),
                                     lambda t, kk: sg[:, hh, t, P * (2 * j + kk):P * (2 * j + kk + 1)])

            def pair_fill(p, idx):
                return Fill(F_RET + idx, p * 4)

            def pair_rest(p):
                u, b = p * 6 + U_RET, p * 3 + B_RET
                unit(u + 1, 1, b, after_={3: [lambda: heads_to_channels(pair_fill(p, 0), p, 2, 0)],
                                          4: [lambda: heads_to_channels(pair_fill(p, 0), p, 2, 1)]})
                unit(u + 2, 0, b + 1, after_={3: [lambda: heads_to_channels(pair_fill(p, 2), p, 4, 0)],
                                              4: [lambda: heads_to_channels(pair_fill(p, 2), p, 4, 1)]})
                unit(u + 3, 1, b + 1, after_={3: [lambda: scores(pair_fill(p, 4), 0)],
                                              5: [lambda: scores(pair_fill(p, 4), 1)]})
                unit(u + 4, 0, b + 2)
                unit(u + 5, 1, b + 2, after_={1: [lambda: values(p, pair_fill(p, 4), pair_fill(p, 8), 0)],
                                              3: [lambda: values(p, pair_fill(p, 4), pair_fill(p, 8), 1)]})

            def pair_tail(p):
                return {5: [lambda: heads_out(pair_fill(p, 12), p, 0)], 7: [lambda: heads_out(pair_fill(p, 12), p, 1)]}

            first_unit(0, U_RET, B_RET)
            pair_rest(0)
            with pe.Fori(1, PAIRS) as p:
                unit(p * 6 + U_RET, 0, p * 3 + B_RET, after_=pair_tail(p - 1))
                pair_rest(p)

            def yt_wait(f):
                return [lambda: pe.wait_ge(consumed[f.bank], f.turn + 1)]

            def out_projection(u0, b0, tail0, tail1, waits0, waits1):
                for b in range(4):
                    unit(u0 + 2 * b, b % 2, b0 + b // 2, yt_hi, yt_lo, 0, True, False,
                         after_=tail0 if b == 0 else {}, before=waits0 if b == 0 else {})
                    unit(u0 + 2 * b + 1, b % 2, b0 + b // 2, yt_hi, yt_lo, KT, False, True,
                         after_=tail1 if b == 0 else {}, before=waits1 if b == 0 else {})

            out_projection(
                U_RET_OUT, B_RET_OUT, pair_tail(3), {},
                {0: [w for j in range(4) for w in yt_wait(pair_fill(2, 12 + j))]},
                {4 + j: yt_wait(pair_fill(3, 12 + j)) for j in range(4)})

            def mlp(phase, u0, b0, f0):
                def hidden_fills(g, j):
                    pe.wait_ge(squared, ((phase // 2) * FF_GROUPS + g) * 8 + 2 * (j + 1))
                    for i in range(2):
                        turn_to_channels(Fill(f0 + 2 * j + i, g * 2),
                                         lambda t, kk: zt[:, j % 2, t, P * (2 * i + kk):P * (2 * i + kk + 1)])

                def hidden_wait(g, c):
                    f = Fill(f0 + c, g * 2)
                    pe.wait_ge(consumed[f.bank], f.turn + 1)

                def rest(g):
                    u, b = g * 8 + u0, g * 4 + b0
                    for j in range(1, 4):
                        unit(u + j, j % 2, b + j // 2, after_={1: [lambda j=j: hidden_fills(g, j - 1)]})
                    unit(u + 4, 0, b + 2, yt_hi, yt_lo, after_={1: [lambda: hidden_fills(g, 3)]},
                         before={c: [lambda c=c: hidden_wait(g, c)] for c in range(CH)})
                    for j in range(1, 4):
                        unit(u + 4 + j, j % 2, b + 2 + j // 2, yt_hi, yt_lo)

                first_unit(phase, u0, b0)
                with pe.Fori(0, FF_GROUPS - 1) as g:
                    rest(g)
                    unit(g * 8 + (u0 + 8), 0, g * 4 + (b0 + 4))
                rest(FF_GROUPS - 1)

            mlp(1, U_MLP0, B_MLP0, F_MLP0)

            def dt_product():
                pe.wait_ge(dtw_lo_ready, 1)
                ut_ready(2, CH - 1)
                f = Fill(F_DT)
                free(f)
                wh = yt_hi[:, 28:32, :].rearrange("p a (b n) -> p (a b) n", n=SHEADS)
                wl = yt_lo[:, 28:32, :].rearrange("p a (b n) -> p (a b) n", n=SHEADS)
                for t in range(T):
                    o = banks[:, f.bank, SHEADS * t:SHEADS * (t + 1)]
                    for k in range(KT):
                        a_hi, a_lo = ut_hi[:, k, P * t:P * (t + 1)], ut_lo[:, k, P * t:P * (t + 1)]
                        pe.matmul(o, a_hi, wh[:, k, :], start=(k == 0), stop=False)
                        pe.matmul(o, a_hi, wl[:, k, :], start=False, stop=False)
                        m_ = pe.matmul(o, a_lo, wh[:, k, :], start=False, stop=(k == KT - 1))
                m_.then_inc(bank_full, 1)

            def decay_sums():
                pe.wait_ge(da_ready, 1)
                f = Fill(F_DECAY)
                free(f)
                pe.matmul(banks[:, f.bank, 0:SHEADS], after, da[:, 0, :], start=True, stop=True)
                pe.matmul(banks[:, f.bank, SHEADS:2 * SHEADS], upto, da[:, 1, :], start=True, stop=True
                          ).then_inc(bank_full, 1)

            def conv_fills(par, turn, f):
                pe.wait_ge(drained[par], turn * 4 + 4)
                for i in range(2):
                    turn_to_channels(f + i, lambda t, kk: nat[:, t, P * (2 * i + kk):P * (2 * i + kk + 1)])

            def group_cb(g, f):
                pe.wait_ge(bcg_ready, g + 1)
                for i, (mt, nt) in enumerate(((0, 0), (0, 1), (1, 1))):
                    free(f + i)
                    pe.matmul(banks[:, (f + i).bank, 0:P], bcg[:, 0, P * mt:P * (mt + 1)],
                              bcg[:, 1, P * nt:P * (nt + 1)], start=True, stop=True).then_inc(bank_full, 1)

            def group_seg(g, f, i):
                pe.wait_ge(da_masked, g * 4 + (i + 1))
                free(f + i)
                pe.matmul(banks[:, (f + i).bank, :], after, mm[:, i, :], start=True, stop=True
                          ).then_inc(bank_full, 1)

            def back_fills(g, f):
                pe.wait_ge(conv_silu, g * 2 + 10)
                for t in range(T):
                    free(f + t)
                    for k in range(4):
                        b_ = pe.transpose(banks[:, (f + t).bank, P * k:P * (k + 1)],
                                          conv[:, k, P * t:P * (t + 1)], ident)
                    b_.then_inc(bank_full, 1)

            def group_y(g, f):
                pe.wait_ge(x_ready, g * 5 + 3)
                pe.wait_ge(m_done, g * 4 + 4)
                for t in range(T):
                    free(f + t)
                    for hh in range(HPG):
                        y_ = pe.matmul(banks[:, (f + t).bank, HD * hh:HD * (hh + 1)],
                                       mm[:, 2 * t + hh // 4, P * (hh % 4):P * (hh % 4 + 1)],
                                       xdt[:, t, HD * hh:HD * (hh + 1)], start=True, stop=True)
                    y_.then_inc(bank_full, 1)
                free(f + 2)
                pe.matmul(banks[:, (f + 2).bank, :], cb[:, 1, :], xoff, start=True, stop=True
                          ).then_inc(bank_full, 1)

            def group_out(g, f):
                pe.wait_ge(group_scaled, g * 2 + 2)
                for i in range(2):
                    turn_to_channels(f + i, lambda t, kk: yy[:, t, P * (2 * i + kk):P * (2 * i + kk + 1)])

            first_unit(2, U_SSD, B_SSD, {6: [dt_product]})
            unit(U_SSD + 1, 1, B_SSD, after_={1: [lambda: conv_fills(0, B_SSD, Fill(F_BC0))], 6: [decay_sums]})
            unit(U_SSD + 2, 0, B_SSD + 1, after_={1: [lambda: conv_fills(1, B_SSD, Fill(F_BC1))]})
            unit(U_SSD + 3, 1, B_SSD + 1, after_={1: [lambda: conv_fills(0, B_SSD + 1, Fill(F_BC2))]})
            unit(U_SSD + 4, 0, B_SSD + 2, after_={
                1: [lambda: conv_fills(1, B_SSD + 1, Fill(F_BC3))],
                4: [lambda: group_cb(0, Fill(F_G0)), lambda: group_seg(0, Fill(F_G0 + 3), 0)],
                5: [lambda: group_seg(0, Fill(F_G0 + 3), 1)],
                6: [lambda: group_seg(0, Fill(F_G0 + 3), 2)],
                7: [lambda: group_seg(0, Fill(F_G0 + 3), 3)]})
            unit(U_SSD + 5, 1, B_SSD + 2, after_={
                1: [lambda: conv_fills(0, B_SSD + 2, Fill(F_G0 + 7))],
                7: [lambda: back_fills(0, Fill(F_G0 + 9))]})
            with pe.Fori(1, GROUPS) as g:
                def gf(idx):
                    return Fill(F_G1 + idx, (g - 1) * 4)
                unit(g * 2 + (U_SSD + 4), 0, g + (B_SSD + 2), after_={
                    2: [lambda: group_y(g - 1, gf(0))],
                    4: [lambda: group_cb(g, gf(3)), lambda: group_seg(g, gf(6), 0)],
                    5: [lambda: group_seg(g, gf(6), 1)],
                    6: [lambda: group_seg(g, gf(6), 2)],
                    7: [lambda: group_seg(g, gf(6), 3)]})
                unit(g * 2 + (U_SSD + 5), 1, g + (B_SSD + 2), after_={
                    1: [lambda: group_out(g - 1, gf(10)), lambda: conv_fills(0, g + (B_SSD + 2), gf(12))],
                    7: [lambda: back_fills(g, gf(14))]})
            out_projection(
                U_SSD_OUT, B_SSD_OUT, {2: [lambda: group_y(7, Fill(F_GTAIL))]},
                {1: [lambda: group_out(7, Fill(F_GTAIL + 3))]},
                {0: [w for j in range(2) for w in yt_wait(Fill(F_G1 + 96 + 10 + j))]},
                {6 + j: yt_wait(Fill(F_GTAIL + 3 + j)) for j in range(2)})
            mlp(3, U_MLP1, B_MLP1, F_MLP1)

        @block.scalar
        def _(act):
            def slot(u, c):
                u, c = u + (c + LEAD) // CH, (c + LEAD) % CH
                if isinstance(u, int) and u >= U_END:
                    return
                act.wait_ge(raw_full[c % RAW], (u * 2 + (c // RAW + 1)) * 16)
                freed = u * CH + (c - SPLIT + 1)
                if not isinstance(freed, int) or freed > 0:
                    act.wait_ge(chunk_done, freed)
                act.activation(w_hi[:, c % SPLIT, :, :], w_raw[:, c % RAW, :, :], ACT.Copy
                               ).then_inc(hi_ready, 1)

            def unit(u, at={}):
                for c in range(CH):
                    slot(u, c)
                    for f in at.get(c, ()):
                        f()

            def block_done(u):
                act.wait_ge(chunk_done, u * CH + CH)

            def split_fill(f, dst, k, col, ready):
                act.wait_ge(bank_full, f.full)
                if col is None:
                    act.activation(dst[:, bass.ds(k, 2), :].rearrange("p a b -> p (a b)"), banks[:, f.bank, :], ACT.Copy
                                   ).then_inc(ready, 1)
                    return
                for kk in range(2):
                    s_ = act.activation(dst[:, k + kk, :], banks[:, f.bank, SEQ * kk:SEQ * (kk + 1)], ACT.Copy,
                                        scale=cols[:, bass.ds(col + kk, 1)])
                s_.then_inc(ready, 1)

            def square(src, t, total, n):
                if not isinstance(n, int) or n >= T:
                    act.wait_ge(squares_done, n - (T - 1))
                act.activation(junk[:, t, :], src, ACT.Square, accum_out=total).then_inc(squares_done, 1)

            def norm_hi(phase, j):
                split_fill(Fill(F_PHASE[phase] + j), ut_hi, 2 * j, COL_PRE[phase] + 2 * j, ut_hi_ready)

            def squares(phase, b):
                if phase == 0:
                    act.wait_ge(x_full[b], 16)
                else:
                    act.wait_ge(h_ready, 8 * (phase - 1) + 2 * b + 2)
                for t in range(T):
                    square(h[:, t, NB * b:NB * (b + 1)], t, ssq[:, 2 * phase, t, b:b + 1],
                           squares_before(2 * phase) + 2 * b + t)

            def root(k):
                act.wait_ge(var_ready, k + 1)
                act.activation(std[:, k, :], var[:, k, :], ACT.Sqrt).then_inc(std_ready, 1)

            def first_unit(phase, u, more={}):
                if phase > 0:
                    root(2 * phase - 1)
                for j in range(3):
                    norm_hi(phase, j)
                at = {c: [lambda c=c: norm_hi(phase, c + 3)] for c in range(5)}
                for b, c in enumerate((1, 3, 4, 5)):
                    at.setdefault(c, []).append(lambda b=b: squares(phase, b))
                at.setdefault(7, []).append(lambda: root(2 * phase))
                for c, fs in more.items():
                    at[c] = list(fs) + at.get(c, [])
                unit(u, at)

            for i, (src, n) in enumerate((
                    (norm_mix_pre.rearrange("l (k c) -> (l k) c", c=P), 32),
                    (norm_ffn_pre.rearrange("l (k c) -> (l k) c", c=P), 32),
                    (ret_gn_w.rearrange("l (k c) -> (l k) c", c=P), 32),
                    (ssd_norm_w.rearrange("l (k c) -> (l k) c", c=P), 32))):
                act.dma_start(rows[32 * i:32 * (i + 1), 0, :], src).then_inc(const_full, 16)
            conv_rows = ssd_conv_w[0].rearrange("a (k c) -> a k c", c=P)
            for i in range(TAPS):
                act.dma_start(rows[CONV_KT * (i % 2):CONV_KT * (i % 2 + 1), 1 + i // 2, :], conv_rows[i]
                              ).then_inc(const_full, 16)
            act.dma_start(rows[0:CONV_KT, 3, :], ssd_conv_b.rearrange("l (k c) -> (l k) c", c=P)
                          ).then_inc(const_full, 16)
            act.dma_start(mask[:, :, :], masks.rearrange("p (a b) -> p a b", a=3)).then_inc(const_full, 16)
            act.dma_start(cos2, rot_cos.rearrange("(t p) d -> p t d", p=P)).then_inc(rot_full, 16)
            act.dma_start(sin2, rot_sin.rearrange("(t p) d -> p t d", p=P)).then_inc(rot_full, 16)
            for dst, src in ((d_bc, ssd_d), (a_bc, ssd_a_log), (dtb_bc, ssd_dt_bias)):
                act.dma_start(dst, src.to_broadcast([P, SHEADS])
                              ).then_inc(ssdc_full, 16)

            def load_wpost(src, f_or_u):
                act.wait_ge(chunk_done, f_or_u * CH)
                act.dma_start(wpost, src.to_broadcast([P, D])).then_inc(wpost_full, 16)

            for c in range(LEAD):
                slot(-1, CH - LEAD + c)
            act.wait_ge(consumed[0], 1)

            def pair_fill(p, idx):
                return Fill(F_RET + idx, p * 4)

            def evacuate_heads(f, dst, hh):
                g = f + hh
                act.wait_ge(bank_full, g.full)
                act.activation(dst[:, hh, :, :].rearrange("p a b -> p (a b)"), banks[:, g.bank, :], ACT.Copy
                               ).then_inc(consumed[g.bank], 1)

            def evacuate_block(u, par, dst, func, k):
                block_done(u)
                act.wait_ge(rstd_ready, k + 1)
                for t in range(T):
                    act.activation(dst[:, t, :], gemm[:, par, t, :], func, scale=rstd[:, k, t:t + 1]
                                   ).then_inc(drained[par], 2)

            def head_root(p):
                act.wait_ge(head_var_ready, p + 1)
                act.activation(head_std[:, :], head_var[:, :], ACT.Sqrt).then_inc(head_std_ready, 1)

            def heads_hi(p, hh):
                for j in (2 * hh, 2 * hh + 1):
                    split_fill(pair_fill(p, 12 + j), yt_hi, p * 8 + 2 * j, p * 8 + (COL_GN + 2 * j), yt_hi_ready)

            def pair_rest(p):
                u = p * 6 + U_RET
                unit(u + 1, {4: [lambda: evacuate_heads(pair_fill(p, 0), qt, 0)],
                             5: [lambda: evacuate_heads(pair_fill(p, 0), qt, 1)]})
                unit(u + 2, {4: [lambda: evacuate_heads(pair_fill(p, 2), kt_, 0)],
                             5: [lambda: evacuate_heads(pair_fill(p, 2), kt_, 1)]})
                unit(u + 3, {0: [lambda: evacuate_block(u + 2, 0, vv[:, 0], ACT.Copy, 0)]})
                unit(u + 4, {0: [lambda: evacuate_block(u + 3, 1, vv[:, 1], ACT.Copy, 0)]})
                unit(u + 5, {0: [lambda: evacuate_block(u + 4, 0, sg[:, 0], ACT.Silu, 0)]})

            def pair_tail(p):
                return {0: [lambda: evacuate_block(p * 6 + (U_RET + 5), 1, sg[:, 1], ACT.Silu, 0)],
                        2: [lambda: head_root(p)], 6: [lambda: heads_hi(p, 0)]}

            first_unit(0, U_RET)
            pair_rest(0)
            with act.Fori(1, PAIRS) as p:
                unit(p * 6 + U_RET, pair_tail(p - 1))
                heads_hi(p - 1, 1)
                pair_rest(p)

            def square_block(u, par, k, b):
                block_done(u)
                for t in range(T):
                    square(gemm[:, par, t, :], t, ssq[:, k, t, b:b + 1], squares_before(k) + 2 * b + t)

            def out_projection(u0, k, post, tail0, tail1):
                for b in range(4):
                    at = dict(tail0) if b == 0 else {0: [lambda b=b: square_block(u0 + 2 * b - 1, (b - 1) % 2, k, b - 1)]}
                    unit(u0 + 2 * b, at)
                    at = dict(tail1) if b == 0 else {}
                    if b == 0:
                        at[6] = [lambda: load_wpost(post, u0 + 1)]
                    unit(u0 + 2 * b + 1, at)
                square_block(u0 + 7, 1, k, 3)

            out_projection(U_RET_OUT, 1, norm_mix_post[0:1, :], pair_tail(3), {0: [lambda: heads_hi(3, 1)]})

            def mlp(phase, u0, f0, post):
                def hidden(g, j):
                    evacuate_block(g * 8 + (u0 + j), j % 2, zt[:, j % 2], ACT.Relu, 2 * phase)

                def hidden_hi(g, j):
                    for i in range(2):
                        split_fill(Fill(f0 + 2 * j + i, g * 2), yt_hi, 4 * j + 2 * i, None, ht_hi_ready)

                def rest(g, last):
                    u = g * 8 + u0
                    for j in range(1, 5):
                        unit(u + j, {0: [lambda j=j: hidden(g, j - 1)], 2: [lambda j=j: hidden_hi(g, j - 1)]})
                    for j in range(1, 4):
                        unit(u + 4 + j, {2: [lambda j=j: square_acc(j - 1)]} if last else {})

                def square_acc(d):
                    act.wait_ge(drained[d % 2], (b_last + d // 2) * 4 + 4)
                    for t in range(T):
                        square(acc[:, t, NB * d:NB * (d + 1)], t, ssq[:, 2 * phase + 1, t, d:d + 1],
                               squares_before(2 * phase + 1) + 2 * d + t)

                b_last = (B_MLP0 if phase == 1 else B_MLP1) + 4 * (FF_GROUPS - 1) + 2
                first_unit(phase, u0)
                with act.Fori(0, FF_GROUPS - 1) as g:
                    rest(g, False)
                    unit(g * 8 + (u0 + 8))
                load_wpost(post, u0 + 8)
                if phase == 1:
                    act.dma_start(dt_raw, w_si_v[:, :, 10240:10304]).then_inc(dtw_full, 16)
                rest(FF_GROUPS - 1, True)
                square_acc(3)

            mlp(1, U_MLP0, F_MLP0, norm_ffn_post[0:1, :])

            def dt_hi():
                act.wait_ge(dtw_full, 16)
                act.activation(yt_hi[:, 28:32, :].rearrange("p a b -> p (a b)"),
                               dt_raw.rearrange("p a b -> p (a b)"), ACT.Copy).then_inc(dtw_hi_ready, 1)

            def exp_abs():
                act.wait_ge(dt_abs, 1)
                act.activation(de, de, ACT.Exp, scale=-1.0).then_inc(dt_exp, 1)

            def exp_a():
                act.wait_ge(ssdc_full, 48)
                act.activation(a_bc, a_bc, ACT.Exp).then_inc(a_exp, 1)

            def exp_edges():
                f = Fill(F_DECAY)
                act.wait_ge(bank_full, f.full)
                act.activation(edge, banks[:, f.bank, 0:2 * SHEADS].rearrange("p (a b) -> p a b", a=2), ACT.Exp
                               ).then_inc(consumed[f.bank], 1)

            def conv_out(f, i, dst):
                g = f + i
                act.wait_ge(consumed[g.bank], g.turn + 1)
                act.activation(dst, conv[:, 2 * i:2 * i + 2, :], ACT.Silu).then_inc(conv_silu, 1)

            def exp_seg(f, i):
                g = f + i
                act.wait_ge(bank_full, g.full)
                act.activation(mm[:, i, :], banks[:, g.bank, :], ACT.Exp).then_inc(consumed[g.bank], 1)

            def group_square(g):
                act.wait_ge(gated, g * 2 + 2)
                for t in range(T):
                    square(yy[:, t, :], t, group_ssq[:, t:t + 1], g * 2 + (40 + t))

            def group_root(g):
                act.wait_ge(group_var_ready, g + 1)
                act.activation(group_std[:, :], group_var[:, :], ACT.Sqrt).then_inc(group_std_ready, 1)

            def group_hi(g, f):
                for i in range(2):
                    split_fill(f + i, yt_hi, g * 4 + 2 * i, g * 4 + (COL_SN + 2 * i), yt_hi_ready)

            def bc_silu(k):
                f = Fill((F_BC0, F_BC1, F_BC2, F_BC3)[k])
                dst = (bt, ct)[k // 2]
                return {4: [lambda: conv_out(f, 0, dst[:, 4 * (k % 2):4 * (k % 2) + 2, :])],
                        6: [lambda: conv_out(f, 1, dst[:, 4 * (k % 2) + 2:4 * (k % 2) + 4, :])]}

            def merged(*ats):
                out_ = {}
                for at in ats:
                    for c, fs in at.items():
                        out_.setdefault(c, []).extend(fs)
                return out_

            def to_nat(u, par):
                return {0: [lambda: evacuate_block(u, par, nat, ACT.Copy, 4)]}

            first_unit(2, U_SSD, {0: [dt_hi]})
            unit(U_SSD + 1, merged(to_nat(U_SSD, 0), {2: [exp_a, exp_abs]}, bc_silu(0)))
            exp_edges()
            unit(U_SSD + 2, merged(to_nat(U_SSD + 1, 1), bc_silu(1)))
            unit(U_SSD + 3, merged(to_nat(U_SSD + 2, 0), bc_silu(2)))
            unit(U_SSD + 4, merged(to_nat(U_SSD + 3, 1), bc_silu(3), {
                5: [lambda: exp_seg(Fill(F_G0 + 3), 0)], 6: [lambda: exp_seg(Fill(F_G0 + 3), 1)],
                7: [lambda: exp_seg(Fill(F_G0 + 3), 2)]}))

            def x_unit_silu(f):
                return {4: [lambda: conv_out(f, 0, conv[:, 0:2, :])], 6: [lambda: conv_out(f, 1, conv[:, 2:4, :])]}

            unit(U_SSD + 5, merged({0: [lambda: exp_seg(Fill(F_G0 + 3), 3)]}, to_nat(U_SSD + 4, 0),
                                   x_unit_silu(Fill(F_G0 + 7))))
            with act.Fori(1, GROUPS) as g:
                def gf(idx):
                    return Fill(F_G1 + idx, (g - 1) * 4)
                u = g * 2 + (U_SSD + 4)
                unit(u, {0: [lambda: evacuate_block(u - 1, 1, sz, ACT.Silu, 4)],
                         5: [lambda: exp_seg(gf(6), 0)], 6: [lambda: exp_seg(gf(6), 1)],
                         7: [lambda: exp_seg(gf(6), 2), lambda: group_square(g - 1)]})
                unit(u + 1, merged({0: [lambda: exp_seg(gf(6), 3)]}, to_nat(u, 0), {
                    1: [lambda: group_root(g - 1)],
                    2: [lambda: group_hi(g - 1, gf(10))]}, x_unit_silu(gf(12))))
            out_projection(U_SSD_OUT, 5, norm_mix_post[1:2, :], {
                0: [lambda: evacuate_block(U_SSD + 19, 1, sz, ACT.Silu, 4)],
                7: [lambda: group_square(7)]},
                {1: [lambda: group_root(7)], 2: [lambda: group_hi(7, Fill(F_GTAIL + 3))]})
            mlp(3, U_MLP1, F_MLP1, norm_ffn_post[1:2, :])
            root(7)

        @block.vector
        def _(dve):
            steps = Steps()

            def slot(u, c):
                u, c = u + (c + LEAD) // CH, (c + LEAD) % CH
                if isinstance(u, int) and u >= U_END:
                    return
                dve.wait_ge(hi_ready, u * CH + (c + 1))
                dve.tensor_tensor(w_lo[:, c % SPLIT, :, :], w_raw[:, c % RAW, :, :],
                                  w_hi[:, c % SPLIT, :, :].bitcast(F32), ALU.subtract).then_inc(lo_ready, 1)

            def unit(u, at={}):
                for c in range(CH):
                    slot(u, c)
                    for f in at.get(c, ()):
                        f()

            def block_done(u):
                dve.wait_ge(chunk_done, u * CH + CH)

            def split_fill(f, hi, lo, k, col, ready, n):
                dve.wait_ge(ready, n)
                if col is None:
                    dve.tensor_tensor(lo[:, k:k + 2, :].rearrange("p a b -> p (a b)"), banks[:, f.bank, :],
                                      hi[:, k:k + 2, :].rearrange("p a b -> p (a b)").bitcast(F32),
                                      ALU.subtract).then_inc(consumed[f.bank], 1)
                    return
                for kk in range(2):
                    s_ = dve.scalar_tensor_tensor(
                        out=lo[:, k + kk, :], in0=banks[:, f.bank, SEQ * kk:SEQ * (kk + 1)],
                        scalar=cols[:, bass.ds(col + kk, 1)], in1=hi[:, k + kk, :].bitcast(F32),
                        op0=ALU.mult, op1=ALU.subtract)
                s_.then_inc(consumed[f.bank], 1)

            def norm_lo(phase, j):
                split_fill(Fill(F_PHASE[phase] + j), ut_hi, ut_lo, 2 * j, COL_PRE[phase] + 2 * j,
                           ut_hi_ready, 8 * phase + j + 1)

            def mean_square(k):
                n = steps.next()
                dve.tensor_reduce(var[:, k, :], ssq[:, k, :, :], AX_X, ALU.add).then_inc(dve_step, 1)
                dve.wait_ge(dve_step, n)
                dve.tensor_scalar(var[:, k, :], var[:, k, :], 1.0 / D, RMS_EPS, ALU.mult, ALU.add
                                  ).then_inc(var_ready, 1)

            def inverse(k):
                dve.wait_ge(std_ready, k + 1)
                dve.reciprocal(rstd[:, k, :], std[:, k, :]).then_inc(rstd_ready, 1)

            def pre_norm(phase):
                dve.wait_ge(squares_done, squares_before(2 * phase) + 8)
                mean_square(2 * phase)
                inverse(2 * phase)

            def residual(k, b):
                dve.wait_ge(rstd_ready, k + 1)
                for t in range(T):
                    hb = h[:, t, NB * b:NB * (b + 1)]
                    dve.scalar_tensor_tensor(out=hb, in0=mw[:, t, NB * b:NB * (b + 1)], scalar=rstd[:, k, t:t + 1],
                                             in1=hb, op0=ALU.mult, op1=ALU.add).then_inc(h_ready, 1)

            def first_unit(phase, u, more={}):
                if phase > 0:
                    mean_square(2 * phase - 1)
                    inverse(2 * phase - 1)
                    residual(2 * phase - 1, 0)
                norm_lo(phase, 0)
                if phase > 0:
                    residual(2 * phase - 1, 1)
                norm_lo(phase, 1)
                norm_lo(phase, 2)
                at = {c: [lambda c=c: norm_lo(phase, c + 3)] for c in range(5)}
                if phase > 0:
                    at[0].append(lambda: residual(2 * phase - 1, 2))
                    at[2].append(lambda: residual(2 * phase - 1, 3))
                at.setdefault(7, []).append(lambda: pre_norm(phase))
                for c, fs in more.items():
                    at[c] = list(fs) + at.get(c, [])
                unit(u, at)

            for c in range(LEAD):
                slot(-1, CH - LEAD + c)
            dve.wait_ge(bank_full, 1)
            dve.tensor_copy(cols[:, 0:COL_CONV], banks[:, 0, 0:COL_CONV])
            dve.tensor_copy(cols[:, COL_CONV:NCOLS], banks[:, 0, COL_CONV:NCOLS]).then_inc(consumed[0], 1)
            dve.wait_ge(consumed[0], 1)

            def pair_fill(p, idx):
                return Fill(F_RET + idx, p * 4)

            def scale_tables():
                dve.wait_ge(rot_full, 32)
                dve.wait_ge(rstd_ready, 1)
                for tab in (cos2, sin2):
                    for t in range(T):
                        n = steps.next()
                        dve.tensor_scalar(tab[:, t, :], tab[:, t, :], rstd[:, 0, t:t + 1], None, ALU.mult
                                          ).then_inc(dve_step, 1)
                dve.wait_ge(dve_step, n)

            def rotate(u, par):
                block_done(u)
                for t in range(T):
                    ps = gemm[:, par, t, :].rearrange("p (h i d) -> p h i d", h=2, i=2)
                    ra = rot_a[:, t, :].rearrange("p (h d) -> p h d", h=2)
                    rb = rot_b[:, t, :].rearrange("p (h i d) -> p h i d", h=2, i=2)
                    dve.tensor_tensor(ra, gemm[:, par, t, :].rearrange("p (h d) -> p h d", h=2),
                                      cos2[:, t, :].unsqueeze(1).to_broadcast([P, 2, DK]), ALU.mult)
                    for i in range(2):
                        r_ = dve.tensor_tensor(
                            rb[:, :, i, :], ps[:, :, 1 - i, :],
                            sin2[:, t, P * i:P * (i + 1)].unsqueeze(1).to_broadcast([P, 2, P]), ALU.mult)
                    r_.then_inc(drained[par], 2)

            def decay_scores(p, hh):
                dve.wait_ge(decay_full, p * 16 + 16)
                for mt in range(T):
                    f = pair_fill(p, 4 + 2 * hh + mt)
                    dve.wait_ge(bank_full, f.full)
                    a, w = 256 * mt, SEQ - P * mt
                    dve.tensor_tensor(sd[:, hh, a:a + w], banks[:, f.bank, 0:w], decay[:, hh, a:a + w], ALU.mult
                                      ).then_inc(consumed[f.bank], 1)

            def head_stats(p, hh):
                for t in range(T):
                    f = pair_fill(p, 8 + 2 * hh + t)
                    i = 2 * hh + t
                    dve.wait_ge(bank_full, f.full)
                    n = steps.next()
                    dve.bn_stats(bn[:, i, :], banks[:, f.bank, :]).then_inc(dve_step, 1)
                    dve.wait_ge(dve_step, n)
                    dve.memset(waited[:, :], 0.0)
                    n = steps.next()
                    dve.bn_aggr(mv[:, i, :], bn[:, i, :]).then_inc(dve_step, 1)
                dve.wait_ge(dve_step, n)

            def head_gate(p, hh):
                dve.wait_ge(drained[hh], (p * 3 + (B_RET + 2)) * 4 + 4)
                for t in range(T):
                    f = pair_fill(p, 8 + 2 * hh + t)
                    i = 2 * hh + t
                    dve.scalar_tensor_tensor(out=sg[:, hh, t, :], in0=banks[:, f.bank, :], scalar=mv[:, i, 0:1],
                                             in1=sg[:, hh, t, :], op0=ALU.subtract, op1=ALU.mult
                                             ).then_inc(consumed[f.bank], 1)

            def head_variance(p):
                dve.tensor_scalar(head_var[:, :], mv[:, :, 1], GN_EPS, None, ALU.add).then_inc(head_var_ready, 1)

            def head_inverse(p):
                dve.wait_ge(head_std_ready, p + 1)
                dve.reciprocal(head_rstd[:, :], head_std[:, :]).then_inc(head_rstd_ready, 1)

            def heads_lo(p, hh):
                for j in (2 * hh, 2 * hh + 1):
                    split_fill(pair_fill(p, 12 + j), yt_hi, yt_lo, p * 8 + 2 * j, p * 8 + (COL_GN + 2 * j),
                               yt_hi_ready, p * 4 + (j + 1))

            def pair_rest(p):
                u = p * 6 + U_RET
                first = [scale_tables] if isinstance(p, int) else []
                unit(u + 1, {0: first + [lambda: rotate(u, 0)]})
                unit(u + 2, {0: [lambda: rotate(u + 1, 1)]})
                unit(u + 3, {4: [lambda: decay_scores(p, 0)], 6: [lambda: decay_scores(p, 1)]})
                unit(u + 4)
                unit(u + 5, {2: [lambda: head_stats(p, 0), lambda: head_gate(p, 0)], 4: [lambda: head_stats(p, 1)]})

            def pair_tail(p):
                return {0: [lambda: head_variance(p)], 1: [lambda: head_gate(p, 1)], 3: [lambda: head_inverse(p)],
                        6: [lambda: heads_lo(p, 0)]}

            first_unit(0, U_RET)
            pair_rest(0)
            with dve.Fori(1, PAIRS) as p:
                steps.loop(p - 1, 8)
                unit(p * 6 + U_RET, pair_tail(p - 1))
                heads_lo(p - 1, 1)
                pair_rest(p)
                steps.end(PAIRS - 1)

            def weigh_block(u, par, b, n):
                block_done(u)
                dve.wait_ge(squares_done, squares_before(1 if n == 1 else 5) + 2 * b + 2)
                dve.wait_ge(wpost_full, 16 * n)
                for t in range(T):
                    dve.tensor_tensor(mw[:, t, NB * b:NB * (b + 1)], gemm[:, par, t, :],
                                      wpost[:, NB * b:NB * (b + 1)], ALU.mult).then_inc(drained[par], 2)

            def out_projection(u0, b0, n, tail0, tail1):
                for b in range(4):
                    at = dict(tail0) if b == 0 else {0: [lambda b=b: weigh_block(u0 + 2 * b - 1, (b - 1) % 2, b - 1, n)]}
                    unit(u0 + 2 * b, at)
                    unit(u0 + 2 * b + 1, tail1 if b == 0 else {})
                weigh_block(u0 + 7, 1, 3, n)
                for par in range(2):
                    dve.wait_ge(drained[par], 4 * (b0 + 2))

            out_projection(U_RET_OUT, B_RET_OUT, 1, pair_tail(3), {0: [lambda: heads_lo(3, 1)]})

            def mlp(phase, u0, b0, f0):
                def hidden_lo(g, j):
                    for i in range(2):
                        split_fill(Fill(f0 + 2 * j + i, g * 2), yt_hi, yt_lo, 4 * j + 2 * i, None,
                                   ht_hi_ready, (g + (phase // 2) * FF_GROUPS) * 8 + (2 * j + i + 1))

                def add_block(u, d):
                    block_done(u)
                    dve.wait_ge(acc_zero, phase // 2 + 1)
                    for t in range(T):
                        a = acc[:, t, NB * d:NB * (d + 1)]
                        dve.tensor_tensor(a, gemm[:, d % 2, t, :], a, ALU.add).then_inc(drained[d % 2], 2)

                def rest(g):
                    u = g * 8 + u0
                    for j in range(1, 5):
                        unit(u + j, {2: [lambda j=j: hidden_lo(g, j - 1)]})
                    for j in range(1, 4):
                        unit(u + 4 + j, {0: [lambda j=j: add_block(u + 3 + j, j - 1)]})

                first_unit(phase, u0)
                with dve.Fori(0, FF_GROUPS - 1) as g:
                    rest(g)
                    unit(g * 8 + (u0 + 8), {0: [lambda: add_block(g * 8 + (u0 + 7), 3)]})
                rest(FF_GROUPS - 1)
                add_block(u0 + 31, 3)
                dve.wait_ge(squares_done, squares_before(2 * phase + 1) + 8)
                dve.wait_ge(mw_ready, (phase // 2 + 1) * 8)

            mlp(1, U_MLP0, B_MLP0, F_MLP0)

            def dt_lo():
                dve.wait_ge(dtw_hi_ready, 1)
                dve.tensor_tensor(yt_lo[:, 28:32, :].rearrange("p a b -> p (a b)"), dt_raw.rearrange("p a b -> p (a b)"),
                                  yt_hi[:, 28:32, :].rearrange("p a b -> p (a b)").bitcast(F32), ALU.subtract
                                  ).then_inc(dtw_lo_ready, 1)

            def chained(make):
                n = steps.next()
                make().then_inc(dve_step, 1)
                dve.wait_ge(dve_step, n)

            def dt_input():
                f = Fill(F_DT)
                dve.wait_ge(bank_full, f.full)
                dve.wait_ge(rstd_ready, 5)
                dve.wait_ge(ssdc_full, 48)
                for t in range(T):
                    s_ = dve.scalar_tensor_tensor(out=dx[:, t, :], in0=banks[:, f.bank, SHEADS * t:SHEADS * (t + 1)],
                                                  scalar=rstd[:, 4, t:t + 1], in1=dtb_bc, op0=ALU.mult, op1=ALU.add)
                s_.then_inc(consumed[f.bank], 1)
                dve.wait_ge(consumed[f.bank], f.turn + 1)
                dve.scalar_tensor_tensor(out=de, in0=dx, scalar=-1.0, in1=dx, op0=ALU.mult, op1=ALU.max
                                         ).then_inc(dt_abs, 1)

            def dt_chain():
                dve.wait_ge(dt_exp, 1)
                dve.wait_ge(a_exp, 1)
                chained(lambda: dve.tensor_scalar(ds2, de, 2.0, None, ALU.add))
                chained(lambda: dve.reciprocal(ds2, ds2))
                chained(lambda: dve.tensor_tensor(ds_, de, ds2, ALU.mult))
                chained(lambda: dve.tensor_tensor(ds2, ds_, ds_, ALU.mult))
                chained(lambda: dve.tensor_scalar(dp, ds2, 1.0 / 15, None, ALU.mult))
                for k in (13, 11, 9, 7, 5, 3):
                    chained(lambda: dve.scalar_tensor_tensor(out=dp, in0=dp, scalar=1.0 / k, in1=ds2,
                                                             op0=ALU.add, op1=ALU.mult))
                chained(lambda: dve.scalar_tensor_tensor(out=dp, in0=dp, scalar=1.0, in1=ds_,
                                                         op0=ALU.add, op1=ALU.mult))
                chained(lambda: dve.tensor_scalar(dx, dx, 0.0, None, ALU.max))
                chained(lambda: dve.scalar_tensor_tensor(out=dt, in0=dp, scalar=2.0, in1=dx,
                                                         op0=ALU.mult, op1=ALU.add))
                for t in range(T):
                    s_ = dve.scalar_tensor_tensor(out=da[:, t, :], in0=dt[:, t, :], scalar=-1.0, in1=a_bc,
                                                  op0=ALU.mult, op1=ALU.mult)
                s_.then_inc(da_ready, 1)

            def edge_weights():
                f = Fill(F_DECAY)
                dve.wait_ge(consumed[f.bank], f.turn + 1)
                dve.tensor_tensor(woff, edge[:, 0, :], dt[:, 0, :], ALU.mult).then_inc(woff_ready, 1)

            def conv_columns(k):
                chained(lambda: dve.tensor_copy(
                    gcol, cols[:, COL_CONV:NCOLS].rearrange("p (a k) -> p a k", k=CONV_KT)[:, :, bass.ds(k, 4)]))

            def convolve(f, i, n):
                g = f + i
                dve.wait_ge(bank_full, g.full)
                dve.wait_ge(conv_silu, n)
                for kk in range(2):
                    k = 2 * i + kk
                    s = steps.next()
                    dve.tensor_scalar(conv[:, k, :], banks[:, g.bank, SEQ * kk:SEQ * (kk + 1)], gcol[:, 3, k:k + 1],
                                      gcol[:, 4, k:k + 1], ALU.mult, ALU.add).then_inc(dve_step, 1)
                for back in (1, 2, 3):
                    for kk in range(2):
                        k = 2 * i + kk
                        dve.wait_ge(dve_step, s - 1 + kk)
                        i_ = dve.scalar_tensor_tensor(
                            out=conv[:, k, back:SEQ], in0=banks[:, g.bank, SEQ * kk:SEQ * (kk + 1) - back],
                            scalar=gcol[:, 3 - back, k:k + 1], in1=conv[:, k, back:SEQ], op0=ALU.mult, op1=ALU.add)
                        if back < 3:
                            i_.then_inc(dve_step, 1)
                    if back < 3:
                        steps.next()
                        s = steps.next()
                i_.then_inc(consumed[g.bank], 1)

            def mask_cb(f):
                for i in range(3):
                    g = f + i
                    dve.wait_ge(bank_full, g.full)
                    if i == 1:
                        dve.tensor_copy(cb[:, i, :], banks[:, g.bank, 0:P]).then_inc(consumed[g.bank], 1)
                    else:
                        dve.tensor_tensor(cb[:, i, :], banks[:, g.bank, 0:P], upto, ALU.mult
                                          ).then_inc(consumed[g.bank], 1)

            def weigh_scores(f, fcb, i):
                g = f + i
                dve.wait_ge(consumed[g.bank], g.turn + 1)
                if i == 0:
                    for j in range(3):
                        dve.wait_ge(consumed[(fcb + j).bank], (fcb + j).turn + 1)
                m4 = mm[:, i, :].rearrange("p (a b) -> p a b", a=4)
                dve.tensor_tensor(m4, m4, cb[:, 2 * (i // 2), :].unsqueeze(1).to_broadcast([P, 4, P]), ALU.mult
                                  ).then_inc(m_done, 1)

            def x_back(f):
                for t in range(T):
                    g = f + t
                    dve.wait_ge(bank_full, g.full)
                    dve.tensor_copy(yy[:, t, :], banks[:, g.bank, :]).then_inc(consumed[g.bank], 1)

            def gather_y(g, f):
                dve.wait_ge(x_ready, g * 5 + 5)
                for t in range(T):
                    fb = f + t
                    dve.wait_ge(bank_full, fb.full)
                    dve.tensor_tensor(yy[:, t, :], banks[:, fb.bank, :], yy[:, t, :], ALU.add
                                      ).then_inc(consumed[fb.bank], 1)
                fb = f + 2
                dve.wait_ge(bank_full, fb.full)
                dve.tensor_tensor(yoff.rearrange("p (a b) -> p a b", a=HPG),
                                  banks[:, fb.bank, :].rearrange("p (a b) -> p a b", a=HPG),
                                  edge[:, 1, bass.ds(g * HPG, HPG)].unsqueeze(2).to_broadcast([P, HPG, HD]),
                                  ALU.mult).then_inc(consumed[fb.bank], 1)

            def group_variance(g):
                dve.wait_ge(squares_done, g * 2 + 42)
                dve.tensor_scalar(group_var[:, :], group_ssq[:, :], 1.0 / NB, RMS_EPS, ALU.mult, ALU.add
                                  ).then_inc(group_var_ready, 1)

            def group_inverse(g):
                dve.wait_ge(group_std_ready, g + 1)
                dve.reciprocal(group_rstd[:, :], group_std[:, :]).then_inc(group_rstd_ready, 1)

            def group_lo(g, f):
                for i in range(2):
                    split_fill(f + i, yt_hi, yt_lo, g * 4 + 2 * i, g * 4 + (COL_SN + 2 * i),
                               yt_hi_ready, g * 2 + (16 + i + 1))

            def bc_conv(k):
                f = Fill((F_BC0, F_BC1, F_BC2, F_BC3)[k])
                return {2: [lambda: conv_columns(32 + 4 * k), lambda: convolve(f, 0, 2 * k)],
                        4: [lambda: convolve(f, 1, 2 * k)]}

            def x_conv(g, f):
                return {2: [lambda: conv_columns(g * 4), lambda: convolve(f, 0, g * 2 + 8)],
                        4: [lambda: convolve(f, 1, g * 2 + 8)]}

            def merged(*ats):
                out_ = {}
                for at in ats:
                    for c, fs in at.items():
                        out_.setdefault(c, []).extend(fs)
                return out_

            first_unit(2, U_SSD, {0: [dt_lo]})
            unit(U_SSD + 1, merged({0: [dt_input], 4: [dt_chain]}, bc_conv(0)))
            unit(U_SSD + 2, merged({0: [edge_weights]}, bc_conv(1)))
            unit(U_SSD + 3, bc_conv(2))
            unit(U_SSD + 4, merged(bc_conv(3), {6: [lambda: mask_cb(Fill(F_G0))]}))
            f0 = Fill(F_G0 + 3)
            unit(U_SSD + 5, merged({0: [lambda: weigh_scores(f0, Fill(F_G0), 0), lambda: weigh_scores(f0, Fill(F_G0), 1)],
                                    1: [lambda: weigh_scores(f0, Fill(F_G0), 2), lambda: weigh_scores(f0, Fill(F_G0), 3)]},
                                   x_conv(0, Fill(F_G0 + 7))))
            with dve.Fori(1, GROUPS) as g:
                steps.loop(g - 1, 13)

                def gf(idx):
                    return Fill(F_G1 + idx, (g - 1) * 4)
                u = g * 2 + (U_SSD + 4)
                back = Fill(F_G1 - 2, (g - 1) * 4)
                unit(u, {0: [lambda: x_back(back)], 3: [lambda: gather_y(g - 1, gf(0))],
                         5: [lambda: mask_cb(gf(3))]})
                unit(u + 1, merged({0: [lambda: group_variance(g - 1), lambda: weigh_scores(gf(6), gf(3), 0),
                                        lambda: weigh_scores(gf(6), gf(3), 1)],
                                    1: [lambda: weigh_scores(gf(6), gf(3), 2), lambda: weigh_scores(gf(6), gf(3), 3),
                                        lambda: group_inverse(g - 1)],
                                    2: [lambda: group_lo(g - 1, gf(10))]}, x_conv(g, gf(12))))
                steps.end(GROUPS - 1)
            out_projection(U_SSD_OUT, B_SSD_OUT, 3, {
                0: [lambda: x_back(Fill(F_GTAIL - 2))], 3: [lambda: gather_y(7, Fill(F_GTAIL))]},
                {0: [lambda: group_variance(7)], 1: [lambda: group_inverse(7)],
                 2: [lambda: group_lo(7, Fill(F_GTAIL + 3))]})
            mlp(3, U_MLP1, B_MLP1, F_MLP1)
            mean_square(7)
            inverse(7)
            for b in range(4):
                residual(7, b)

        @block.gpsimd
        def _(pool):
            steps = Steps()

            def rotate_add(p, k):
                for t in range(T):
                    pool.wait_ge(drained[k], (p * 3 + B_RET) * 4 + 2 * (t + 1))
                    pool.tensor_tensor(rot_a[:, t, :], rot_a[:, t, :], rot_b[:, t, :], ALU.add).then_inc(rot_done, 1)

            def heads_scale(p):
                pool.wait_ge(head_rstd_ready, p + 1)
                for i in range(4):
                    if i % 2 == 0:
                        f = Fill(F_RET + 8 + i, p * 4)
                        pool.wait_ge(consumed[f.bank], f.turn + 1)
                        f = f + 1
                        pool.wait_ge(consumed[f.bank], f.turn + 1)
                    y = sg[:, i // 2, i % 2, :]
                    pool.tensor_tensor(y, y, head_rstd[:, i:i + 1].to_broadcast([P, NB]), ALU.mult).then_inc(y_scaled, 1)

            with pool.Fori(0, PAIRS) as p:
                rotate_add(p, 0)
                rotate_add(p, 1)
                heads_scale(p)

            def mlp(phase, u0, b0):
                pool.wait_ge(h_ready, 8 * phase)
                pool.memset(acc, 0.0).then_inc(acc_zero, 1)
                with pool.Fori(0, FF_GROUPS) as g:
                    for j in range(4):
                        for t in range(T):
                            pool.wait_ge(drained[j % 2], (g * 4 + (b0 + j // 2)) * 4 + 2 * (t + 1))
                            z = zt[:, j % 2, t, :]
                            pool.tensor_tensor(z, z, z, ALU.mult).then_inc(squared, 1)
                pool.wait_ge(wpost_full, 16 * (phase + 1))
                for d in range(4):
                    for t in range(T):
                        pool.wait_ge(drained[d % 2], (b0 + 14 + d // 2) * 4 + 2 * (t + 1))
                        c = slice(NB * d, NB * (d + 1))
                        pool.tensor_tensor(mw[:, t, c], acc[:, t, c], wpost[:, c], ALU.mult).then_inc(mw_ready, 1)

            mlp(1, U_MLP0, B_MLP0)

            def copy_bc(g):
                pool.tensor_copy(bcg[:, 0, :], bt[:, g, :])
                pool.tensor_copy(bcg[:, 1, :], ct[:, g, :]).then_inc(bcg_ready, 1)

            def mask_da(g):
                for i in range(4):
                    t, q = i // 2, i % 2
                    pool.tensor_tensor(mm[:, i, :].rearrange("p (a b) -> p a b", a=4),
                                       upto.unsqueeze(1).to_broadcast([P, 4, P]),
                                       da[:, t, bass.ds(g * HPG + 4 * q, 4)].unsqueeze(2).to_broadcast([P, 4, P]),
                                       ALU.mult).then_inc(da_masked, 1)

            def x_products(g, back):
                def per_head(v):
                    return v.rearrange("p (a b) -> p a b", a=HPG)

                def head_row(v):
                    return v[:, bass.ds(g * HPG, HPG)].unsqueeze(2).to_broadcast([P, HPG, HD])
                for t in range(T):
                    f = back + t
                    pool.wait_ge(consumed[f.bank], f.turn + 1)
                    pool.tensor_tensor(per_head(xdt[:, t, :]), per_head(yy[:, t, :]), head_row(dt[:, t, :]), ALU.mult
                                       ).then_inc(x_ready, 1)
                pool.tensor_tensor(per_head(xoff), per_head(yy[:, 0, :]), head_row(woff), ALU.mult
                                   ).then_inc(x_ready, 1)
                for t in range(T):
                    pool.tensor_tensor(per_head(yy[:, t, :]), per_head(yy[:, t, :]), head_row(d_bc), ALU.mult
                                       ).then_inc(x_ready, 1)

            def gate(g, f):
                for i in range(3):
                    pool.wait_ge(consumed[(f + i).bank], (f + i).turn + 1)
                n = steps.next()
                pool.tensor_tensor(yy[:, 1, :], yy[:, 1, :], yoff, ALU.add).then_inc(pool_step, 1)
                pool.wait_ge(drained[1], (g + (B_SSD + 2)) * 4 + 4)
                pool.tensor_tensor(yy[:, 0, :], yy[:, 0, :], sz[:, 0, :], ALU.mult).then_inc(gated, 1)
                pool.wait_ge(pool_step, n)
                pool.tensor_tensor(yy[:, 1, :], yy[:, 1, :], sz[:, 1, :], ALU.mult).then_inc(gated, 1)

            def group_scale(g):
                pool.wait_ge(group_rstd_ready, g + 1)
                for t in range(T):
                    pool.tensor_tensor(yy[:, t, :], yy[:, t, :], group_rstd[:, t:t + 1].to_broadcast([P, NB]),
                                       ALU.mult).then_inc(group_scaled, 1)

            pool.wait_ge(da_ready, 1)
            pool.wait_ge(woff_ready, 1)
            mask_da(0)
            pool.wait_ge(conv_silu, 6)
            copy_bc(0)
            pool.wait_ge(conv_silu, 8)
            with pool.Fori(1, GROUPS) as g:
                def gf(idx):
                    return Fill(F_G1 + idx, (g - 1) * 4)
                x_products(g - 1, Fill(F_G1 - 2, (g - 1) * 4))
                steps.loop(g - 1, 1)
                copy_bc(g)
                pool.wait_ge(bank_full, gf(2).full)
                mask_da(g)
                gate(g - 1, gf(0))
                steps.end(GROUPS - 1)
                group_scale(g - 1)
            x_products(7, Fill(F_GTAIL - 2))
            gate(7, Fill(F_GTAIL))
            group_scale(7)
            mlp(3, U_MLP1, B_MLP1)


_INS = ["x", "norm_mix_pre", "norm_mix_post", "norm_ffn_pre", "norm_ffn_post", "ret_w_in", "ret_gn_w", "ret_w_out",
        "ssd_w_in", "ssd_conv_w", "ssd_conv_b", "ssd_dt_bias", "ssd_a_log", "ssd_d", "ssd_norm_w", "ssd_w_out",
        "mlp_w_up", "mlp_w_down"]
_OUTS = [((1, SEQ, D), "float32")]


def _constants():
    f32 = np.float32
    half = DK // 2
    inv_freq = (f32(10000.0) ** (-np.arange(half, dtype=f32) / f32(half))).astype(f32)
    ang = (np.arange(SEQ, dtype=f32)[:, None] * inv_freq[None, :]).astype(np.float64)
    cos, sin = np.cos(ang), np.sin(ang)
    log_gamma = np.log1p(-np.exp2(-5.0 - np.arange(HEADS)))
    n = np.arange(SEQ)
    seen = (n[:, None] // DECAY_CHUNK) <= (n[None, :] // DECAY_CHUNK)
    full = np.exp(np.abs(n[:, None] - n[None, :])[None] * log_gamma[:, None, None]) * seen * DK ** -0.5
    tiles = np.concatenate([full[:, 0:P, :], full[:, P:SEQ, P:SEQ]], axis=2)
    i = np.arange(P)
    masks = np.stack([i[:, None] == i[None, :], i[:, None] <= i[None, :], i[:, None] > i[None, :]], axis=1)
    return {
        "rot_cos": np.concatenate([cos, cos], 1).astype(f32),
        "rot_sin": np.concatenate([-sin, sin], 1).astype(f32),
        "ret_decay": np.ascontiguousarray(tiles.transpose(1, 0, 2).reshape(P, -1)).astype(f32),
        "masks": np.ascontiguousarray(masks.reshape(P, -1)).astype(f32),
    }


def kernel(**inputs):
    import numpy as _np
    import concourse.bacc as _bacc
    from concourse import mybir as _mybir
    from concourse.bass_utils import run_bass_kernel_spmd as _run

    nc = _bacc.Bacc("TRN2", target_bir_lowering=False, num_devices=1, dynamic_dma_scratch_size=1024)
    arrays, args = {}, []
    named = [(name, _np.ascontiguousarray(inputs[name])) for name in _INS] + list(_constants().items())
    for name, a in named:
        arrays[f"in_{name}_dram"] = a
        args.append(nc.dram_tensor(f"in_{name}_dram", a.shape, _mybir.dt.from_np(a.dtype), kind="ExternalInput").ap())
    for i, (shape, dtype) in enumerate(_OUTS):
        dt = _mybir.dt.from_np(_np.dtype(dtype))
        args.append(nc.dram_tensor(f"out_{i}_dram", shape, dt, kind="ExternalOutput").ap())
    hybrid_trunk(nc, *args)
    r = _run(nc, [arrays], core_ids=[0])
    got = tuple(r.results[0][f"out_{i}_dram"] for i in range(len(_OUTS)))
    return got[0]
```

```python
from contextlib import ExitStack

import numpy as np

import concourse.bass as bass
from concourse import mybir

ALU = mybir.AluOpType
ACT = mybir.ActivationFunctionType
AX_X = mybir.AxisListType.X
F32 = mybir.dt.float32
F32R = mybir.dt.float32r
BF16 = mybir.dt.bfloat16

P = 128
SEQ = 256
T = SEQ // P
D = 2048
KT = D // P
NB = 512
CH = 8
CK = KT // CH
RAW = 4
SPLIT = 4
LEAD = 3
NBANK = 4
DECAY_CHUNK = 64

HEADS = 8
DK = 256
DV = 512
PAIRS = HEADS // 2
INNER = 4096
GROUPS = 8
SHEADS = 64
HPG = SHEADS // GROUPS
HD = 64
TAPS = 4
CONV_KT = 48
FF_GROUPS = 4
RMS_EPS = 1e-6
GN_EPS = 1e-5

U_RET, U_RET_OUT, U_MLP0, U_SSD, U_SSD_OUT, U_MLP1, U_END = 0, 24, 32, 64, 84, 92, 124
B_RET, B_RET_OUT, B_MLP0, B_SSD, B_SSD_OUT, B_MLP1 = 0, 12, 14, 30, 40, 42
F_COLS, F_PHASE0, F_ROW0, F_RET, F_PHASE1, F_PHASE2 = 0, 1, 9, 10, 58, 66
F_DT, F_DT_BACK, F_ROW2, F_DECAY, F_G0, F_G1, F_GTAIL, F_PHASE3 = 74, 75, 76, 77, 78, 85, 169, 174
F_PHASE = (F_PHASE0, F_PHASE1, F_PHASE2, F_PHASE3)

COL_PRE = (0, 32, 16, 48)
COL_GN = 64
COL_SN = 96
COL_CONV = 128
NCOLS = COL_CONV + (TAPS + 1) * CONV_KT


class Fill:

    def __init__(self, static, turns=0):
        self.bank = static % NBANK
        self.full = turns * NBANK + (static + 1)
        self.turn = turns + static // NBANK
        self.static, self.turns = static, turns

    def __add__(self, n):
        return Fill(self.static + n, self.turns)


def squares_before(k):
    return 8 * k + (2 * GROUPS if k > 4 else 0)


class Steps:

    def __init__(self):
        self.base, self.n = 0, 0

    def next(self):
        self.n += 1
        return self.base + self.n

    def loop(self, i, per):
        self.start, self.per = self.base + self.n, per
        self.base, self.n = i * per + self.start, 0

    def end(self, times):
        assert self.n == self.per, (self.n, self.per)
        self.base, self.n = self.start + times * self.per, 0


def hybrid_trunk(nc, x, norm_mix_pre, norm_mix_post, norm_ffn_pre, norm_ffn_post, ret_w_in, ret_gn_w,
                 ret_w_out, ssd_w_in, ssd_conv_w, ssd_conv_b, ssd_dt_bias, ssd_a_log, ssd_d, ssd_norm_w,
                 ssd_w_out, mlp_w_up, mlp_w_down, rot_cos, rot_sin, ret_decay, masks, out):
    with ExitStack() as ctx:
        def sb(name, shape, dt=F32):
            return ctx.enter_context(nc.sbuf_tensor(name, shape, dt))

        def sem(name):
            return ctx.enter_context(nc.semaphore(name))

        h = sb("h", [P, T, D])
        ut_hi = sb("ut_hi", [P, KT, SEQ], F32R)
        ut_lo = sb("ut_lo", [P, KT, SEQ], F32R)
        yt_hi = sb("yt_hi", [P, 2 * KT, SEQ], F32R)
        yt_lo = sb("yt_lo", [P, 2 * KT, SEQ], F32R)
        w_raw = sb("w_raw", [P, RAW, CK, NB])
        w_hi = sb("w_hi", [P, SPLIT, CK, NB], F32R)
        w_lo = sb("w_lo", [P, SPLIT, CK, NB], F32R)
        cols = sb("cols", [P, NCOLS])
        mask = sb("mask", [P, 3, P])
        ident, upto, after = mask[:, 0, :], mask[:, 1, :], mask[:, 2, :]
        ssq = sb("ssq", [P, 8, T, 4])
        var = sb("var", [P, 8, T])
        std = sb("std", [P, 8, T])
        rstd = sb("rstd", [P, 8, T])
        inv_ms = sb("inv_ms", [P, 2, T])
        rms_row = sb("rms_row", [P, SEQ])
        bn = sb("bn", [P, 4, 6])
        mv = sb("mv", [P, 4, 2])
        waited = sb("waited", [P, 1])
        head_var = sb("head_var", [P, 4])
        head_std = sb("head_std", [P, 4])
        head_rstd = sb("head_rstd", [P, 4])
        group_ssq = sb("group_ssq", [P, T])
        group_var = sb("group_var", [P, T])
        group_std = sb("group_std", [P, T])
        group_rstd = sb("group_rstd", [P, T])
        junk = sb("junk", [P, T, NB], BF16)

        arena = sb("arena", [P, 13568])

        def part(at, *shape):
            n = int(np.prod(shape))
            v = arena[:, at:at + n]
            if len(shape) == 2:
                v = v.rearrange("p (a b) -> p a b", a=shape[0])
            if len(shape) == 3:
                v = v.rearrange("p (a b c) -> p a b c", a=shape[0], b=shape[1])
            return v

        cos_t = part(0, SEQ)
        sin_t = part(SEQ, SEQ)
        rms_cols0 = part(512, T, P)
        rot_a = part(1024, 2, NB)
        rot_b = part(2048, 2, NB)
        qt = part(3072, 2, 2, SEQ)
        kt_ = part(4096, 2, 2, SEQ)
        vv = part(5120, 2, T, DV)
        sg = part(7168, 2, T, DV)
        sd = part(9216, 2, 384)
        decay = part(9984, 2, 384)
        rows = part(10752, 4, P)
        acc = part(0, T, D)
        mw = part(4096, T, D)
        zt = part(8192, 2, 2, NB)
        wpost = part(10240, D)
        bt = part(0, GROUPS, SEQ)
        ct = part(2048, GROUPS, SEQ)
        pre = part(4096, 2, NB)
        conv = part(5120, 4, SEQ)
        yoff = part(5120, NB)
        yy = part(6144, T, NB)
        xdt = part(7168, T, NB)
        xoff = part(8192, NB)
        sz = part(8704, T, NB)
        mm = part(9728, 4, NB)
        cb = part(11776, 3, P)
        bcg = part(12160, 2, SEQ)
        dt_raw = part(12288, KT, SHEADS)
        dt = part(12672, T, SHEADS)
        da = part(12800, T, SHEADS)
        edge = part(12928, 2, SHEADS)
        woff = part(13056, SHEADS)
        d_bc = part(13312, SHEADS)
        a_bc = part(13376, SHEADS)
        dtb_bc = part(13440, SHEADS)
        gcol = part(13504, TAPS + 1, 4)
        dt_t = part(7168, SEQ)
        rms_cols2 = part(7424, T, P)
        dx, de, ds_, ds2, dp = (part(6144 + 128 * i, T, SHEADS) for i in range(5))

        gemm = ctx.enter_context(nc.psum_tensor("gemm", [P, 2, T, NB], F32))
        banks = ctx.enter_context(nc.psum_tensor("banks", [P, NBANK, NB], F32))

        raw_full = [sem(f"raw_full{i}") for i in range(RAW)]
        hi_ready, lo_ready, chunk_done = sem("hi_ready"), sem("lo_ready"), sem("chunk_done")
        drained = [sem(f"drained{i}") for i in range(2)]
        bank_full = sem("bank_full")
        consumed = [sem(f"consumed{i}") for i in range(NBANK)]
        x_full = [sem(f"x_full{i}") for i in range(4)]
        const_full, rot_full, ssdc_full = sem("const_full"), sem("rot_full"), sem("ssdc_full")
        decay_full, wpost_full, dtw_full = sem("decay_full"), sem("wpost_full"), sem("dtw_full")
        ut_hi_ready, yt_hi_ready, ht_hi_ready = sem("ut_hi_ready"), sem("yt_hi_ready"), sem("ht_hi_ready")
        h_ready, squares_done = sem("h_ready"), sem("squares_done")
        var_ready, std_ready, rstd_ready = sem("var_ready"), sem("std_ready"), sem("rstd_ready")
        dve_step, pool_step = sem("dve_step"), sem("pool_step")
        rot_done, head_var_ready, head_std_ready = sem("rot_done"), sem("head_var_ready"), sem("head_std_ready")
        head_rstd_ready, y_scaled = sem("head_rstd_ready"), sem("y_scaled")
        rms_cols_ready, ht_lo_ready = sem("rms_cols_ready"), sem("ht_lo_ready")
        conv_done = sem("conv_done")
        squared, acc_zero, mw_ready = sem("squared"), sem("acc_zero"), sem("mw_ready")
        dtw_hi_ready, dtw_lo_ready = sem("dtw_hi_ready"), sem("dtw_lo_ready")
        dt_abs, dt_exp, a_exp, da_ready = sem("dt_abs"), sem("dt_exp"), sem("a_exp"), sem("da_ready")
        woff_ready, conv_silu, bcg_ready = sem("woff_ready"), sem("conv_silu"), sem("bcg_ready")
        da_masked, m_done, x_ready, gated = sem("da_masked"), sem("m_done"), sem("x_ready"), sem("gated")
        group_var_ready = sem("group_var_ready")
        group_std_ready, group_rstd_ready = sem("group_std_ready"), sem("group_rstd_ready")
        group_scaled, out_done = sem("group_scaled"), sem("out_done")

        w_in_v = ret_w_in[0].rearrange("(k p) n -> p k n", p=P)
        w_ro_v = ret_w_out[0].rearrange("(k p) n -> p k n", p=P)
        w_si_v = ssd_w_in[0].rearrange("(k p) n -> p k n", p=P)
        w_so_v = ssd_w_out[0].rearrange("(k p) n -> p k n", p=P)
        w_up_v = [mlp_w_up[i].rearrange("(k p) n -> p k n", p=P) for i in range(2)]
        w_dn_v = [mlp_w_down[i].rearrange("(k p) n -> p k n", p=P) for i in range(2)]

        block = ctx.enter_context(nc.Block())

        @block.sync
        def _(sp):
            def load_unit(u, w, kt0, col):
                for c in range(CH):
                    free = u * CH + (c - RAW + 1)
                    if not isinstance(free, int) or free > 0:
                        sp.wait_ge(lo_ready, free)
                    sp.dma_start(w_raw[:, c % RAW, :, :],
                                 w[:, bass.ds(kt0 + CK * c, CK), bass.ds(col, NB)]
                                 ).then_inc(raw_full[c % RAW], 16)

            def load_pair(p):
                u = p * 6 + U_RET
                load_unit(u, w_in_v, 0, p * 512)
                if not isinstance(p, int):
                    f = Fill(F_RET + 3, (p - 1) * 3)
                    sp.wait_ge(consumed[f.bank], f.turn + 1)
                sp.dma_start(decay, ret_decay[:, bass.ds(p * 768, 768)].rearrange("p (a b) -> p a b", a=2)
                             ).then_inc(decay_full, 16)
                load_unit(u + 1, w_in_v, 0, p * 512 + 2048)
                for i in range(2):
                    load_unit(u + (2 + i), w_in_v, 0, p * 1024 + (4096 + 512 * i))
                for i in range(2):
                    load_unit(u + (4 + i), w_in_v, 0, p * 1024 + (8192 + 512 * i))

            def load_out(u0, w):
                for b in range(4):
                    for half in range(2):
                        load_unit(u0 + 2 * b + half, w, KT * half, NB * b)

            def load_mlp(u0, layer):
                with sp.Fori(0, FF_GROUPS) as g:
                    for j in range(4):
                        load_unit(g * 8 + (u0 + j), w_up_v[layer], 0, g * 2048 + NB * j)
                    for j in range(4):
                        load_unit(g * 8 + (u0 + 4 + j), w_dn_v[layer], g * KT, NB * j)

            for i in range(4):
                sp.dma_start(h[:, :, NB * i:NB * (i + 1)],
                             x[0].rearrange("(t p) d -> p t d", p=P)[:, :, NB * i:NB * (i + 1)]
                             ).then_inc(x_full[i], 16)
            load_pair(0)
            with sp.Fori(1, PAIRS) as p:
                load_pair(p)
            load_out(U_RET_OUT, w_ro_v)
            load_mlp(U_MLP0, 0)
            for k, col in enumerate((8192, 8704, 9216, 9728)):
                load_unit(U_SSD + k, w_si_v, 0, col)
            with sp.Fori(1, GROUPS + 1) as g1:
                load_unit(g1 * 2 + (U_SSD + 2), w_si_v, 0, g1 * NB + (INNER - NB))
                load_unit(g1 * 2 + (U_SSD + 3), w_si_v, 0, g1 * NB + (-NB))
            load_out(U_SSD_OUT, w_so_v)
            load_mlp(U_MLP1, 1)
            for i in range(4):
                sp.wait_ge(h_ready, 24 + 2 * (i + 1))
                sp.dma_start(out[0].rearrange("(t p) d -> p t d", p=P)[:, :, NB * i:NB * (i + 1)],
                             h[:, :, NB * i:NB * (i + 1)]).then_inc(out_done, 16)
            sp.wait_ge(out_done, 64)

        @block.tensor
        def _(pe):
            def chunk(u, c, hi, lo, kt0, par, start, stop):
                pe.wait_ge(lo_ready, u * CH + (c + 1))
                s = c % SPLIT
                for kk in range(CK):
                    k = kt0 + CK * c + kk
                    first = start and c == 0 and kk == 0
                    last = stop and c == CH - 1 and kk == CK - 1
                    for t in range(T):
                        o = gemm[:, par, t, :]
                        a_hi, a_lo = hi[:, k, P * t:P * (t + 1)], lo[:, k, P * t:P * (t + 1)]
                        pe.matmul(o, a_hi, w_hi[:, s, kk, :], start=first, stop=False)
                        pe.matmul(o, a_hi, w_lo[:, s, kk, :], start=False, stop=False)
                        mm_ = pe.matmul(o, a_lo, w_hi[:, s, kk, :], start=False, stop=last)
                mm_.then_inc(chunk_done, 1)

            def chunk_t(u, c, par):
                pe.wait_ge(lo_ready, u * CH + (c + 1))
                s = c % SPLIT
                for kk in range(CK):
                    k = CK * c + kk
                    for r in range(4):
                        o = gemm[:, par, r // 2, SEQ * (r % 2):SEQ * (r % 2 + 1)]
                        b_hi, b_lo = w_hi[:, s, kk, P * r:P * (r + 1)], w_lo[:, s, kk, P * r:P * (r + 1)]
                        pe.matmul(o, b_hi, ut_hi[:, k, :], start=(k == 0 and r % 2 == 0), stop=False)
                        pe.matmul(o, b_hi, ut_lo[:, k, :], start=False, stop=False)
                        mm_ = pe.matmul(o, b_lo, ut_hi[:, k, :], start=False, stop=(k == KT - 1 and r % 2 == 1))
                mm_.then_inc(chunk_done, 1)

            def unit(u, par, turn, hi=ut_hi, lo=ut_lo, kt0=0, start=True, stop=True, turned=False, before={}, after_={}):
                if start and (not isinstance(turn, int) or turn > 0):
                    pe.wait_ge(drained[par], turn * 4)
                for c in range(CH):
                    for f in before.get(c, ()):
                        f()
                    if turned:
                        chunk_t(u, c, par)
                    else:
                        chunk(u, c, hi, lo, kt0, par, start, stop)
                    for f in after_.get(c, ()):
                        f()

            def unit_t(u, par, turn, before={}, after_={}):
                unit(u, par, turn, turned=True, before=before, after_=after_)

            def free(f):
                if not isinstance(f.turn, int) or f.turn > 0:
                    pe.wait_ge(consumed[f.bank], f.turn)

            def turn_to_channels(f, src):
                free(f)
                for kk in range(2):
                    for t in range(T):
                        at = SEQ * kk + P * t
                        tr = pe.transpose(banks[:, f.bank, at:at + P], src(t, kk), ident)
                tr.then_inc(bank_full, 1)

            def norm_fill(phase, j):
                if phase == 0:
                    pe.wait_ge(x_full[j // 2], 16)
                else:
                    pe.wait_ge(h_ready, 8 * (phase - 1) + 2 * (j // 2) + 2)
                turn_to_channels(Fill(F_PHASE[phase] + j),
                                 lambda t, kk: h[:, t, P * (2 * j + kk):P * (2 * j + kk + 1)])

            def ut_ready(phase, j):
                f = Fill(F_PHASE[phase] + j)
                pe.wait_ge(consumed[f.bank], f.turn + 1)

            def first_unit(phase, u, turn, more={}):
                for j in range(3):
                    norm_fill(phase, j)
                aft = {c: [lambda c=c: norm_fill(phase, c + 3)] for c in range(5)}
                for c, fs in more.items():
                    aft[c] = aft.get(c, []) + list(fs)
                unit_t(u, 0, turn, before={c: [lambda c=c: ut_ready(phase, c)] for c in range(CH)}, after_=aft)

            def rms_fill(f, n, src):
                pe.wait_ge(rms_cols_ready, n)
                free(f)
                for t in range(T):
                    tr = pe.transpose(banks[:, f.bank, P * t:P * (t + 1)], src[:, t, :], ident)
                tr.then_inc(bank_full, 1)

            pe.wait_ge(const_full, 16 * 10)
            at = 0
            for i, n in enumerate((128, 96, 96, 48)):
                tr = pe.transpose(banks[:, 0, at:at + n], rows[0:n, i, :], ident[0:n, 0:n])
                at += n
            tr.then_inc(bank_full, 1)

            def scores(p, f, hh):
                pe.wait_ge(rot_done, p * 8 + (4 + 2 * (hh + 1)))
                for mt in range(T):
                    g = f + (2 * hh + mt)
                    free(g)
                    w = SEQ - P * mt
                    for k in range(2):
                        s_ = pe.matmul(banks[:, g.bank, 0:w], kt_[:, hh, k, P * mt:P * (mt + 1)],
                                       qt[:, hh, k, P * mt:SEQ], start=(k == 0), stop=(k == 1))
                    s_.then_inc(bank_full, 1)

            def values(p, fs, f, hh):
                for mt in range(T):
                    g = fs + (2 * hh + mt)
                    pe.wait_ge(consumed[g.bank], g.turn + 1)
                pe.wait_ge(drained[hh], (p * 3 + (B_RET + 1)) * 4 + 4)
                for t in range(T):
                    g = f + (2 * hh + t)
                    free(g)
                    o = banks[:, g.bank, :]
                    v_ = pe.matmul(o, sd[:, hh, P * t:P * (t + 1)], vv[:, hh, 0, :], start=True, stop=(t == 0))
                    if t == 1:
                        v_ = pe.matmul(o, sd[:, hh, 256:384], vv[:, hh, 1, :], start=False, stop=True)
                    v_.then_inc(bank_full, 1)

            def heads_out(f, p, hh):
                pe.wait_ge(y_scaled, p * 4 + 2 * (hh + 1))
                for j in range(2):
                    turn_to_channels(f + (2 * hh + j),
                                     lambda t, kk: sg[:, hh, t, P * (2 * j + kk):P * (2 * j + kk + 1)])

            def pair_fill(p, idx):
                return Fill(F_RET + idx, p * 3)

            def pair_rest(p):
                u, b = p * 6 + U_RET, p * 3 + B_RET
                unit_t(u + 1, 1, b, after_={1: [lambda: rms_fill(Fill(F_ROW0), 1, rms_cols0)]} if isinstance(p, int) else {})
                unit(u + 2, 0, b + 1)
                unit(u + 3, 1, b + 1, after_={3: [lambda: scores(p, pair_fill(p, 0), 0)],
                                              5: [lambda: scores(p, pair_fill(p, 0), 1)]})
                unit(u + 4, 0, b + 2)
                unit(u + 5, 1, b + 2, after_={1: [lambda: values(p, pair_fill(p, 0), pair_fill(p, 4), 0)],
                                              3: [lambda: values(p, pair_fill(p, 0), pair_fill(p, 4), 1)]})

            def pair_tail(p):
                return {5: [lambda: heads_out(pair_fill(p, 8), p, 0)], 7: [lambda: heads_out(pair_fill(p, 8), p, 1)]}

            first_unit(0, U_RET, B_RET)
            pair_rest(0)
            with pe.Fori(1, PAIRS) as p:
                unit_t(p * 6 + U_RET, 0, p * 3 + B_RET, after_=pair_tail(p - 1))
                pair_rest(p)

            def yt_wait(f):
                return [lambda: pe.wait_ge(consumed[f.bank], f.turn + 1)]

            def out_projection(u0, b0, tail0, tail1, waits0, waits1):
                for b in range(4):
                    unit(u0 + 2 * b, b % 2, b0 + b // 2, yt_hi, yt_lo, 0, True, False,
                         after_=tail0 if b == 0 else {}, before=waits0 if b == 0 else {})
                    unit(u0 + 2 * b + 1, b % 2, b0 + b // 2, yt_hi, yt_lo, KT, False, True,
                         after_=tail1 if b == 0 else {}, before=waits1 if b == 0 else {})

            out_projection(
                U_RET_OUT, B_RET_OUT, pair_tail(3), {},
                {0: [w for j in range(4) for w in yt_wait(pair_fill(2, 8 + j))]},
                {4 + j: yt_wait(pair_fill(3, 8 + j)) for j in range(4)})

            def mlp(phase, u0, b0):
                def hidden_wait(g, c):
                    pe.wait_ge(ht_lo_ready, (g + (phase // 2) * FF_GROUPS) * 8 + (c + 1))

                def rest(g):
                    u, b = g * 8 + u0, g * 4 + b0
                    for j in range(1, 4):
                        unit_t(u + j, j % 2, b + j // 2)
                    unit(u + 4, 0, b + 2, yt_hi, yt_lo,
                         before={c: [lambda c=c: hidden_wait(g, c)] for c in range(CH)})
                    for j in range(1, 4):
                        unit(u + 4 + j, j % 2, b + 2 + j // 2, yt_hi, yt_lo)

                first_unit(phase, u0, b0)
                with pe.Fori(0, FF_GROUPS - 1) as g:
                    rest(g)
                    unit_t(g * 8 + (u0 + 8), 0, g * 4 + (b0 + 4))
                rest(FF_GROUPS - 1)

            mlp(1, U_MLP0, B_MLP0)

            def dt_product():
                pe.wait_ge(dtw_lo_ready, 1)
                ut_ready(2, CH - 1)
                f = Fill(F_DT)
                free(f)
                wh = yt_hi[:, 28:32, :].rearrange("p a (b n) -> p (a b) n", n=SHEADS)
                wl = yt_lo[:, 28:32, :].rearrange("p a (b n) -> p (a b) n", n=SHEADS)
                o = banks[0:SHEADS, f.bank, 0:SEQ]
                for k in range(KT):
                    pe.matmul(o, wh[:, k, :], ut_hi[:, k, :], start=(k == 0), stop=False)
                    pe.matmul(o, wh[:, k, :], ut_lo[:, k, :], start=False, stop=False)
                    m_ = pe.matmul(o, wl[:, k, :], ut_hi[:, k, :], start=False, stop=(k == KT - 1))
                m_.then_inc(bank_full, 1)

            def dt_back():
                f = Fill(F_DT)
                pe.wait_ge(consumed[f.bank], f.turn + 1)
                f = Fill(F_DT_BACK)
                free(f)
                for t in range(T):
                    tr = pe.transpose(banks[:, f.bank, SHEADS * t:SHEADS * (t + 1)],
                                      dt_t[0:SHEADS, P * t:P * (t + 1)], ident[0:SHEADS, 0:SHEADS])
                tr.then_inc(bank_full, 1)

            def decay_sums():
                pe.wait_ge(da_ready, 1)
                f = Fill(F_DECAY)
                free(f)
                pe.matmul(banks[:, f.bank, 0:SHEADS], after, da[:, 0, :], start=True, stop=True)
                pe.matmul(banks[:, f.bank, SHEADS:2 * SHEADS], upto, da[:, 1, :], start=True, stop=True
                          ).then_inc(bank_full, 1)

            def group_cb(g, f):
                pe.wait_ge(bcg_ready, g + 1)
                free(f)
                pe.matmul(banks[:, f.bank, 0:SEQ], bcg[:, 0, 0:P], bcg[:, 1, :], start=True, stop=True)
                pe.matmul(banks[:, f.bank, SEQ:SEQ + P], bcg[:, 0, P:SEQ], bcg[:, 1, P:SEQ], start=True, stop=True
                          ).then_inc(bank_full, 1)

            def group_seg(g, f, i):
                pe.wait_ge(da_masked, g * 4 + (i + 1))
                free(f + i)
                pe.matmul(banks[:, (f + i).bank, :], after, mm[:, i, :], start=True, stop=True
                          ).then_inc(bank_full, 1)

            def back_fills(g, f):
                pe.wait_ge(conv_silu, g * 2 + 10)
                for t in range(T):
                    free(f + t)
                    for k in range(4):
                        b_ = pe.transpose(banks[:, (f + t).bank, P * k:P * (k + 1)],
                                          conv[:, k, P * t:P * (t + 1)], ident)
                    b_.then_inc(bank_full, 1)

            def group_y(g, f):
                pe.wait_ge(x_ready, g * 5 + 3)
                pe.wait_ge(m_done, g * 4 + 4)
                for t in range(T):
                    free(f + t)
                    for hh in range(HPG):
                        y_ = pe.matmul(banks[:, (f + t).bank, HD * hh:HD * (hh + 1)],
                                       mm[:, 2 * t + hh // 4, P * (hh % 4):P * (hh % 4 + 1)],
                                       xdt[:, t, HD * hh:HD * (hh + 1)], start=True, stop=True)
                    y_.then_inc(bank_full, 1)
                free(f + 2)
                pe.matmul(banks[:, (f + 2).bank, :], cb[:, 1, :], xoff, start=True, stop=True
                          ).then_inc(bank_full, 1)

            def group_out(g, f):
                pe.wait_ge(group_scaled, g * 2 + 2)
                for i in range(2):
                    turn_to_channels(f + i, lambda t, kk: yy[:, t, P * (2 * i + kk):P * (2 * i + kk + 1)])

            first_unit(2, U_SSD, B_SSD, {6: [dt_product]})
            unit_t(U_SSD + 1, 1, B_SSD, after_={0: [dt_back], 1: [lambda: rms_fill(Fill(F_ROW2), 2, rms_cols2)],
                                                6: [decay_sums]})
            unit_t(U_SSD + 2, 0, B_SSD + 1)
            unit_t(U_SSD + 3, 1, B_SSD + 1)
            unit_t(U_SSD + 4, 0, B_SSD + 2, after_={
                4: [lambda: group_cb(0, Fill(F_G0)), lambda: group_seg(0, Fill(F_G0 + 1), 0)],
                5: [lambda: group_seg(0, Fill(F_G0 + 1), 1)],
                6: [lambda: group_seg(0, Fill(F_G0 + 1), 2)],
                7: [lambda: group_seg(0, Fill(F_G0 + 1), 3)]})
            unit(U_SSD + 5, 1, B_SSD + 2, after_={6: [lambda: back_fills(0, Fill(F_G0 + 5))]})
            with pe.Fori(1, GROUPS) as g:
                def gf(idx):
                    return Fill(F_G1 + idx, (g - 1) * 3)
                unit_t(g * 2 + (U_SSD + 4), 0, g + (B_SSD + 2), after_={
                    2: [lambda: group_y(g - 1, gf(0))],
                    4: [lambda: group_cb(g, gf(3)), lambda: group_seg(g, gf(4), 0)],
                    5: [lambda: group_seg(g, gf(4), 1)],
                    6: [lambda: group_seg(g, gf(4), 2)],
                    7: [lambda: group_seg(g, gf(4), 3)]})
                unit(g * 2 + (U_SSD + 5), 1, g + (B_SSD + 2), after_={
                    2: [lambda: group_out(g - 1, gf(8))],
                    6: [lambda: back_fills(g, gf(10))]})
            out_projection(
                U_SSD_OUT, B_SSD_OUT, {2: [lambda: group_y(7, Fill(F_GTAIL))]},
                {2: [lambda: group_out(7, Fill(F_GTAIL + 3))]},
                {0: [w for j in range(2) for w in yt_wait(Fill(F_G1 + 72 + 8 + j))]},
                {6 + j: yt_wait(Fill(F_GTAIL + 3 + j)) for j in range(2)})
            mlp(3, U_MLP1, B_MLP1)

        @block.scalar
        def _(act):
            def slot(u, c):
                u, c = u + (c + LEAD) // CH, (c + LEAD) % CH
                if isinstance(u, int) and u >= U_END:
                    return
                act.wait_ge(raw_full[c % RAW], (u * 2 + (c // RAW + 1)) * 16)
                freed = u * CH + (c - SPLIT + 1)
                if not isinstance(freed, int) or freed > 0:
                    act.wait_ge(chunk_done, freed)
                act.activation(w_hi[:, c % SPLIT, :, :], w_raw[:, c % RAW, :, :], ACT.Copy
                               ).then_inc(hi_ready, 1)

            def unit(u, at={}):
                for c in range(CH):
                    slot(u, c)
                    for f in at.get(c, ()):
                        f()

            def block_done(u):
                act.wait_ge(chunk_done, u * CH + CH)

            def split_fill(f, dst, k, col, ready):
                act.wait_ge(bank_full, f.full)
                if col is None:
                    act.activation(dst[:, bass.ds(k, 2), :].rearrange("p a b -> p (a b)"), banks[:, f.bank, :], ACT.Copy
                                   ).then_inc(ready, 1)
                    return
                for kk in range(2):
                    s_ = act.activation(dst[:, k + kk, :], banks[:, f.bank, SEQ * kk:SEQ * (kk + 1)], ACT.Copy,
                                        scale=cols[:, bass.ds(col + kk, 1)])
                s_.then_inc(ready, 1)

            def square(src, t, total, n):
                if not isinstance(n, int) or n >= T:
                    act.wait_ge(squares_done, n - (T - 1))
                act.activation(junk[:, t, :], src, ACT.Square, accum_out=total).then_inc(squares_done, 1)

            def norm_hi(phase, j):
                split_fill(Fill(F_PHASE[phase] + j), ut_hi, 2 * j, COL_PRE[phase] + 2 * j, ut_hi_ready)

            def squares(phase, b):
                if phase == 0:
                    act.wait_ge(x_full[b], 16)
                else:
                    act.wait_ge(h_ready, 8 * (phase - 1) + 2 * b + 2)
                for t in range(T):
                    square(h[:, t, NB * b:NB * (b + 1)], t, ssq[:, 2 * phase, t, b:b + 1],
                           squares_before(2 * phase) + 2 * b + t)

            def root(k):
                act.wait_ge(var_ready, k + 1)
                act.activation(std[:, k, :], var[:, k, :], ACT.Sqrt).then_inc(std_ready, 1)

            def first_unit(phase, u, more={}):
                if phase > 0:
                    root(2 * phase - 1)
                for j in range(3):
                    norm_hi(phase, j)
                at = {c: [lambda c=c: norm_hi(phase, c + 3)] for c in range(5)}
                for b, c in enumerate((1, 3, 4, 5)):
                    at.setdefault(c, []).append(lambda b=b: squares(phase, b))
                at.setdefault(7, []).append(lambda: root(2 * phase))
                for c, fs in more.items():
                    at[c] = list(fs) + at.get(c, [])
                unit(u, at)

            for i, (src, n) in enumerate((
                    (norm_mix_pre.rearrange("l (k c) -> (l k) c", c=P), 32),
                    (norm_ffn_pre.rearrange("l (k c) -> (l k) c", c=P), 32),
                    (ret_gn_w.rearrange("l (k c) -> (l k) c", c=P), 32),
                    (ssd_norm_w.rearrange("l (k c) -> (l k) c", c=P), 32))):
                act.dma_start(rows[32 * i:32 * (i + 1), 0, :], src).then_inc(const_full, 16)
            conv_rows = ssd_conv_w[0].rearrange("a (k c) -> a k c", c=P)
            for i in range(TAPS):
                act.dma_start(rows[CONV_KT * (i % 2):CONV_KT * (i % 2 + 1), 1 + i // 2, :], conv_rows[i]
                              ).then_inc(const_full, 16)
            act.dma_start(rows[0:CONV_KT, 3, :], ssd_conv_b.rearrange("l (k c) -> (l k) c", c=P)
                          ).then_inc(const_full, 16)
            act.dma_start(mask[:, :, :], masks.rearrange("p (a b) -> p a b", a=3)).then_inc(const_full, 16)
            act.dma_start(cos_t, rot_cos[:, :]).then_inc(rot_full, 16)
            act.dma_start(sin_t, rot_sin[:, :]).then_inc(rot_full, 16)
            for dst, src in ((d_bc, ssd_d), (a_bc, ssd_a_log), (dtb_bc, ssd_dt_bias)):
                act.dma_start(dst, src.to_broadcast([P, SHEADS])
                              ).then_inc(ssdc_full, 16)

            def load_wpost(src, f_or_u):
                act.wait_ge(chunk_done, f_or_u * CH)
                act.dma_start(wpost, src.to_broadcast([P, D])).then_inc(wpost_full, 16)

            for c in range(LEAD):
                slot(-1, CH - LEAD + c)
            act.wait_ge(consumed[0], 1)

            def pair_fill(p, idx):
                return Fill(F_RET + idx, p * 3)

            def evacuate_block(u, par, dst, func, k):
                block_done(u)
                act.wait_ge(rstd_ready, k + 1)
                for t in range(T):
                    act.activation(dst[:, t, :], gemm[:, par, t, :], func, scale=rstd[:, k, t:t + 1]
                                   ).then_inc(drained[par], 2)

            def head_root(p):
                act.wait_ge(head_var_ready, p + 1)
                act.activation(head_std[:, :], head_var[:, :], ACT.Sqrt).then_inc(head_std_ready, 1)

            def heads_hi(p, hh):
                for j in (2 * hh, 2 * hh + 1):
                    split_fill(pair_fill(p, 8 + j), yt_hi, p * 8 + 2 * j, p * 8 + (COL_GN + 2 * j), yt_hi_ready)

            def pair_rest(p):
                u = p * 6 + U_RET
                unit(u + 1)
                unit(u + 2)
                unit(u + 3, {0: [lambda: evacuate_block(u + 2, 0, vv[:, 0], ACT.Copy, 0)]})
                unit(u + 4, {0: [lambda: evacuate_block(u + 3, 1, vv[:, 1], ACT.Copy, 0)]})
                unit(u + 5, {0: [lambda: evacuate_block(u + 4, 0, sg[:, 0], ACT.Silu, 0)]})

            def pair_tail(p):
                return {0: [lambda: evacuate_block(p * 6 + (U_RET + 5), 1, sg[:, 1], ACT.Silu, 0)],
                        2: [lambda: head_root(p)], 6: [lambda: heads_hi(p, 0)]}

            first_unit(0, U_RET)
            pair_rest(0)
            with act.Fori(1, PAIRS) as p:
                unit(p * 6 + U_RET, pair_tail(p - 1))
                heads_hi(p - 1, 1)
                pair_rest(p)

            def square_block(u, par, k, b):
                block_done(u)
                for t in range(T):
                    square(gemm[:, par, t, :], t, ssq[:, k, t, b:b + 1], squares_before(k) + 2 * b + t)

            def out_projection(u0, k, post, tail0, tail1):
                for b in range(4):
                    at = dict(tail0) if b == 0 else {0: [lambda b=b: square_block(u0 + 2 * b - 1, (b - 1) % 2, k, b - 1)]}
                    unit(u0 + 2 * b, at)
                    at = dict(tail1) if b == 0 else {}
                    if b == 0:
                        at[6] = [lambda: load_wpost(post, u0 + 1)]
                    unit(u0 + 2 * b + 1, at)
                square_block(u0 + 7, 1, k, 3)

            out_projection(U_RET_OUT, 1, norm_mix_post[0:1, :], pair_tail(3), {0: [lambda: heads_hi(3, 1)]})

            def mlp(phase, u0, post):
                def hidden(g, j):
                    block_done(g * 8 + (u0 + j))
                    for i in range(2):
                        act.activation(zt[:, j % 2, i, :], gemm[:, j % 2, i, :], ACT.Relu).then_inc(drained[j % 2], 2)

                def hidden_hi(g, j):
                    for i in range(2):
                        act.wait_ge(squared, (g + (phase // 2) * FF_GROUPS) * 8 + (2 * j + i + 1))
                        act.activation(yt_hi[:, 4 * j + 2 * i:4 * j + 2 * i + 2, :].rearrange("p a b -> p (a b)"),
                                       zt[:, j % 2, i, :], ACT.Copy).then_inc(ht_hi_ready, 1)

                def rest(g, last):
                    u = g * 8 + u0
                    for j in range(1, 5):
                        unit(u + j, {0: [lambda j=j: hidden(g, j - 1)], 2: [lambda j=j: hidden_hi(g, j - 1)]})
                    for j in range(1, 4):
                        unit(u + 4 + j, {2: [lambda j=j: square_acc(j - 1)]} if last else {})

                def square_acc(d):
                    act.wait_ge(drained[d % 2], (b_last + d // 2) * 4 + 4)
                    for t in range(T):
                        square(acc[:, t, NB * d:NB * (d + 1)], t, ssq[:, 2 * phase + 1, t, d:d + 1],
                               squares_before(2 * phase + 1) + 2 * d + t)

                b0 = B_MLP0 if phase == 1 else B_MLP1
                b_last = b0 + 4 * (FF_GROUPS - 1) + 2
                first_unit(phase, u0)
                with act.Fori(0, FF_GROUPS - 1) as g:
                    rest(g, False)
                    unit(g * 8 + (u0 + 8))
                load_wpost(post, u0 + 8)
                if phase == 1:
                    act.dma_start(dt_raw, w_si_v[:, :, 10240:10304]).then_inc(dtw_full, 16)
                rest(FF_GROUPS - 1, True)
                square_acc(3)

            mlp(1, U_MLP0, norm_ffn_post[0:1, :])

            def dt_hi():
                act.wait_ge(dtw_full, 16)
                act.activation(yt_hi[:, 28:32, :].rearrange("p a b -> p (a b)"),
                               dt_raw.rearrange("p a b -> p (a b)"), ACT.Copy).then_inc(dtw_hi_ready, 1)

            def exp_abs():
                act.wait_ge(dt_abs, 1)
                act.activation(de, de, ACT.Exp, scale=-1.0).then_inc(dt_exp, 1)

            def exp_a():
                act.wait_ge(ssdc_full, 48)
                act.activation(a_bc, a_bc, ACT.Exp).then_inc(a_exp, 1)

            def exp_edges():
                f = Fill(F_DECAY)
                act.wait_ge(bank_full, f.full)
                act.activation(edge, banks[:, f.bank, 0:2 * SHEADS].rearrange("p (a b) -> p a b", a=2), ACT.Exp
                               ).then_inc(consumed[f.bank], 1)

            def dt_out():
                f = Fill(F_DT)
                act.wait_ge(bank_full, f.full)
                act.activation(dt_t[0:SHEADS, :], banks[0:SHEADS, f.bank, 0:SEQ], ACT.Copy).then_inc(consumed[f.bank], 1)

            def conv_out(n, i, dst):
                act.wait_ge(conv_done, n + (i + 1))
                act.activation(dst, conv[:, 2 * i:2 * i + 2, :], ACT.Silu).then_inc(conv_silu, 1)

            def exp_seg(f, i):
                g = f + i
                act.wait_ge(bank_full, g.full)
                act.activation(mm[:, i, :], banks[:, g.bank, :], ACT.Exp).then_inc(consumed[g.bank], 1)

            def group_square(g):
                act.wait_ge(gated, g * 2 + 2)
                for t in range(T):
                    square(yy[:, t, :], t, group_ssq[:, t:t + 1], g * 2 + (40 + t))

            def group_root(g):
                act.wait_ge(group_var_ready, g + 1)
                act.activation(group_std[:, :], group_var[:, :], ACT.Sqrt).then_inc(group_std_ready, 1)

            def group_hi(g, f):
                for i in range(2):
                    split_fill(f + i, yt_hi, g * 4 + 2 * i, g * 4 + (COL_SN + 2 * i), yt_hi_ready)

            def bc_silu(k, c0=3):
                dst = (bt, ct)[k // 2]
                return {c0 + 2 * i: [lambda i=i: conv_out(2 * k, i, dst[:, 4 * (k % 2) + 2 * i:4 * (k % 2) + 2 * i + 2, :])]
                        for i in range(2)}

            def merged(*ats):
                out_ = {}
                for at in ats:
                    for c, fs in at.items():
                        out_.setdefault(c, []).extend(fs)
                return out_

            first_unit(2, U_SSD, {0: [dt_hi]})
            dt_out()
            unit(U_SSD + 1, merged({2: [exp_a, exp_abs]}, bc_silu(0, 5)))
            exp_edges()
            unit(U_SSD + 2, bc_silu(1))
            unit(U_SSD + 3, bc_silu(2))
            unit(U_SSD + 4, merged(bc_silu(3), {
                5: [lambda: exp_seg(Fill(F_G0 + 1), 0)], 6: [lambda: exp_seg(Fill(F_G0 + 1), 1)],
                7: [lambda: exp_seg(Fill(F_G0 + 1), 2)]}))

            def x_silu(g):
                return {3 + 2 * i: [lambda i=i: conv_out(g * 2 + 8, i, conv[:, 2 * i:2 * i + 2, :])] for i in range(2)}

            unit(U_SSD + 5, merged({0: [lambda: exp_seg(Fill(F_G0 + 1), 3)]}, x_silu(0)))
            with act.Fori(1, GROUPS) as g:
                def gf(idx):
                    return Fill(F_G1 + idx, (g - 1) * 3)
                u = g * 2 + (U_SSD + 4)
                unit(u, {0: [lambda: evacuate_block(u - 1, 1, sz, ACT.Silu, 4)],
                         5: [lambda: exp_seg(gf(4), 0)], 6: [lambda: exp_seg(gf(4), 1)],
                         7: [lambda: exp_seg(gf(4), 2), lambda: group_square(g - 1)]})
                unit(u + 1, merged({0: [lambda: exp_seg(gf(4), 3)]}, {
                    1: [lambda: group_root(g - 1)],
                    3: [lambda: group_hi(g - 1, gf(8))]}, x_silu(g)))
            out_projection(U_SSD_OUT, 5, norm_mix_post[1:2, :], {
                0: [lambda: evacuate_block(U_SSD + 19, 1, sz, ACT.Silu, 4)],
                7: [lambda: group_square(7)]},
                {1: [lambda: group_root(7)], 3: [lambda: group_hi(7, Fill(F_GTAIL + 3))]})
            mlp(3, U_MLP1, norm_ffn_post[1:2, :])
            root(7)

        @block.vector
        def _(dve):
            steps = Steps()

            def slot(u, c):
                u, c = u + (c + LEAD) // CH, (c + LEAD) % CH
                if isinstance(u, int) and u >= U_END:
                    return
                dve.wait_ge(hi_ready, u * CH + (c + 1))
                dve.tensor_tensor(w_lo[:, c % SPLIT, :, :], w_raw[:, c % RAW, :, :],
                                  w_hi[:, c % SPLIT, :, :].bitcast(F32), ALU.subtract).then_inc(lo_ready, 1)

            def unit(u, at={}):
                for c in range(CH):
                    slot(u, c)
                    for f in at.get(c, ()):
                        f()

            def block_done(u):
                dve.wait_ge(chunk_done, u * CH + CH)

            def split_fill(f, hi, lo, k, col, ready, n):
                dve.wait_ge(ready, n)
                if col is None:
                    dve.tensor_tensor(lo[:, k:k + 2, :].rearrange("p a b -> p (a b)"), banks[:, f.bank, :],
                                      hi[:, k:k + 2, :].rearrange("p a b -> p (a b)").bitcast(F32),
                                      ALU.subtract).then_inc(consumed[f.bank], 1)
                    return
                for kk in range(2):
                    s_ = dve.scalar_tensor_tensor(
                        out=lo[:, k + kk, :], in0=banks[:, f.bank, SEQ * kk:SEQ * (kk + 1)],
                        scalar=cols[:, bass.ds(col + kk, 1)], in1=hi[:, k + kk, :].bitcast(F32),
                        op0=ALU.mult, op1=ALU.subtract)
                s_.then_inc(consumed[f.bank], 1)

            def norm_lo(phase, j):
                split_fill(Fill(F_PHASE[phase] + j), ut_hi, ut_lo, 2 * j, COL_PRE[phase] + 2 * j,
                           ut_hi_ready, 8 * phase + j + 1)

            def mean_square(k):
                n = steps.next()
                dve.tensor_reduce(var[:, k, :], ssq[:, k, :, :], AX_X, ALU.add).then_inc(dve_step, 1)
                dve.wait_ge(dve_step, n)
                dve.tensor_scalar(var[:, k, :], var[:, k, :], 1.0 / D, RMS_EPS, ALU.mult, ALU.add
                                  ).then_inc(var_ready, 1)

            def inverse(k):
                dve.wait_ge(std_ready, k + 1)
                dve.reciprocal(rstd[:, k, :], std[:, k, :]).then_inc(rstd_ready, 1)

            def pre_norm(phase):
                dve.wait_ge(squares_done, squares_before(2 * phase) + 8)
                mean_square(2 * phase)
                inverse(2 * phase)
                if phase % 2 == 1:
                    dve.wait_ge(rstd_ready, 2 * phase + 1)
                    n = steps.next()
                    r = rstd[:, 2 * phase, :]
                    dve.tensor_tensor(inv_ms[:, phase // 2, :], r, r, ALU.mult).then_inc(dve_step, 1)
                    dve.wait_ge(dve_step, n)

            def residual(k, b):
                dve.wait_ge(rstd_ready, k + 1)
                for t in range(T):
                    hb = h[:, t, NB * b:NB * (b + 1)]
                    dve.scalar_tensor_tensor(out=hb, in0=mw[:, t, NB * b:NB * (b + 1)], scalar=rstd[:, k, t:t + 1],
                                             in1=hb, op0=ALU.mult, op1=ALU.add).then_inc(h_ready, 1)

            def first_unit(phase, u, more={}):
                if phase > 0:
                    mean_square(2 * phase - 1)
                    inverse(2 * phase - 1)
                    residual(2 * phase - 1, 0)
                norm_lo(phase, 0)
                if phase > 0:
                    residual(2 * phase - 1, 1)
                norm_lo(phase, 1)
                norm_lo(phase, 2)
                at = {c: [lambda c=c: norm_lo(phase, c + 3)] for c in range(5)}
                if phase > 0:
                    at[0].append(lambda: residual(2 * phase - 1, 2))
                    at[2].append(lambda: residual(2 * phase - 1, 3))
                at.setdefault(7, []).append(lambda: pre_norm(phase))
                for c, fs in more.items():
                    at[c] = list(fs) + at.get(c, [])
                unit(u, at)

            for c in range(LEAD):
                slot(-1, CH - LEAD + c)
            dve.wait_ge(bank_full, 1)
            dve.tensor_copy(cols[:, 0:COL_CONV], banks[:, 0, 0:COL_CONV])
            dve.tensor_copy(cols[:, COL_CONV:NCOLS], banks[:, 0, COL_CONV:NCOLS]).then_inc(consumed[0], 1)
            dve.wait_ge(consumed[0], 1)

            def pair_fill(p, idx):
                return Fill(F_RET + idx, p * 3)

            def spread_rms(k, dst):
                dve.wait_ge(rstd_ready, k + 1)
                dve.tensor_copy(dst, rstd[:, k, :].unsqueeze(2).to_broadcast([P, T, P])).then_inc(rms_cols_ready, 1)

            def scale_tables():
                dve.wait_ge(rot_full, 32)
                f = Fill(F_ROW0)
                dve.wait_ge(bank_full, f.full)
                n = steps.next()
                dve.tensor_tensor(cos_t, cos_t, banks[:, f.bank, 0:SEQ], ALU.mult).then_inc(dve_step, 1)
                dve.tensor_tensor(sin_t, sin_t, banks[:, f.bank, 0:SEQ], ALU.mult).then_inc(consumed[f.bank], 1)
                dve.wait_ge(dve_step, n)
                dve.wait_ge(consumed[f.bank], f.turn + 1)

            def rotate(p, k):
                block_done(p * 6 + (U_RET + k))
                if not isinstance(p, int) or k > 0:
                    dve.wait_ge(rot_done, p * 8 + 4 * k)
                for hh in range(2):
                    for dst, table in ((rot_a, cos_t), (rot_b, sin_t)):
                        r_ = dve.tensor_tensor(dst[:, hh, :].rearrange("p (i n) -> p i n", i=2),
                                               gemm[:, k, hh, :].rearrange("p (i n) -> p i n", i=2),
                                               table.unsqueeze(1).to_broadcast([P, 2, SEQ]), ALU.mult)
                    r_.then_inc(drained[k], 2)

            def decay_scores(p, hh):
                dve.wait_ge(decay_full, p * 16 + 16)
                for mt in range(T):
                    f = pair_fill(p, 2 * hh + mt)
                    dve.wait_ge(bank_full, f.full)
                    a, w = 256 * mt, SEQ - P * mt
                    dve.tensor_tensor(sd[:, hh, a:a + w], banks[:, f.bank, 0:w], decay[:, hh, a:a + w], ALU.mult
                                      ).then_inc(consumed[f.bank], 1)

            def head_stats(p, hh):
                for t in range(T):
                    f = pair_fill(p, 4 + 2 * hh + t)
                    i = 2 * hh + t
                    dve.wait_ge(bank_full, f.full)
                    n = steps.next()
                    dve.bn_stats(bn[:, i, :], banks[:, f.bank, :]).then_inc(dve_step, 1)
                    dve.wait_ge(dve_step, n)
                    dve.memset(waited[:, :], 0.0)
                    n = steps.next()
                    dve.bn_aggr(mv[:, i, :], bn[:, i, :]).then_inc(dve_step, 1)
                dve.wait_ge(dve_step, n)

            def head_gate(p, hh):
                dve.wait_ge(drained[hh], (p * 3 + (B_RET + 2)) * 4 + 4)
                for t in range(T):
                    f = pair_fill(p, 4 + 2 * hh + t)
                    i = 2 * hh + t
                    dve.scalar_tensor_tensor(out=sg[:, hh, t, :], in0=banks[:, f.bank, :], scalar=mv[:, i, 0:1],
                                             in1=sg[:, hh, t, :], op0=ALU.subtract, op1=ALU.mult
                                             ).then_inc(consumed[f.bank], 1)

            def head_variance(p):
                dve.tensor_scalar(head_var[:, :], mv[:, :, 1], GN_EPS, None, ALU.add).then_inc(head_var_ready, 1)

            def head_inverse(p):
                dve.wait_ge(head_std_ready, p + 1)
                dve.reciprocal(head_rstd[:, :], head_std[:, :]).then_inc(head_rstd_ready, 1)

            def heads_lo(p, hh):
                for j in (2 * hh, 2 * hh + 1):
                    split_fill(pair_fill(p, 8 + j), yt_hi, yt_lo, p * 8 + 2 * j, p * 8 + (COL_GN + 2 * j),
                               yt_hi_ready, p * 4 + (j + 1))

            def pair_rest(p):
                u = p * 6 + U_RET
                if isinstance(p, int):
                    unit(u + 1, {0: [lambda: spread_rms(0, rms_cols0)], 2: [scale_tables, lambda: rotate(p, 0)]})
                else:
                    unit(u + 1, {0: [lambda: rotate(p, 0)]})
                unit(u + 2, {0: [lambda: rotate(p, 1)]})
                unit(u + 3, {4: [lambda: decay_scores(p, 0)], 6: [lambda: decay_scores(p, 1)]})
                unit(u + 4)
                unit(u + 5, {2: [lambda: head_stats(p, 0), lambda: head_gate(p, 0)], 4: [lambda: head_stats(p, 1)]})

            def pair_tail(p):
                return {0: [lambda: head_variance(p)], 1: [lambda: head_gate(p, 1)], 3: [lambda: head_inverse(p)],
                        6: [lambda: heads_lo(p, 0)]}

            first_unit(0, U_RET)
            pair_rest(0)
            with dve.Fori(1, PAIRS) as p:
                steps.loop(p - 1, 8)
                unit(p * 6 + U_RET, pair_tail(p - 1))
                heads_lo(p - 1, 1)
                pair_rest(p)
                steps.end(PAIRS - 1)

            def weigh_block(u, par, b, n):
                block_done(u)
                dve.wait_ge(squares_done, squares_before(1 if n == 1 else 5) + 2 * b + 2)
                dve.wait_ge(wpost_full, 16 * n)
                for t in range(T):
                    dve.tensor_tensor(mw[:, t, NB * b:NB * (b + 1)], gemm[:, par, t, :],
                                      wpost[:, NB * b:NB * (b + 1)], ALU.mult).then_inc(drained[par], 2)

            def out_projection(u0, b0, n, tail0, tail1):
                for b in range(4):
                    at = dict(tail0) if b == 0 else {0: [lambda b=b: weigh_block(u0 + 2 * b - 1, (b - 1) % 2, b - 1, n)]}
                    unit(u0 + 2 * b, at)
                    unit(u0 + 2 * b + 1, tail1 if b == 0 else {})
                weigh_block(u0 + 7, 1, 3, n)
                for par in range(2):
                    dve.wait_ge(drained[par], 4 * (b0 + 2))

            out_projection(U_RET_OUT, B_RET_OUT, 1, pair_tail(3), {0: [lambda: heads_lo(3, 1)]})

            def mlp(phase, u0, b0):
                def hidden_lo(g, j):
                    for i in range(2):
                        dve.wait_ge(ht_hi_ready, (g + (phase // 2) * FF_GROUPS) * 8 + (2 * j + i + 1))
                        k = 4 * j + 2 * i
                        dve.tensor_tensor(yt_lo[:, k:k + 2, :].rearrange("p a b -> p (a b)"), zt[:, j % 2, i, :],
                                          yt_hi[:, k:k + 2, :].rearrange("p a b -> p (a b)").bitcast(F32),
                                          ALU.subtract).then_inc(ht_lo_ready, 1)

                def add_block(u, d):
                    block_done(u)
                    dve.wait_ge(acc_zero, phase // 2 + 1)
                    for t in range(T):
                        a = acc[:, t, NB * d:NB * (d + 1)]
                        dve.scalar_tensor_tensor(out=a, in0=gemm[:, d % 2, t, :], scalar=inv_ms[:, phase // 2, t:t + 1],
                                                 in1=a, op0=ALU.mult, op1=ALU.add).then_inc(drained[d % 2], 2)

                def rest(g):
                    u = g * 8 + u0
                    for j in range(1, 5):
                        unit(u + j, {3: [lambda j=j: hidden_lo(g, j - 1)]})
                    for j in range(1, 4):
                        unit(u + 4 + j, {0: [lambda j=j: add_block(u + 3 + j, j - 1)]})

                first_unit(phase, u0)
                with dve.Fori(0, FF_GROUPS - 1) as g:
                    rest(g)
                    unit(g * 8 + (u0 + 8), {0: [lambda: add_block(g * 8 + (u0 + 7), 3)]})
                rest(FF_GROUPS - 1)
                add_block(u0 + 31, 3)
                dve.wait_ge(squares_done, squares_before(2 * phase + 1) + 8)
                dve.wait_ge(mw_ready, (phase // 2 + 1) * 8)

            mlp(1, U_MLP0, B_MLP0)

            def dt_lo():
                dve.wait_ge(dtw_hi_ready, 1)
                dve.tensor_tensor(yt_lo[:, 28:32, :].rearrange("p a b -> p (a b)"), dt_raw.rearrange("p a b -> p (a b)"),
                                  yt_hi[:, 28:32, :].rearrange("p a b -> p (a b)").bitcast(F32), ALU.subtract
                                  ).then_inc(dtw_lo_ready, 1)

            def chained(make):
                n = steps.next()
                make().then_inc(dve_step, 1)
                dve.wait_ge(dve_step, n)

            def dt_input():
                f = Fill(F_DT_BACK)
                dve.wait_ge(bank_full, f.full)
                dve.wait_ge(rstd_ready, 5)
                dve.wait_ge(ssdc_full, 48)
                for t in range(T):
                    s_ = dve.scalar_tensor_tensor(out=dx[:, t, :], in0=banks[:, f.bank, SHEADS * t:SHEADS * (t + 1)],
                                                  scalar=rstd[:, 4, t:t + 1], in1=dtb_bc, op0=ALU.mult, op1=ALU.add)
                s_.then_inc(consumed[f.bank], 1)
                dve.wait_ge(consumed[f.bank], f.turn + 1)
                dve.scalar_tensor_tensor(out=de, in0=dx, scalar=-1.0, in1=dx, op0=ALU.mult, op1=ALU.max
                                         ).then_inc(dt_abs, 1)

            def dt_chain():
                dve.wait_ge(dt_exp, 1)
                dve.wait_ge(a_exp, 1)
                chained(lambda: dve.tensor_scalar(ds2, de, 2.0, None, ALU.add))
                chained(lambda: dve.reciprocal(ds2, ds2))
                chained(lambda: dve.tensor_tensor(ds_, de, ds2, ALU.mult))
                chained(lambda: dve.tensor_tensor(ds2, ds_, ds_, ALU.mult))
                chained(lambda: dve.tensor_scalar(dp, ds2, 1.0 / 15, None, ALU.mult))
                for k in (13, 11, 9, 7, 5, 3):
                    chained(lambda: dve.scalar_tensor_tensor(out=dp, in0=dp, scalar=1.0 / k, in1=ds2,
                                                             op0=ALU.add, op1=ALU.mult))
                chained(lambda: dve.scalar_tensor_tensor(out=dp, in0=dp, scalar=1.0, in1=ds_,
                                                         op0=ALU.add, op1=ALU.mult))
                chained(lambda: dve.tensor_scalar(dx, dx, 0.0, None, ALU.max))
                chained(lambda: dve.scalar_tensor_tensor(out=dt, in0=dp, scalar=2.0, in1=dx,
                                                         op0=ALU.mult, op1=ALU.add))
                for t in range(T):
                    s_ = dve.scalar_tensor_tensor(out=da[:, t, :], in0=dt[:, t, :], scalar=-1.0, in1=a_bc,
                                                  op0=ALU.mult, op1=ALU.mult)
                s_.then_inc(da_ready, 1)

            def edge_weights():
                f = Fill(F_DECAY)
                dve.wait_ge(consumed[f.bank], f.turn + 1)
                dve.tensor_tensor(woff, edge[:, 0, :], dt[:, 0, :], ALU.mult).then_inc(woff_ready, 1)

            def conv_columns(k):
                chained(lambda: dve.tensor_copy(
                    gcol, cols[:, COL_CONV:NCOLS].rearrange("p (a k) -> p a k", k=CONV_KT)[:, :, bass.ds(k, 4)]))

            def load_rms_row():
                f = Fill(F_ROW2)
                dve.wait_ge(bank_full, f.full)
                dve.tensor_copy(rms_row[:, :], banks[:, f.bank, 0:SEQ]).then_inc(consumed[f.bank], 1)
                dve.wait_ge(consumed[f.bank], f.turn + 1)

            def before_conv(u, par, turn):
                block_done(u)
                for i in range(2):
                    dve.tensor_tensor(pre[:, i, :].rearrange("p (a n) -> p a n", a=2),
                                      gemm[:, par, i, :].rearrange("p (a n) -> p a n", a=2),
                                      rms_row[:, :].unsqueeze(1).to_broadcast([P, 2, SEQ]), ALU.mult
                                      ).then_inc(drained[par], 2)
                dve.wait_ge(drained[par], turn * 4 + 4)

            def convolve(i, n):
                if not isinstance(n, int) or n > 0:
                    dve.wait_ge(conv_silu, n)
                for kk in range(2):
                    k = 2 * i + kk
                    s = steps.next()
                    dve.tensor_scalar(conv[:, k, :], pre[:, i, SEQ * kk:SEQ * (kk + 1)], gcol[:, 3, k:k + 1],
                                      gcol[:, 4, k:k + 1], ALU.mult, ALU.add).then_inc(dve_step, 1)
                for back in (1, 2, 3):
                    for kk in range(2):
                        k = 2 * i + kk
                        dve.wait_ge(dve_step, s - 1 + kk)
                        i_ = dve.scalar_tensor_tensor(
                            out=conv[:, k, back:SEQ], in0=pre[:, i, SEQ * kk:SEQ * (kk + 1) - back],
                            scalar=gcol[:, 3 - back, k:k + 1], in1=conv[:, k, back:SEQ], op0=ALU.mult, op1=ALU.add)
                        if back < 3:
                            i_.then_inc(dve_step, 1)
                    if back < 3:
                        steps.next()
                        s = steps.next()
                i_.then_inc(conv_done, 1)

            def mask_cb(f):
                dve.wait_ge(bank_full, f.full)
                for i in (0, 1, 2):
                    o, v = cb[:, i, :], banks[:, f.bank, P * i:P * (i + 1)]
                    c_ = dve.tensor_copy(o, v) if i == 1 else dve.tensor_tensor(o, v, upto, ALU.mult)
                c_.then_inc(consumed[f.bank], 1)

            def weigh_scores(f, fcb, i):
                g = f + i
                dve.wait_ge(consumed[g.bank], g.turn + 1)
                if i == 0:
                    dve.wait_ge(consumed[fcb.bank], fcb.turn + 1)
                m4 = mm[:, i, :].rearrange("p (a b) -> p a b", a=4)
                dve.tensor_tensor(m4, m4, cb[:, 2 * (i // 2), :].unsqueeze(1).to_broadcast([P, 4, P]), ALU.mult
                                  ).then_inc(m_done, 1)

            def x_back(f):
                for t in range(T):
                    g = f + t
                    dve.wait_ge(bank_full, g.full)
                    dve.tensor_copy(yy[:, t, :], banks[:, g.bank, :]).then_inc(consumed[g.bank], 1)

            def gather_y(g, f):
                dve.wait_ge(x_ready, g * 5 + 5)
                for t in range(T):
                    fb = f + t
                    dve.wait_ge(bank_full, fb.full)
                    dve.tensor_tensor(yy[:, t, :], banks[:, fb.bank, :], yy[:, t, :], ALU.add
                                      ).then_inc(consumed[fb.bank], 1)
                fb = f + 2
                dve.wait_ge(bank_full, fb.full)
                dve.tensor_tensor(yoff.rearrange("p (a b) -> p a b", a=HPG),
                                  banks[:, fb.bank, :].rearrange("p (a b) -> p a b", a=HPG),
                                  edge[:, 1, bass.ds(g * HPG, HPG)].unsqueeze(2).to_broadcast([P, HPG, HD]),
                                  ALU.mult).then_inc(consumed[fb.bank], 1)

            def group_variance(g):
                dve.wait_ge(squares_done, g * 2 + 42)
                dve.tensor_scalar(group_var[:, :], group_ssq[:, :], 1.0 / NB, RMS_EPS, ALU.mult, ALU.add
                                  ).then_inc(group_var_ready, 1)

            def group_inverse(g):
                dve.wait_ge(group_std_ready, g + 1)
                dve.reciprocal(group_rstd[:, :], group_std[:, :]).then_inc(group_rstd_ready, 1)

            def group_lo(g, f):
                for i in range(2):
                    split_fill(f + i, yt_hi, yt_lo, g * 4 + 2 * i, g * 4 + (COL_SN + 2 * i),
                               yt_hi_ready, g * 2 + (16 + i + 1))

            def conv_unit(u, par, turn, k, n, c0=0, first=()):
                return {c0: list(first) + [lambda: before_conv(u, par, turn), lambda: conv_columns(k)],
                        c0 + 1: [lambda: convolve(0, n)], c0 + 3: [lambda: convolve(1, n)]}

            def bc_conv(k, c0=0, first=()):
                return conv_unit(U_SSD + k, k % 2, B_SSD + k // 2, 32 + 4 * k, 2 * k, c0, first)

            def x_conv(g):
                return conv_unit(g * 2 + (U_SSD + 4), 0, g + (B_SSD + 2), g * 4, g * 2 + 8)

            def merged(*ats):
                out_ = {}
                for at in ats:
                    for c, fs in at.items():
                        out_.setdefault(c, []).extend(fs)
                return out_

            first_unit(2, U_SSD, {0: [dt_lo]})
            spread_rms(4, rms_cols2)
            unit(U_SSD + 1, merged({1: [dt_input], 4: [dt_chain]}, bc_conv(0, 2, [load_rms_row])))
            unit(U_SSD + 2, merged({0: [edge_weights]}, bc_conv(1)))
            unit(U_SSD + 3, bc_conv(2))
            unit(U_SSD + 4, merged(bc_conv(3), {6: [lambda: mask_cb(Fill(F_G0))]}))
            f0 = Fill(F_G0 + 1)
            unit(U_SSD + 5, merged(x_conv(0), {
                0: [lambda: weigh_scores(f0, Fill(F_G0), 0), lambda: weigh_scores(f0, Fill(F_G0), 1)],
                1: [lambda: weigh_scores(f0, Fill(F_G0), 2), lambda: weigh_scores(f0, Fill(F_G0), 3)],
                7: [lambda: x_back(Fill(F_G0 + 5))]}))
            with dve.Fori(1, GROUPS) as g:
                steps.loop(g - 1, 13)

                def gf(idx):
                    return Fill(F_G1 + idx, (g - 1) * 3)
                u = g * 2 + (U_SSD + 4)
                unit(u, {3: [lambda: gather_y(g - 1, gf(0))],
                         5: [lambda: mask_cb(gf(3))]})
                unit(u + 1, merged(x_conv(g), {
                    0: [lambda: weigh_scores(gf(4), gf(3), 0),
                        lambda: weigh_scores(gf(4), gf(3), 1), lambda: group_variance(g - 1)],
                    1: [lambda: weigh_scores(gf(4), gf(3), 2), lambda: weigh_scores(gf(4), gf(3), 3),
                        lambda: group_inverse(g - 1)],
                    3: [lambda: group_lo(g - 1, gf(8))],
                    7: [lambda: x_back(gf(10))]}))
                steps.end(GROUPS - 1)
            out_projection(U_SSD_OUT, B_SSD_OUT, 3, {
                3: [lambda: gather_y(7, Fill(F_GTAIL))]},
                {0: [lambda: group_variance(7)], 1: [lambda: group_inverse(7)],
                 3: [lambda: group_lo(7, Fill(F_GTAIL + 3))]})
            mlp(3, U_MLP1, B_MLP1)
            mean_square(7)
            inverse(7)
            for b in range(4):
                residual(7, b)

        @block.gpsimd
        def _(pool):
            steps = Steps()

            def rotate_add(p, k):
                dst = (qt, kt_)[k]
                for hh in range(2):
                    pool.wait_ge(drained[k], (p * 3 + B_RET) * 4 + 2 * (hh + 1))
                    for i in range(2):
                        pool.tensor_tensor(dst[:, hh, i, :], rot_a[:, hh, SEQ * i:SEQ * (i + 1)],
                                           rot_b[:, hh, SEQ * (1 - i):SEQ * (2 - i)], (ALU.subtract, ALU.add)[i]
                                           ).then_inc(rot_done, 1)

            def heads_scale(p):
                pool.wait_ge(head_rstd_ready, p + 1)
                for i in range(4):
                    if i % 2 == 0:
                        f = Fill(F_RET + 4 + i, p * 3)
                        pool.wait_ge(consumed[f.bank], f.turn + 1)
                        f = f + 1
                        pool.wait_ge(consumed[f.bank], f.turn + 1)
                    y = sg[:, i // 2, i % 2, :]
                    pool.tensor_tensor(y, y, head_rstd[:, i:i + 1].to_broadcast([P, NB]), ALU.mult).then_inc(y_scaled, 1)

            with pool.Fori(0, PAIRS) as p:
                rotate_add(p, 0)
                rotate_add(p, 1)
                heads_scale(p)

            def mlp(phase, u0, b0):
                pool.wait_ge(h_ready, 8 * phase)
                pool.memset(acc, 0.0).then_inc(acc_zero, 1)
                with pool.Fori(0, FF_GROUPS) as g:
                    for j in range(4):
                        for i in range(2):
                            pool.wait_ge(drained[j % 2], (g * 4 + (b0 + j // 2)) * 4 + 2 * (i + 1))
                            z = zt[:, j % 2, i, :]
                            pool.tensor_tensor(z, z, z, ALU.mult).then_inc(squared, 1)
                pool.wait_ge(wpost_full, 16 * (phase + 1))
                for d in range(4):
                    for t in range(T):
                        pool.wait_ge(drained[d % 2], (b0 + 14 + d // 2) * 4 + 2 * (t + 1))
                        c = slice(NB * d, NB * (d + 1))
                        pool.tensor_tensor(mw[:, t, c], acc[:, t, c], wpost[:, c], ALU.mult).then_inc(mw_ready, 1)

            mlp(1, U_MLP0, B_MLP0)

            def copy_bc(g):
                pool.tensor_copy(bcg[:, 0, :], bt[:, g, :])
                pool.tensor_copy(bcg[:, 1, :], ct[:, g, :]).then_inc(bcg_ready, 1)

            def mask_da(g):
                for i in range(4):
                    t, q = i // 2, i % 2
                    pool.tensor_tensor(mm[:, i, :].rearrange("p (a b) -> p a b", a=4),
                                       upto.unsqueeze(1).to_broadcast([P, 4, P]),
                                       da[:, t, bass.ds(g * HPG + 4 * q, 4)].unsqueeze(2).to_broadcast([P, 4, P]),
                                       ALU.mult).then_inc(da_masked, 1)

            def x_products(g, back):
                def per_head(v):
                    return v.rearrange("p (a b) -> p a b", a=HPG)

                def head_row(v):
                    return v[:, bass.ds(g * HPG, HPG)].unsqueeze(2).to_broadcast([P, HPG, HD])
                for t in range(T):
                    f = back + t
                    pool.wait_ge(consumed[f.bank], f.turn + 1)
                    pool.tensor_tensor(per_head(xdt[:, t, :]), per_head(yy[:, t, :]), head_row(dt[:, t, :]), ALU.mult
                                       ).then_inc(x_ready, 1)
                pool.tensor_tensor(per_head(xoff), per_head(yy[:, 0, :]), head_row(woff), ALU.mult
                                   ).then_inc(x_ready, 1)
                for t in range(T):
                    pool.tensor_tensor(per_head(yy[:, t, :]), per_head(yy[:, t, :]), head_row(d_bc), ALU.mult
                                       ).then_inc(x_ready, 1)

            def gate(g, f):
                for i in range(3):
                    pool.wait_ge(consumed[(f + i).bank], (f + i).turn + 1)
                n = steps.next()
                pool.tensor_tensor(yy[:, 1, :], yy[:, 1, :], yoff, ALU.add).then_inc(pool_step, 1)
                pool.wait_ge(drained[1], (g + (B_SSD + 2)) * 4 + 4)
                pool.tensor_tensor(yy[:, 0, :], yy[:, 0, :], sz[:, 0, :], ALU.mult).then_inc(gated, 1)
                pool.wait_ge(pool_step, n)
                pool.tensor_tensor(yy[:, 1, :], yy[:, 1, :], sz[:, 1, :], ALU.mult).then_inc(gated, 1)

            def group_scale(g):
                pool.wait_ge(group_rstd_ready, g + 1)
                for t in range(T):
                    pool.tensor_tensor(yy[:, t, :], yy[:, t, :], group_rstd[:, t:t + 1].to_broadcast([P, NB]),
                                       ALU.mult).then_inc(group_scaled, 1)

            pool.wait_ge(da_ready, 1)
            pool.wait_ge(woff_ready, 1)
            mask_da(0)
            pool.wait_ge(conv_silu, 6)
            copy_bc(0)
            pool.wait_ge(conv_silu, 8)
            with pool.Fori(1, GROUPS) as g:
                def gf(idx):
                    return Fill(F_G1 + idx, (g - 1) * 3)
                x_products(g - 1, Fill(F_G1 - 2, (g - 1) * 3))
                steps.loop(g - 1, 1)
                copy_bc(g)
                pool.wait_ge(bank_full, gf(2).full)
                mask_da(g)
                gate(g - 1, gf(0))
                steps.end(GROUPS - 1)
                group_scale(g - 1)
            x_products(7, Fill(F_GTAIL - 2))
            gate(7, Fill(F_GTAIL))
            group_scale(7)
            mlp(3, U_MLP1, B_MLP1)


_INS = ["x", "norm_mix_pre", "norm_mix_post", "norm_ffn_pre", "norm_ffn_post", "ret_w_in", "ret_gn_w", "ret_w_out",
        "ssd_w_in", "ssd_conv_w", "ssd_conv_b", "ssd_dt_bias", "ssd_a_log", "ssd_d", "ssd_norm_w", "ssd_w_out",
        "mlp_w_up", "mlp_w_down"]
_OUTS = [((1, SEQ, D), "float32")]


def _constants():
    f32 = np.float32
    half = DK // 2
    inv_freq = (f32(10000.0) ** (-np.arange(half, dtype=f32) / f32(half))).astype(f32)
    ang = (np.arange(SEQ, dtype=f32)[:, None] * inv_freq[None, :]).astype(np.float64)
    cos, sin = np.cos(ang), np.sin(ang)
    log_gamma = np.log1p(-np.exp2(-5.0 - np.arange(HEADS)))
    n = np.arange(SEQ)
    seen = (n[:, None] // DECAY_CHUNK) <= (n[None, :] // DECAY_CHUNK)
    full = np.exp(np.abs(n[:, None] - n[None, :])[None] * log_gamma[:, None, None]) * seen * DK ** -0.5
    tiles = np.concatenate([full[:, 0:P, :], full[:, P:SEQ, P:SEQ]], axis=2)
    i = np.arange(P)
    masks = np.stack([i[:, None] == i[None, :], i[:, None] <= i[None, :], i[:, None] > i[None, :]], axis=1)
    return {
        "rot_cos": np.ascontiguousarray(cos.T).astype(f32),
        "rot_sin": np.ascontiguousarray(sin.T).astype(f32),
        "ret_decay": np.ascontiguousarray(tiles.transpose(1, 0, 2).reshape(P, -1)).astype(f32),
        "masks": np.ascontiguousarray(masks.reshape(P, -1)).astype(f32),
    }


def kernel(**inputs):
    import numpy as _np
    import concourse.bacc as _bacc
    from concourse import mybir as _mybir
    from concourse.bass_utils import run_bass_kernel_spmd as _run

    nc = _bacc.Bacc("TRN2", target_bir_lowering=False, num_devices=1, dynamic_dma_scratch_size=1024)
    arrays, args = {}, []
    named = [(name, _np.ascontiguousarray(inputs[name])) for name in _INS] + list(_constants().items())
    for name, a in named:
        arrays[f"in_{name}_dram"] = a
        args.append(nc.dram_tensor(f"in_{name}_dram", a.shape, _mybir.dt.from_np(a.dtype), kind="ExternalInput").ap())
    for i, (shape, dtype) in enumerate(_OUTS):
        dt = _mybir.dt.from_np(_np.dtype(dtype))
        args.append(nc.dram_tensor(f"out_{i}_dram", shape, dt, kind="ExternalOutput").ap())
    hybrid_trunk(nc, *args)
    r = _run(nc, [arrays], core_ids=[0])
    got = tuple(r.results[0][f"out_{i}_dram"] for i in range(len(_OUTS)))
    return got[0]
```

```python
from contextlib import ExitStack

import numpy as np

import concourse.bass as bass
from concourse import mybir

ALU = mybir.AluOpType
ACT = mybir.ActivationFunctionType
AX_X = mybir.AxisListType.X
F32 = mybir.dt.float32
F32R = mybir.dt.float32r
BF16 = mybir.dt.bfloat16

P = 128
SEQ = 256
T = SEQ // P
D = 2048
KT = D // P
NB = 512
CH = 8
CK = KT // CH
RAW = 4
SPLIT = 4
LEAD = 3
NBANK = 4
DECAY_CHUNK = 64

HEADS = 8
DK = 256
DV = 512
PAIRS = HEADS // 2
INNER = 4096
GROUPS = 8
SHEADS = 64
HPG = SHEADS // GROUPS
HD = 64
TAPS = 4
CONV_KT = 48
FF_GROUPS = 4
RMS_EPS = 1e-6
GN_EPS = 1e-5

U_RET, U_RET_OUT, U_MLP0, U_SSD, U_SSD_OUT, U_MLP1, U_END = 0, 24, 32, 64, 84, 92, 124
B_RET, B_RET_OUT, B_MLP0, B_SSD, B_SSD_OUT, B_MLP1 = 0, 12, 14, 30, 40, 42
F_PHASE0 = 0
F_ROW0 = F_PHASE0 + 8
F_RET = F_ROW0 + 1
F_PHASE1 = F_RET + 12 * PAIRS
F_PHASE2 = F_PHASE1 + 8
F_DT = F_PHASE2 + 8
F_DT_BACK, F_ROW2, F_DECAY = F_DT + 1, F_DT + 2, F_DT + 3
F_G0 = F_DECAY + 1
F_G1 = F_G0 + 7
F_GTAIL = F_G1 + 12 * (GROUPS - 1)
F_PHASE3 = F_GTAIL + 5
F_PHASE = (F_PHASE0, F_PHASE1, F_PHASE2, F_PHASE3)

COL_FFN = 32
COL_PRE = (0, COL_FFN, 16, COL_FFN + 16)
COL_GN = 64
COL_SN = 96
COL_CONV = 128
NCOLS = COL_CONV + (TAPS + 1) * CONV_KT
CONST_LOADS = 6


class Fill:

    def __init__(self, static, turns=0):
        self.bank = static % NBANK
        self.full = turns * NBANK + (static + 1)
        self.turn = turns + static // NBANK
        self.static, self.turns = static, turns

    def __add__(self, n):
        return Fill(self.static + n, self.turns)


def squares_before(k):
    return 8 * k + (2 * GROUPS if k > 4 else 0)


def residual_source(k, b, t, drained, mw_ready):
    if k % 4 == 1:
        return drained[b % 2], 4 * ((B_RET_OUT if k == 1 else B_SSD_OUT) + b // 2) + 2 * (t + 1)
    return mw_ready, 8 * (k // 4) + 2 * b + t + 1


POOL_FROM = 2


def residual_counts(k, j):
    f = POOL_FROM
    return ((f + 8) * (k // 2) + j + 1 + min(j + 1, f), (8 - f) * (k // 2) + max(j + 1 - f, 0))


class Steps:

    def __init__(self):
        self.base, self.n = 0, 0

    def next(self):
        self.n += 1
        return self.base + self.n

    def loop(self, i, per):
        self.start, self.per = self.base + self.n, per
        self.base, self.n = i * per + self.start, 0

    def end(self, times):
        assert self.n == self.per, (self.n, self.per)
        self.base, self.n = self.start + times * self.per, 0


def hybrid_trunk(nc, x, norm_mix_pre, norm_mix_post, norm_ffn_pre, norm_ffn_post, ret_w_in, ret_gn_w,
                 ret_w_out, ssd_w_in, ssd_conv_w, ssd_conv_b, ssd_dt_bias, ssd_a_log, ssd_d, ssd_norm_w,
                 ssd_w_out, mlp_w_up, mlp_w_down, rot_cos, rot_sin, ret_decay, masks, out):
    with ExitStack() as ctx:
        def sb(name, shape, dt=F32):
            return ctx.enter_context(nc.sbuf_tensor(name, shape, dt))

        def sem(name):
            return ctx.enter_context(nc.semaphore(name))

        h = sb("h", [P, T, D])
        ut_hi = sb("ut_hi", [P, KT, SEQ], F32R)
        ut_lo = sb("ut_lo", [P, KT, SEQ], F32R)
        yt_hi = sb("yt_hi", [P, 2 * KT, SEQ], F32R)
        yt_lo = sb("yt_lo", [P, 2 * KT, SEQ], F32R)
        w_raw = sb("w_raw", [P, RAW, CK, NB])
        w_hi = sb("w_hi", [P, SPLIT, CK, NB], F32R)
        w_lo = sb("w_lo", [P, SPLIT, CK, NB], F32R)
        cols = sb("cols", [P, NCOLS])
        mask = sb("mask", [P, 3, P])
        ident, upto, after = mask[:, 0, :], mask[:, 1, :], mask[:, 2, :]
        ssq = sb("ssq", [P, 8, T, 4])
        var = sb("var", [P, 8, T])
        std = sb("std", [P, 8, T])
        rstd = sb("rstd", [P, 8, T])
        inv_ms = sb("inv_ms", [P, 2, T])
        rms_row = sb("rms_row", [P, SEQ])
        bn = sb("bn", [P, 4, 6])
        mv = sb("mv", [P, 4, 2])
        waited = sb("waited", [P, 1])
        head_var = sb("head_var", [P, 4])
        head_std = sb("head_std", [P, 4])
        head_rstd = sb("head_rstd", [P, 4])
        group_ssq = sb("group_ssq", [P, T])
        group_var = sb("group_var", [P, T])
        group_std = sb("group_std", [P, T])
        group_rstd = sb("group_rstd", [P, T])
        junk = sb("junk", [P, T, NB], BF16)

        split = sb("split", [P, 2 * 384], F32R)
        sd_hi, sd_lo = split[:, 0:384], split[:, 384:768]
        after_r = split[:, 0:P]
        da_hi, da_lo = (split[:, a:a + T * SHEADS].rearrange("p (t h) -> p t h", t=T) for a in (128, 256))
        arena = sb("arena", [P, 13568])

        def part(at, *shape):
            n = int(np.prod(shape))
            v = arena[:, at:at + n]
            if len(shape) == 2:
                v = v.rearrange("p (a b) -> p a b", a=shape[0])
            if len(shape) == 3:
                v = v.rearrange("p (a b c) -> p a b c", a=shape[0], b=shape[1])
            return v

        cos_t = part(0, SEQ)
        sin_t = part(SEQ, SEQ)
        rms_cols0 = part(512, T, P)
        rot_a = part(1024, 2, NB)
        rot_b = part(2048, 2, NB)
        qt = part(3072, 2, 2, SEQ)
        kt_ = part(4096, 2, 2, SEQ)
        v_hi, v_lo = (y[:, 24:32, :].rearrange("p (h t k) n -> p h t (k n)", h=2, t=T) for y in (yt_hi, yt_lo))
        sg = part(7168, 2, T, DV)
        sd = part(9216, 2, 384)
        decay = part(9984, 2, 384)
        rows = part(10752, 4, P)
        acc = part(0, T, D)
        mw = part(4096, T, D)
        zt = part(8192, 2, 2, NB)
        wpost = part(10240, D)
        bt = part(0, GROUPS, SEQ)
        ct = part(2048, GROUPS, SEQ)
        pre = part(4096, 2, NB)
        conv = part(5120, 4, SEQ)
        yoff = part(5120, NB)
        yy = part(6144, T, NB)
        xdt = part(7168, T, NB)
        xoff = part(8192, NB)
        sz = part(8704, T, NB)
        mm = part(9728, 4, NB)
        masked_hi = yt_hi[:, 24:32, :].rearrange("p (i k) n -> p i (k n)", i=4)
        masked_lo = yt_lo[:, 24:32, :].rearrange("p (i k) n -> p i (k n)", i=4)
        cb = part(11776, 3, P)
        bcg = part(12160, 2, SEQ)
        dt_raw = part(12288, KT, SHEADS)
        dt = part(12672, T, SHEADS)
        da = part(12800, T, SHEADS)
        edge = part(12928, 2, SHEADS)
        woff = part(13056, SHEADS)
        d_bc = part(13312, SHEADS)
        a_bc = part(13376, SHEADS)
        dtb_bc = part(13440, SHEADS)
        gcol = part(13504, TAPS + 1, 4)
        dt_t = part(7168, SEQ)
        rms_cols2 = part(7424, T, P)
        dx, de, ds_, ds2, dp = (part(6144 + 128 * i, T, SHEADS) for i in range(5))

        gemm = ctx.enter_context(nc.psum_tensor("gemm", [P, 2, T, NB], F32))
        banks = ctx.enter_context(nc.psum_tensor("banks", [P, NBANK, NB], F32))

        raw_full = [sem(f"raw_full{i}") for i in range(RAW)]
        hi_ready, lo_ready, chunk_done = sem("hi_ready"), sem("lo_ready"), sem("chunk_done")
        drained = [sem(f"drained{i}") for i in range(2)]
        bank_full = sem("bank_full")
        consumed = [sem(f"consumed{i}") for i in range(NBANK)]
        x_full = [sem(f"x_full{i}") for i in range(4)]
        pre_full, mask_full, const_full = sem("pre_full"), sem("mask_full"), sem("const_full")
        cols_full, cols_ready = sem("cols_full"), sem("cols_ready")
        rot_full, ssdc_full = sem("rot_full"), sem("ssdc_full")
        decay_full, wpost_full, dtw_full = sem("decay_full"), sem("wpost_full"), sem("dtw_full")
        ut_hi_ready, yt_hi_ready, ht_hi_ready = sem("ut_hi_ready"), sem("yt_hi_ready"), sem("ht_hi_ready")
        h_dve_ready, h_pool_ready, squares_done = sem("h_dve_ready"), sem("h_pool_ready"), sem("squares_done")
        var_ready, std_ready, rstd_ready = sem("var_ready"), sem("std_ready"), sem("rstd_ready")
        dve_step, pool_step = sem("dve_step"), sem("pool_step")
        v_hi_ready, sd_hi_ready, sd_lo_ready = sem("v_hi_ready"), sem("sd_hi_ready"), sem("sd_lo_ready")
        rot_done, head_var_ready, head_std_ready = sem("rot_done"), sem("head_var_ready"), sem("head_std_ready")
        head_rstd_ready, y_scaled = sem("head_rstd_ready"), sem("y_scaled")
        rms_cols_ready, ht_lo_ready = sem("rms_cols_ready"), sem("ht_lo_ready")
        conv_done = sem("conv_done")
        squared, acc_zero, mw_ready, mw_scaled = sem("squared"), sem("acc_zero"), sem("mw_ready"), sem("mw_scaled")
        dtw_hi_ready, dtw_lo_ready = sem("dtw_hi_ready"), sem("dtw_lo_ready")
        dt_abs, dt_exp, a_exp, da_ready = sem("dt_abs"), sem("dt_exp"), sem("a_exp"), sem("da_ready")
        woff_ready, conv_silu, bcg_ready = sem("woff_ready"), sem("conv_silu"), sem("bcg_ready")
        da_hi_ready, da_lo_ready = sem("da_hi_ready"), sem("da_lo_ready")
        da_masked, m_done, x_ready, gated = sem("da_masked"), sem("m_done"), sem("x_ready"), sem("gated")
        group_var_ready = sem("group_var_ready")
        group_std_ready, group_rstd_ready = sem("group_std_ready"), sem("group_rstd_ready")
        group_scaled, out_done = sem("group_scaled"), sem("out_done")

        def residual_half(engine, k, j, t):
            ready, n = residual_source(k, j // 2, t, drained, mw_ready)
            engine.wait_ge(ready, n)
            c = slice(SEQ * j, SEQ * (j + 1))
            if engine is nc.gpsimd:
                if k == 7:
                    engine.wait_ge(mw_scaled, j // 2)
                else:
                    n = pool_steps.next()
                    engine.tensor_tensor(mw[:, t, c], mw[:, t, c], rstd[:, k, t:t + 1].to_broadcast([P, SEQ]), ALU.mult
                                         ).then_inc(pool_step, 1)
                    engine.wait_ge(pool_step, n)
                engine.tensor_tensor(h[:, t, c], h[:, t, c], mw[:, t, c], ALU.add).then_inc(h_pool_ready, 1)
            else:
                engine.scalar_tensor_tensor(out=h[:, t, c], in0=mw[:, t, c], scalar=rstd[:, k, t:t + 1], in1=h[:, t, c],
                                            op0=ALU.mult, op1=ALU.add).then_inc(h_dve_ready, 1)

        def wait_h(engine, k, j):
            n_dve, n_pool = residual_counts(k, j)
            engine.wait_ge(h_dve_ready, n_dve)
            if n_pool > 0:
                engine.wait_ge(h_pool_ready, n_pool)

        w_in_v = ret_w_in[0].rearrange("(k p) n -> p k n", p=P)
        w_ro_v = ret_w_out[0].rearrange("(k p) n -> p k n", p=P)
        w_si_v = ssd_w_in[0].rearrange("(k p) n -> p k n", p=P)
        w_so_v = ssd_w_out[0].rearrange("(k p) n -> p k n", p=P)
        w_up_v = [mlp_w_up[i].rearrange("(k p) n -> p k n", p=P) for i in range(2)]
        w_dn_v = [mlp_w_down[i].rearrange("(k p) n -> p k n", p=P) for i in range(2)]

        pool_steps = Steps()
        block = ctx.enter_context(nc.Block())

        @block.sync
        def _(sp):
            def load_unit(u, w, kt0, col, before={}):
                for c in range(CH):
                    if c in before:
                        before[c]()
                    free = u * CH + (c - RAW + 1)
                    if not isinstance(free, int) or free > 0:
                        sp.wait_ge(lo_ready, free)
                    sp.dma_start(w_raw[:, c % RAW, :, :],
                                 w[:, bass.ds(kt0 + CK * c, CK), bass.ds(col, NB)]
                                 ).then_inc(raw_full[c % RAW], 16)

            def load_x(i):
                sp.dma_start(h[:, :, NB * i:NB * (i + 1)],
                             x[0].rearrange("(t p) d -> p t d", p=P)[:, :, NB * i:NB * (i + 1)]
                             ).then_inc(x_full[i], 16)

            def load_norm_rows():
                for i, src in enumerate((norm_ffn_pre, ret_gn_w, ssd_norm_w)):
                    sp.dma_start(rows[32 * (i + 1):32 * (i + 2), 0, :], src.rearrange("l (k c) -> (l k) c", c=P)
                                 ).then_inc(const_full, 16)

            def load_conv_rows():
                taps = ssd_conv_w[0].rearrange("a (k c) -> (a k) c", c=P)
                for i in range(2):
                    sp.dma_start(rows[0:2 * CONV_KT, 1 + i, :], taps[2 * CONV_KT * i:2 * CONV_KT * (i + 1), :]
                                 ).then_inc(const_full, 16)
                sp.dma_start(rows[0:CONV_KT, 3, :], ssd_conv_b.rearrange("l (k c) -> (l k) c", c=P)
                             ).then_inc(const_full, 16)

            def load_tables():
                sp.dma_start(cos_t, rot_cos[:, :]).then_inc(rot_full, 16)
                sp.dma_start(sin_t, rot_sin[:, :]).then_inc(rot_full, 16)

            def load_ssd_rows():
                for dst, src in ((d_bc, ssd_d), (a_bc, ssd_a_log), (dtb_bc, ssd_dt_bias)):
                    sp.dma_start(dst, src.to_broadcast([P, SHEADS])).then_inc(ssdc_full, 16)

            def first_loads():
                loads = {i: lambda i=i: load_x(i) for i in range(4)}
                loads.update({4: load_norm_rows, 5: load_conv_rows, 6: load_tables, 7: load_ssd_rows})
                return loads

            def load_pair(p):
                u = p * 6 + U_RET
                load_unit(u, w_in_v, 0, p * 512, before=first_loads() if isinstance(p, int) else {})
                if not isinstance(p, int):
                    f = Fill(F_RET + 3, (p - 1) * 3)
                    sp.wait_ge(consumed[f.bank], f.turn + 1)
                sp.dma_start(decay, ret_decay[:, bass.ds(p * 768, 768)].rearrange("p (a b) -> p a b", a=2)
                             ).then_inc(decay_full, 16)
                load_unit(u + 1, w_in_v, 0, p * 512 + 2048)
                for i in range(2):
                    load_unit(u + (2 + i), w_in_v, 0, p * 1024 + (4096 + 512 * i))
                for i in range(2):
                    load_unit(u + (4 + i), w_in_v, 0, p * 1024 + (8192 + 512 * i))

            def load_out(u0, w):
                for b in range(4):
                    for half in range(2):
                        load_unit(u0 + 2 * b + half, w, KT * half, NB * b)

            def load_mlp(u0, layer):
                with sp.Fori(0, FF_GROUPS) as g:
                    for j in range(4):
                        load_unit(g * 8 + (u0 + j), w_up_v[layer], 0, g * 2048 + NB * j)
                    for j in range(4):
                        load_unit(g * 8 + (u0 + 4 + j), w_dn_v[layer], g * KT, NB * j)

            sp.dma_start(mask[:, :, :], masks.rearrange("p (a b) -> p a b", a=3)).then_inc(mask_full, 16)
            load_pair(0)
            with sp.Fori(1, PAIRS) as p:
                load_pair(p)
            load_out(U_RET_OUT, w_ro_v)
            load_mlp(U_MLP0, 0)
            for k, col in enumerate((8192, 8704, 9216, 9728)):
                load_unit(U_SSD + k, w_si_v, 0, col)
            with sp.Fori(1, GROUPS + 1) as g1:
                load_unit(g1 * 2 + (U_SSD + 2), w_si_v, 0, g1 * NB + (INNER - NB))
                load_unit(g1 * 2 + (U_SSD + 3), w_si_v, 0, g1 * NB + (-NB))
            load_out(U_SSD_OUT, w_so_v)
            load_mlp(U_MLP1, 1)
            for i in range(4):
                wait_h(sp, 7, 2 * i + 1)
                sp.dma_start(out[0].rearrange("(t p) d -> p t d", p=P)[:, :, NB * i:NB * (i + 1)],
                             h[:, :, NB * i:NB * (i + 1)]).then_inc(out_done, 16)
            sp.wait_ge(out_done, 64)

        @block.tensor
        def _(pe):
            def chunk(u, c, hi, lo, kt0, par, start, stop):
                pe.wait_ge(lo_ready, u * CH + (c + 1))
                s = c % SPLIT
                for kk in range(CK):
                    k = kt0 + CK * c + kk
                    first = start and c == 0 and kk == 0
                    last = stop and c == CH - 1 and kk == CK - 1
                    for t in range(T):
                        o = gemm[:, par, t, :]
                        a_hi, a_lo = hi[:, k, P * t:P * (t + 1)], lo[:, k, P * t:P * (t + 1)]
                        pe.matmul(o, a_hi, w_hi[:, s, kk, :], start=first, stop=False)
                        pe.matmul(o, a_hi, w_lo[:, s, kk, :], start=False, stop=False)
                        mm_ = pe.matmul(o, a_lo, w_hi[:, s, kk, :], start=False, stop=last)
                mm_.then_inc(chunk_done, 1)

            def chunk_t(u, c, par):
                pe.wait_ge(lo_ready, u * CH + (c + 1))
                s = c % SPLIT
                for kk in range(CK):
                    k = CK * c + kk
                    for r in range(4):
                        o = gemm[:, par, r // 2, SEQ * (r % 2):SEQ * (r % 2 + 1)]
                        b_hi, b_lo = w_hi[:, s, kk, P * r:P * (r + 1)], w_lo[:, s, kk, P * r:P * (r + 1)]
                        pe.matmul(o, b_hi, ut_hi[:, k, :], start=(k == 0 and r % 2 == 0), stop=False)
                        pe.matmul(o, b_hi, ut_lo[:, k, :], start=False, stop=False)
                        mm_ = pe.matmul(o, b_lo, ut_hi[:, k, :], start=False, stop=(k == KT - 1 and r % 2 == 1))
                mm_.then_inc(chunk_done, 1)

            def unit(u, par, turn, hi=ut_hi, lo=ut_lo, kt0=0, start=True, stop=True, turned=False, before={}, after_={}):
                if start and (not isinstance(turn, int) or turn > 0):
                    pe.wait_ge(drained[par], turn * 4)
                for c in range(CH):
                    for f in before.get(c, ()):
                        f()
                    if turned:
                        chunk_t(u, c, par)
                    else:
                        chunk(u, c, hi, lo, kt0, par, start, stop)
                    for f in after_.get(c, ()):
                        f()

            def unit_t(u, par, turn, before={}, after_={}):
                unit(u, par, turn, turned=True, before=before, after_=after_)

            def free(f):
                if not isinstance(f.turn, int) or f.turn > 0:
                    pe.wait_ge(consumed[f.bank], f.turn)

            def turn_to_channels(f, src):
                free(f)
                for kk in range(2):
                    for t in range(T):
                        at = SEQ * kk + P * t
                        tr = pe.transpose(banks[:, f.bank, at:at + P], src(t, kk), ident)
                tr.then_inc(bank_full, 1)

            def norm_fill(phase, j):
                if phase == 0:
                    pe.wait_ge(x_full[j // 2], 16)
                else:
                    wait_h(pe, 2 * phase - 1, j)
                turn_to_channels(Fill(F_PHASE[phase] + j),
                                 lambda t, kk: h[:, t, P * (2 * j + kk):P * (2 * j + kk + 1)])

            def ut_ready(phase, j):
                f = Fill(F_PHASE[phase] + j)
                pe.wait_ge(consumed[f.bank], f.turn + 1)

            def keep_warm(phase):
                f = Fill(F_PHASE[phase])
                free(f)
                for i in range(14):
                    pe.matmul(banks[:, f.bank, :], ut_hi[:, 0, 0:P], w_hi[:, 3, 1, :], start=True, stop=True)

            def columns(loaded, n_loaded, parts):
                pe.wait_ge(loaded, n_loaded)
                at = 0
                for i, n in enumerate(parts):
                    tr = pe.transpose(gemm[:, 1, 0, at:at + n], rows[0:n, i, :], ident[0:n, 0:n])
                    at += n
                tr.then_inc(cols_full, 1)

            def first_unit(phase, u, turn, more={}):
                if phase > 0:
                    keep_warm(phase)
                for j in range(2):
                    norm_fill(phase, j)
                if phase == 0:
                    columns(pre_full, 16, (COL_FFN,))
                aft = {c: [lambda c=c: norm_fill(phase, c + 3)] for c in range(5)}
                aft[0].insert(0, lambda: norm_fill(phase, 2))
                if phase == 0:
                    aft[5] = [lambda: pe.wait_ge(cols_ready, 1),
                              lambda: columns(const_full, 16 * CONST_LOADS, (128, 96, 96, 48))]
                for c, fs in more.items():
                    aft[c] = aft.get(c, []) + list(fs)
                unit_t(u, 0, turn, before={c: [lambda c=c: ut_ready(phase, c)] for c in range(CH)}, after_=aft)

            def rms_fill(f, n, src):
                pe.wait_ge(rms_cols_ready, n)
                free(f)
                for t in range(T):
                    tr = pe.transpose(banks[:, f.bank, P * t:P * (t + 1)], src[:, t, :], ident)
                tr.then_inc(bank_full, 1)

            def scores(p, f, hh):
                pe.wait_ge(rot_done, p * 8 + (4 + 2 * (hh + 1)))
                for mt in range(T):
                    g = f + (2 * hh + mt)
                    free(g)
                    w = SEQ - P * mt
                    for k in range(2):
                        s_ = pe.matmul(banks[:, g.bank, 0:w], kt_[:, hh, k, P * mt:P * (mt + 1)],
                                       qt[:, hh, k, P * mt:SEQ], start=(k == 0), stop=(k == 1))
                    s_.then_inc(bank_full, 1)

            def values(p, f, hh):
                pe.wait_ge(sd_lo_ready, p * 2 + (hh + 1))
                pe.wait_ge(drained[hh], (p * 3 + (B_RET + 1)) * 4 + 4)
                for t in range(T):
                    g = f + (2 * hh + t)
                    free(g)
                    o = banks[:, g.bank, :]
                    for mt in range(t + 1):
                        at = P * t if mt == 0 else 256
                        a_hi, a_lo = sd_hi[:, at:at + P], sd_lo[:, at:at + P]
                        pe.matmul(o, a_hi, v_hi[:, hh, mt, :], start=(mt == 0), stop=False)
                        pe.matmul(o, a_hi, v_lo[:, hh, mt, :], start=False, stop=False)
                        v_ = pe.matmul(o, a_lo, v_hi[:, hh, mt, :], start=False, stop=(mt == t))
                    v_.then_inc(bank_full, 1)

            def heads_out(f, p, hh):
                pe.wait_ge(y_scaled, p * 4 + 2 * (hh + 1))
                for j in range(2):
                    turn_to_channels(f + (2 * hh + j),
                                     lambda t, kk: sg[:, hh, t, P * (2 * j + kk):P * (2 * j + kk + 1)])

            def pair_fill(p, idx):
                return Fill(F_RET + idx, p * 3)

            def pair_rest(p):
                u, b = p * 6 + U_RET, p * 3 + B_RET
                unit_t(u + 1, 1, b, after_={1: [lambda: rms_fill(Fill(F_ROW0), 1, rms_cols0)]} if isinstance(p, int) else {})
                unit(u + 2, 0, b + 1)
                unit(u + 3, 1, b + 1, after_={3: [lambda: scores(p, pair_fill(p, 0), 0)],
                                              5: [lambda: scores(p, pair_fill(p, 0), 1)]})
                unit(u + 4, 0, b + 2, after_={1: [lambda: values(p, pair_fill(p, 4), 0)]})
                unit(u + 5, 1, b + 2, after_={1: [lambda: values(p, pair_fill(p, 4), 1)]})

            def pair_tail(p):
                return {5: [lambda: heads_out(pair_fill(p, 8), p, 0)], 7: [lambda: heads_out(pair_fill(p, 8), p, 1)]}

            pe.wait_ge(mask_full, 16)
            first_unit(0, U_RET, B_RET)
            pe.wait_ge(cols_ready, 2)
            pair_rest(0)
            with pe.Fori(1, PAIRS) as p:
                unit_t(p * 6 + U_RET, 0, p * 3 + B_RET, after_=pair_tail(p - 1))
                pair_rest(p)

            def yt_wait(f):
                return [lambda: pe.wait_ge(consumed[f.bank], f.turn + 1)]

            def out_projection(u0, b0, tail0, tail1, waits0, waits1):
                for b in range(4):
                    unit(u0 + 2 * b, b % 2, b0 + b // 2, yt_hi, yt_lo, 0, True, False,
                         after_=tail0 if b == 0 else {}, before=waits0 if b == 0 else {})
                    unit(u0 + 2 * b + 1, b % 2, b0 + b // 2, yt_hi, yt_lo, KT, False, True,
                         after_=tail1 if b == 0 else {}, before=waits1 if b == 0 else {})

            out_projection(
                U_RET_OUT, B_RET_OUT, pair_tail(3), {},
                {0: [w for j in range(4) for w in yt_wait(pair_fill(2, 8 + j))]},
                {4 + j: yt_wait(pair_fill(3, 8 + j)) for j in range(4)})

            def mlp(phase, u0, b0):
                def hidden_wait(g, c):
                    pe.wait_ge(ht_lo_ready, (g + (phase // 2) * FF_GROUPS) * 8 + (c + 1))

                def rest(g):
                    u, b = g * 8 + u0, g * 4 + b0
                    for j in range(1, 4):
                        unit_t(u + j, j % 2, b + j // 2)
                    unit(u + 4, 0, b + 2, yt_hi, yt_lo,
                         before={c: [lambda c=c: hidden_wait(g, c)] for c in range(CH)})
                    for j in range(1, 4):
                        unit(u + 4 + j, j % 2, b + 2 + j // 2, yt_hi, yt_lo)

                first_unit(phase, u0, b0)
                with pe.Fori(0, FF_GROUPS - 1) as g:
                    rest(g)
                    unit_t(g * 8 + (u0 + 8), 0, g * 4 + (b0 + 4))
                rest(FF_GROUPS - 1)

            mlp(1, U_MLP0, B_MLP0)

            def dt_product():
                pe.wait_ge(dtw_lo_ready, 1)
                ut_ready(2, CH - 1)
                f = Fill(F_DT)
                free(f)
                wh = yt_hi[:, 28:32, :].rearrange("p a (b n) -> p (a b) n", n=SHEADS)
                wl = yt_lo[:, 28:32, :].rearrange("p a (b n) -> p (a b) n", n=SHEADS)
                o = banks[0:SHEADS, f.bank, 0:SEQ]
                for k in range(KT):
                    pe.matmul(o, wh[:, k, :], ut_hi[:, k, :], start=(k == 0), stop=False)
                    pe.matmul(o, wh[:, k, :], ut_lo[:, k, :], start=False, stop=False)
                    m_ = pe.matmul(o, wl[:, k, :], ut_hi[:, k, :], start=False, stop=(k == KT - 1))
                m_.then_inc(bank_full, 1)

            def dt_back():
                f = Fill(F_DT)
                pe.wait_ge(consumed[f.bank], f.turn + 1)
                f = Fill(F_DT_BACK)
                free(f)
                for t in range(T):
                    tr = pe.transpose(banks[:, f.bank, SHEADS * t:SHEADS * (t + 1)],
                                      dt_t[0:SHEADS, P * t:P * (t + 1)], ident[0:SHEADS, 0:SHEADS])
                tr.then_inc(bank_full, 1)

            def decay_sums():
                pe.wait_ge(da_ready, 1)
                f = Fill(F_DECAY)
                free(f)
                pe.matmul(banks[:, f.bank, 0:SHEADS], after, da[:, 0, :], start=True, stop=True)
                pe.matmul(banks[:, f.bank, SHEADS:2 * SHEADS], upto, da[:, 1, :], start=True, stop=True
                          ).then_inc(bank_full, 1)

            def group_cb(g, f):
                pe.wait_ge(bcg_ready, g + 1)
                free(f)
                pe.matmul(banks[:, f.bank, 0:SEQ], bcg[:, 0, 0:P], bcg[:, 1, :], start=True, stop=True)
                pe.matmul(banks[:, f.bank, SEQ:SEQ + P], bcg[:, 0, P:SEQ], bcg[:, 1, P:SEQ], start=True, stop=True
                          ).then_inc(bank_full, 1)

            def group_seg(g, f, i):
                pe.wait_ge(da_masked, g * 4 + (i + 1))
                free(f + i)
                pe.matmul(banks[:, (f + i).bank, :], after_r, masked_hi[:, i, :], start=True, stop=False)
                pe.matmul(banks[:, (f + i).bank, :], after_r, masked_lo[:, i, :], start=False, stop=True
                          ).then_inc(bank_full, 1)

            def back_fills(g, f):
                pe.wait_ge(conv_silu, g * 2 + 10)
                for t in range(T):
                    free(f + t)
                    for k in range(4):
                        b_ = pe.transpose(banks[:, (f + t).bank, P * k:P * (k + 1)],
                                          conv[:, k, P * t:P * (t + 1)], ident)
                    b_.then_inc(bank_full, 1)

            def group_y(g, f):
                pe.wait_ge(x_ready, g * 5 + 3)
                pe.wait_ge(m_done, g * 4 + 4)
                for t in range(T):
                    free(f + t)
                    for hh in range(HPG):
                        y_ = pe.matmul(banks[:, (f + t).bank, HD * hh:HD * (hh + 1)],
                                       mm[:, 2 * t + hh // 4, P * (hh % 4):P * (hh % 4 + 1)],
                                       xdt[:, t, HD * hh:HD * (hh + 1)], start=True, stop=True)
                    y_.then_inc(bank_full, 1)
                free(f + 2)
                pe.matmul(banks[:, (f + 2).bank, :], cb[:, 1, :], xoff, start=True, stop=True
                          ).then_inc(bank_full, 1)

            def group_out(g, f):
                pe.wait_ge(group_scaled, g * 2 + 2)
                for i in range(2):
                    turn_to_channels(f + i, lambda t, kk: yy[:, t, P * (2 * i + kk):P * (2 * i + kk + 1)])

            first_unit(2, U_SSD, B_SSD, {6: [dt_product]})
            unit_t(U_SSD + 1, 1, B_SSD, after_={0: [dt_back], 1: [lambda: rms_fill(Fill(F_ROW2), 2, rms_cols2)]})
            unit_t(U_SSD + 2, 0, B_SSD + 1, after_={2: [decay_sums]})
            unit_t(U_SSD + 3, 1, B_SSD + 1)
            unit_t(U_SSD + 4, 0, B_SSD + 2, after_={
                4: [lambda: group_cb(0, Fill(F_G0)), lambda: group_seg(0, Fill(F_G0 + 1), 0)],
                5: [lambda: group_seg(0, Fill(F_G0 + 1), 1)],
                6: [lambda: group_seg(0, Fill(F_G0 + 1), 2)],
                7: [lambda: group_seg(0, Fill(F_G0 + 1), 3)]})
            unit(U_SSD + 5, 1, B_SSD + 2, after_={6: [lambda: back_fills(0, Fill(F_G0 + 5))]})
            with pe.Fori(1, GROUPS) as g:
                def gf(idx):
                    return Fill(F_G1 + idx, (g - 1) * 3)
                unit_t(g * 2 + (U_SSD + 4), 0, g + (B_SSD + 2), after_={
                    2: [lambda: group_y(g - 1, gf(0))],
                    4: [lambda: group_cb(g, gf(3)), lambda: group_seg(g, gf(4), 0)],
                    5: [lambda: group_seg(g, gf(4), 1)],
                    6: [lambda: group_seg(g, gf(4), 2)],
                    7: [lambda: group_seg(g, gf(4), 3)]})
                unit(g * 2 + (U_SSD + 5), 1, g + (B_SSD + 2), after_={
                    4: [lambda: group_out(g - 1, gf(8))],
                    6: [lambda: back_fills(g, gf(10))]})
            out_projection(
                U_SSD_OUT, B_SSD_OUT, {2: [lambda: group_y(7, Fill(F_GTAIL))]},
                {4: [lambda: group_out(7, Fill(F_GTAIL + 3))]},
                {0: [w for j in range(2) for w in yt_wait(Fill(F_G1 + 72 + 8 + j))]},
                {6 + j: yt_wait(Fill(F_GTAIL + 3 + j)) for j in range(2)})
            mlp(3, U_MLP1, B_MLP1)

        @block.scalar
        def _(act):
            def slot(u, c):
                u, c = u + (c + LEAD) // CH, (c + LEAD) % CH
                if isinstance(u, int) and u >= U_END:
                    return
                act.wait_ge(raw_full[c % RAW], (u * 2 + (c // RAW + 1)) * 16)
                freed = u * CH + (c - SPLIT + 1)
                if not isinstance(freed, int) or freed > 0:
                    act.wait_ge(chunk_done, freed)
                act.activation(w_hi[:, c % SPLIT, :, :], w_raw[:, c % RAW, :, :], ACT.Copy
                               ).then_inc(hi_ready, 1)

            def unit(u, at={}):
                for c in range(CH):
                    slot(u, c)
                    for f in at.get(c, ()):
                        f()

            def block_done(u):
                act.wait_ge(chunk_done, u * CH + CH)

            def split_fill(f, dst, k, col, ready):
                act.wait_ge(bank_full, f.full)
                for kk in range(2):
                    s_ = act.activation(dst[:, k + kk, :], banks[:, f.bank, SEQ * kk:SEQ * (kk + 1)], ACT.Copy,
                                        scale=cols[:, bass.ds(col + kk, 1)])
                s_.then_inc(ready, 1)

            def square(src, t, total, n):
                if not isinstance(n, int) or n >= T:
                    act.wait_ge(squares_done, n - (T - 1))
                act.activation(junk[:, t, :], src, ACT.Square, accum_out=total).then_inc(squares_done, 1)

            def norm_hi(phase, j):
                split_fill(Fill(F_PHASE[phase] + j), ut_hi, 2 * j, COL_PRE[phase] + 2 * j, ut_hi_ready)

            def squares(phase, b):
                if phase == 0:
                    act.wait_ge(x_full[b], 16)
                else:
                    wait_h(act, 2 * phase - 1, 2 * b + 1)
                for t in range(T):
                    square(h[:, t, NB * b:NB * (b + 1)], t, ssq[:, 2 * phase, t, b:b + 1],
                           squares_before(2 * phase) + 2 * b + t)

            def root(k):
                act.wait_ge(var_ready, k + 1)
                act.activation(std[:, k, :], var[:, k, :], ACT.Sqrt).then_inc(std_ready, 1)

            def first_unit(phase, u, more={}):
                if phase > 0:
                    root(2 * phase - 1)
                    norm_hi(phase, 0)
                    norm_hi(phase, 1)
                at = {c: [lambda c=c: norm_hi(phase, c + 2)] for c in range(6)}
                for b, c in enumerate((1, 3, 4, 5)):
                    at.setdefault(c, []).append(lambda b=b: squares(phase, b))
                at.setdefault(7, []).append(lambda: root(2 * phase))
                for c, fs in more.items():
                    at[c] = list(fs) + at.get(c, [])
                unit(u, at)

            act.dma_start(rows[0:32, 0, :], norm_mix_pre.rearrange("l (k c) -> (l k) c", c=P)).then_inc(pre_full, 16)

            def load_wpost(src, f_or_u):
                act.wait_ge(chunk_done, f_or_u * CH)
                act.dma_start(wpost, src.to_broadcast([P, D])).then_inc(wpost_full, 16)

            slot(-1, CH - 3)
            act.wait_ge(cols_ready, 1)
            norm_hi(0, 0)
            slot(-1, CH - 2)
            norm_hi(0, 1)
            slot(-1, CH - 1)

            def pair_fill(p, idx):
                return Fill(F_RET + idx, p * 3)

            def evacuate_block(u, par, dst, func, k):
                block_done(u)
                act.wait_ge(rstd_ready, k + 1)
                for t in range(T):
                    act.activation(dst[:, t, :], gemm[:, par, t, :], func, scale=rstd[:, k, t:t + 1]
                                   ).then_inc(drained[par], 2)

            def values_hi(p, hh):
                block_done(p * 6 + (U_RET + 2 + hh))
                act.wait_ge(rstd_ready, 1)
                for t in range(T):
                    act.activation(v_hi[:, hh, t, :], gemm[:, hh, t, :], ACT.Copy, scale=rstd[:, 0, t:t + 1]
                                   ).then_inc(v_hi_ready, 1)

            def scores_hi(p, hh):
                for mt in range(T):
                    f = pair_fill(p, 2 * hh + mt)
                    act.wait_ge(consumed[f.bank], f.turn + 1)
                if hh == 1 or not isinstance(p, int):
                    act.wait_ge(bank_full, pair_fill(p, 5 if hh == 1 else -5).full)
                act.activation(sd_hi, sd[:, hh, :], ACT.Copy).then_inc(sd_hi_ready, 1)

            def head_root(p):
                act.wait_ge(head_var_ready, p + 1)
                act.activation(head_std[:, :], head_var[:, :], ACT.Sqrt).then_inc(head_std_ready, 1)

            def heads_hi(p, hh):
                for j in (2 * hh, 2 * hh + 1):
                    split_fill(pair_fill(p, 8 + j), yt_hi, p * 8 + 2 * j, p * 8 + (COL_GN + 2 * j), yt_hi_ready)

            def pair_rest(p):
                u = p * 6 + U_RET
                unit(u + 1)
                unit(u + 2)
                unit(u + 3, {0: [lambda: values_hi(p, 0)], 5: [lambda: scores_hi(p, 0)]})
                unit(u + 4, {0: [lambda: values_hi(p, 1)], 3: [lambda: scores_hi(p, 1)]})
                unit(u + 5, {0: [lambda: evacuate_block(u + 4, 0, sg[:, 0], ACT.Silu, 0)]})

            def pair_tail(p):
                return {0: [lambda: evacuate_block(p * 6 + (U_RET + 5), 1, sg[:, 1], ACT.Silu, 0)],
                        2: [lambda: head_root(p)], 6: [lambda: heads_hi(p, 0)]}

            first_unit(0, U_RET)
            pair_rest(0)
            with act.Fori(1, PAIRS) as p:
                unit(p * 6 + U_RET, pair_tail(p - 1))
                heads_hi(p - 1, 1)
                pair_rest(p)

            def square_block(u, par, k, b):
                block_done(u)
                for t in range(T):
                    square(gemm[:, par, t, :], t, ssq[:, k, t, b:b + 1], squares_before(k) + 2 * b + t)

            def out_projection(u0, k, post, tail0, tail1):
                for b in range(4):
                    at = dict(tail0) if b == 0 else {0: [lambda b=b: square_block(u0 + 2 * b - 1, (b - 1) % 2, k, b - 1)]}
                    unit(u0 + 2 * b, at)
                    at = dict(tail1) if b == 0 else {}
                    if b == 0:
                        at[6] = [lambda: load_wpost(post, u0 + 1)]
                    unit(u0 + 2 * b + 1, at)
                square_block(u0 + 7, 1, k, 3)

            out_projection(U_RET_OUT, 1, norm_mix_post[0:1, :], pair_tail(3), {0: [lambda: heads_hi(3, 1)]})

            def mlp(phase, u0, post):
                def hidden(g, j):
                    block_done(g * 8 + (u0 + j))
                    for i in range(2):
                        act.activation(zt[:, j % 2, i, :], gemm[:, j % 2, i, :], ACT.Relu).then_inc(drained[j % 2], 2)

                def hidden_hi(g, j):
                    for i in range(2):
                        act.wait_ge(squared, (g + (phase // 2) * FF_GROUPS) * 8 + (2 * j + i + 1))
                        act.activation(yt_hi[:, 4 * j + 2 * i:4 * j + 2 * i + 2, :].rearrange("p a b -> p (a b)"),
                                       zt[:, j % 2, i, :], ACT.Copy).then_inc(ht_hi_ready, 1)

                def rest(g, last):
                    u = g * 8 + u0
                    for j in range(1, 5):
                        unit(u + j, {0: [lambda j=j: hidden(g, j - 1)], 2: [lambda j=j: hidden_hi(g, j - 1)]})
                    for j in range(1, 4):
                        unit(u + 4 + j, {2: [lambda j=j: square_acc(j - 1)]} if last else {})

                def square_acc(d):
                    for t in range(T):
                        act.wait_ge(drained[d % 2], (b_last + d // 2) * 4 + 2 * (t + 1))
                        square(acc[:, t, NB * d:NB * (d + 1)], t, ssq[:, 2 * phase + 1, t, d:d + 1],
                               squares_before(2 * phase + 1) + 2 * d + t)

                b0 = B_MLP0 if phase == 1 else B_MLP1
                b_last = b0 + 4 * (FF_GROUPS - 1) + 2
                first_unit(phase, u0)
                with act.Fori(0, FF_GROUPS - 1) as g:
                    rest(g, False)
                    unit(g * 8 + (u0 + 8))
                load_wpost(post, u0 + 8)
                if phase == 1:
                    act.dma_start(dt_raw, w_si_v[:, :, 10240:10304]).then_inc(dtw_full, 16)
                rest(FF_GROUPS - 1, True)
                square_acc(3)

            mlp(1, U_MLP0, norm_ffn_post[0:1, :])

            def dt_hi():
                act.wait_ge(dtw_full, 16)
                act.activation(yt_hi[:, 28:32, :].rearrange("p a b -> p (a b)"),
                               dt_raw.rearrange("p a b -> p (a b)"), ACT.Copy).then_inc(dtw_hi_ready, 1)

            def split_da():
                act.activation(after_r, after, ACT.Copy)
                act.wait_ge(da_ready, 1)
                act.activation(da_hi, da, ACT.Copy).then_inc(da_hi_ready, 1)

            def exp_abs():
                act.wait_ge(dt_abs, 1)
                act.activation(de, de, ACT.Exp, scale=-1.0).then_inc(dt_exp, 1)

            def exp_a():
                act.wait_ge(ssdc_full, 48)
                act.activation(a_bc, a_bc, ACT.Exp).then_inc(a_exp, 1)

            def exp_edges():
                f = Fill(F_DECAY)
                act.wait_ge(bank_full, f.full)
                act.activation(edge, banks[:, f.bank, 0:2 * SHEADS].rearrange("p (a b) -> p a b", a=2), ACT.Exp
                               ).then_inc(consumed[f.bank], 1)

            def dt_out():
                f = Fill(F_DT)
                act.wait_ge(bank_full, f.full)
                act.activation(dt_t[0:SHEADS, :], banks[0:SHEADS, f.bank, 0:SEQ], ACT.Copy).then_inc(consumed[f.bank], 1)

            def conv_out(n, i, dst):
                act.wait_ge(conv_done, n + (i + 1))
                act.activation(dst, conv[:, 2 * i:2 * i + 2, :], ACT.Silu).then_inc(conv_silu, 1)

            def exp_seg(f, i):
                g = f + i
                act.wait_ge(bank_full, g.full)
                act.activation(mm[:, i, :], banks[:, g.bank, :], ACT.Exp).then_inc(consumed[g.bank], 1)

            def group_square(g):
                act.wait_ge(gated, g * 2 + 2)
                for t in range(T):
                    square(yy[:, t, :], t, group_ssq[:, t:t + 1], g * 2 + (40 + t))

            def group_root(g):
                act.wait_ge(group_var_ready, g + 1)
                act.activation(group_std[:, :], group_var[:, :], ACT.Sqrt).then_inc(group_std_ready, 1)

            def group_hi(g, f):
                for i in range(2):
                    split_fill(f + i, yt_hi, g * 4 + 2 * i, g * 4 + (COL_SN + 2 * i), yt_hi_ready)

            def bc_silu(k, c0=3):
                dst = (bt, ct)[k // 2]
                return {c0 + 2 * i: [lambda i=i: conv_out(2 * k, i, dst[:, 4 * (k % 2) + 2 * i:4 * (k % 2) + 2 * i + 2, :])]
                        for i in range(2)}

            def merged(*ats):
                out_ = {}
                for at in ats:
                    for c, fs in at.items():
                        out_.setdefault(c, []).extend(fs)
                return out_

            first_unit(2, U_SSD, {0: [dt_hi]})
            dt_out()
            unit(U_SSD + 1, merged({2: [exp_a, exp_abs]}, bc_silu(0, 5)))
            unit(U_SSD + 2, merged({3: [split_da, exp_edges]}, bc_silu(1)))
            unit(U_SSD + 3, bc_silu(2))
            unit(U_SSD + 4, merged(bc_silu(3), {
                5: [lambda: exp_seg(Fill(F_G0 + 1), 0)], 6: [lambda: exp_seg(Fill(F_G0 + 1), 1)],
                7: [lambda: exp_seg(Fill(F_G0 + 1), 2)]}))

            def x_silu(g):
                return {3 + 2 * i: [lambda i=i: conv_out(g * 2 + 8, i, conv[:, 2 * i:2 * i + 2, :])] for i in range(2)}

            unit(U_SSD + 5, merged({0: [lambda: exp_seg(Fill(F_G0 + 1), 3)]}, x_silu(0)))
            with act.Fori(1, GROUPS) as g:
                def gf(idx):
                    return Fill(F_G1 + idx, (g - 1) * 3)
                u = g * 2 + (U_SSD + 4)
                unit(u, {0: [lambda: evacuate_block(u - 1, 1, sz, ACT.Silu, 4)],
                         5: [lambda: exp_seg(gf(4), 0)], 6: [lambda: exp_seg(gf(4), 1)],
                         7: [lambda: exp_seg(gf(4), 2), lambda: group_square(g - 1)]})
                unit(u + 1, merged({0: [lambda: exp_seg(gf(4), 3)]}, {
                    1: [lambda: group_root(g - 1)],
                    5: [lambda: group_hi(g - 1, gf(8))]}, x_silu(g)))
            out_projection(U_SSD_OUT, 5, norm_mix_post[1:2, :], {
                0: [lambda: evacuate_block(U_SSD + 19, 1, sz, ACT.Silu, 4)],
                7: [lambda: group_square(7)]},
                {1: [lambda: group_root(7)], 5: [lambda: group_hi(7, Fill(F_GTAIL + 3))]})
            mlp(3, U_MLP1, norm_ffn_post[1:2, :])
            root(7)
            act.wait_ge(rstd_ready, 8)
            for b in range(1, 4):
                act.wait_ge(*residual_source(7, b, 1, drained, mw_ready))
                act.activation(mw[:, 1, NB * b:NB * (b + 1)], mw[:, 1, NB * b:NB * (b + 1)], ACT.Copy,
                               scale=rstd[:, 7, 1:2]).then_inc(mw_scaled, 1)

        @block.vector
        def _(dve):
            steps = Steps()

            def slot(u, c):
                u, c = u + (c + LEAD) // CH, (c + LEAD) % CH
                if isinstance(u, int) and u >= U_END:
                    return
                dve.wait_ge(hi_ready, u * CH + (c + 1))
                dve.tensor_tensor(w_lo[:, c % SPLIT, :, :], w_raw[:, c % RAW, :, :],
                                  w_hi[:, c % SPLIT, :, :].bitcast(F32), ALU.subtract).then_inc(lo_ready, 1)

            def unit(u, at={}):
                for c in range(CH):
                    slot(u, c)
                    for f in at.get(c, ()):
                        f()

            def block_done(u):
                dve.wait_ge(chunk_done, u * CH + CH)

            def split_fill(f, hi, lo, k, col, ready, n):
                dve.wait_ge(ready, n)
                for kk in range(2):
                    s_ = dve.scalar_tensor_tensor(
                        out=lo[:, k + kk, :], in0=banks[:, f.bank, SEQ * kk:SEQ * (kk + 1)],
                        scalar=cols[:, bass.ds(col + kk, 1)], in1=hi[:, k + kk, :].bitcast(F32),
                        op0=ALU.mult, op1=ALU.subtract)
                s_.then_inc(consumed[f.bank], 1)

            def norm_lo(phase, j):
                split_fill(Fill(F_PHASE[phase] + j), ut_hi, ut_lo, 2 * j, COL_PRE[phase] + 2 * j,
                           ut_hi_ready, 8 * phase + j + 1)

            def mean_square(k):
                n = steps.next()
                dve.tensor_reduce(var[:, k, :], ssq[:, k, :, :], AX_X, ALU.add).then_inc(dve_step, 1)
                dve.wait_ge(dve_step, n)
                dve.tensor_scalar(var[:, k, :], var[:, k, :], 1.0 / D, RMS_EPS, ALU.mult, ALU.add
                                  ).then_inc(var_ready, 1)

            def inverse(k):
                dve.wait_ge(std_ready, k + 1)
                dve.reciprocal(rstd[:, k, :], std[:, k, :]).then_inc(rstd_ready, 1)

            def pre_norm(phase):
                dve.wait_ge(squares_done, squares_before(2 * phase) + 8)
                mean_square(2 * phase)
                inverse(2 * phase)
                if phase % 2 == 1:
                    dve.wait_ge(rstd_ready, 2 * phase + 1)
                    n = steps.next()
                    r = rstd[:, 2 * phase, :]
                    dve.tensor_tensor(inv_ms[:, phase // 2, :], r, r, ALU.mult).then_inc(dve_step, 1)
                    dve.wait_ge(dve_step, n)

            def residual(k, j):
                if j == 0:
                    dve.wait_ge(rstd_ready, k + 1)
                for t in range(2 if j < POOL_FROM else 1):
                    residual_half(dve, k, j, t)

            def post_norm(k):
                dve.wait_ge(squares_done, squares_before(k) + 8)
                mean_square(k)
                inverse(k)

            def first_unit(phase, u, more={}, late=()):
                at = {c: [lambda c=c: norm_lo(phase, c + 2)] for c in range(6)}
                if phase > 0:
                    k = 2 * phase - 1
                    post_norm(k)
                    residual(k, 0)
                    residual(k, 1)
                    norm_lo(phase, 0)
                    residual(k, 2)
                    residual(k, 3)
                    norm_lo(phase, 1)
                    at[0] += [lambda: residual(k, 4), lambda: residual(k, 5)] + list(late)
                    at[1] += [lambda: residual(k, 6), lambda: residual(k, 7)]
                else:
                    at[6] = [lambda: copy_columns(1, COL_FFN, NCOLS)]
                at.setdefault(7, []).append(lambda: pre_norm(phase))
                for c, fs in more.items():
                    at[c] = list(fs) + at.get(c, [])
                unit(u, at)

            def copy_columns(n, a, b):
                dve.wait_ge(cols_full, n + 1)
                dve.tensor_copy(cols[:, a:b], gemm[:, 1, 0, a:b]).then_inc(cols_ready, 1)
                dve.wait_ge(cols_ready, n + 1)

            copy_columns(0, 0, COL_FFN)
            slot(-1, CH - 3)
            norm_lo(0, 0)
            slot(-1, CH - 2)
            norm_lo(0, 1)
            slot(-1, CH - 1)

            def pair_fill(p, idx):
                return Fill(F_RET + idx, p * 3)

            def spread_rms(k, dst):
                dve.wait_ge(rstd_ready, k + 1)
                dve.tensor_copy(dst, rstd[:, k, :].unsqueeze(2).to_broadcast([P, T, P])).then_inc(rms_cols_ready, 1)

            def scale_tables():
                dve.wait_ge(rot_full, 32)
                f = Fill(F_ROW0)
                dve.wait_ge(bank_full, f.full)
                n = steps.next()
                dve.tensor_tensor(cos_t, cos_t, banks[:, f.bank, 0:SEQ], ALU.mult).then_inc(dve_step, 1)
                dve.tensor_tensor(sin_t, sin_t, banks[:, f.bank, 0:SEQ], ALU.mult).then_inc(consumed[f.bank], 1)
                dve.wait_ge(dve_step, n)
                dve.wait_ge(consumed[f.bank], f.turn + 1)

            def rotate(p, k):
                block_done(p * 6 + (U_RET + k))
                if not isinstance(p, int) or k > 0:
                    dve.wait_ge(rot_done, p * 8 + 4 * k)
                for hh in range(2):
                    for dst, table in ((rot_a, cos_t), (rot_b, sin_t)):
                        r_ = dve.tensor_tensor(dst[:, hh, :].rearrange("p (i n) -> p i n", i=2),
                                               gemm[:, k, hh, :].rearrange("p (i n) -> p i n", i=2),
                                               table.unsqueeze(1).to_broadcast([P, 2, SEQ]), ALU.mult)
                    r_.then_inc(drained[k], 2)

            def decay_scores(p, hh):
                dve.wait_ge(decay_full, p * 16 + 16)
                for mt in range(T):
                    f = pair_fill(p, 2 * hh + mt)
                    dve.wait_ge(bank_full, f.full)
                    a, w = 256 * mt, SEQ - P * mt
                    dve.tensor_tensor(sd[:, hh, a:a + w], banks[:, f.bank, 0:w], decay[:, hh, a:a + w], ALU.mult
                                      ).then_inc(consumed[f.bank], 1)

            def values_lo(p, hh):
                for t in range(T):
                    dve.wait_ge(v_hi_ready, p * 4 + (2 * hh + t + 1))
                    dve.scalar_tensor_tensor(out=v_lo[:, hh, t, :], in0=gemm[:, hh, t, :], scalar=rstd[:, 0, t:t + 1],
                                             in1=v_hi[:, hh, t, :].bitcast(F32), op0=ALU.mult, op1=ALU.subtract
                                             ).then_inc(drained[hh], 2)

            def head_stats(p, hh):
                for t in range(T):
                    f = pair_fill(p, 4 + 2 * hh + t)
                    i = 2 * hh + t
                    dve.wait_ge(bank_full, f.full)
                    n = steps.next()
                    dve.bn_stats(bn[:, i, :], banks[:, f.bank, :]).then_inc(dve_step, 1)
                    dve.wait_ge(dve_step, n)
                    dve.memset(waited[:, :], 0.0)
                    n = steps.next()
                    dve.bn_aggr(mv[:, i, :], bn[:, i, :]).then_inc(dve_step, 1)
                dve.wait_ge(dve_step, n)

            def head_gate(p, hh):
                dve.wait_ge(drained[hh], (p * 3 + (B_RET + 2)) * 4 + 4)
                for t in range(T):
                    f = pair_fill(p, 4 + 2 * hh + t)
                    i = 2 * hh + t
                    dve.scalar_tensor_tensor(out=sg[:, hh, t, :], in0=banks[:, f.bank, :], scalar=mv[:, i, 0:1],
                                             in1=sg[:, hh, t, :], op0=ALU.subtract, op1=ALU.mult
                                             ).then_inc(consumed[f.bank], 1)

            def head_variance(p):
                dve.tensor_scalar(head_var[:, :], mv[:, :, 1], GN_EPS, None, ALU.add).then_inc(head_var_ready, 1)

            def head_inverse(p):
                dve.wait_ge(head_std_ready, p + 1)
                dve.reciprocal(head_rstd[:, :], head_std[:, :]).then_inc(head_rstd_ready, 1)

            def heads_lo(p, hh):
                for j in (2 * hh, 2 * hh + 1):
                    split_fill(pair_fill(p, 8 + j), yt_hi, yt_lo, p * 8 + 2 * j, p * 8 + (COL_GN + 2 * j),
                               yt_hi_ready, p * 4 + (j + 1))

            def pair_rest(p):
                u = p * 6 + U_RET
                if isinstance(p, int):
                    unit(u + 1, {0: [lambda: spread_rms(0, rms_cols0)], 2: [scale_tables, lambda: rotate(p, 0)]})
                else:
                    unit(u + 1, {0: [lambda: rotate(p, 0)]})
                unit(u + 2, {0: [lambda: rotate(p, 1)]})
                unit(u + 3, {0: [lambda: values_lo(p, 0)], 4: [lambda: decay_scores(p, 0)],
                             6: [lambda: decay_scores(p, 1)]})
                unit(u + 4, {0: [lambda: values_lo(p, 1)]})
                unit(u + 5, {2: [lambda: head_stats(p, 0), lambda: head_gate(p, 0)], 4: [lambda: head_stats(p, 1)]})

            def pair_tail(p):
                return {0: [lambda: head_variance(p)], 1: [lambda: head_gate(p, 1)], 3: [lambda: head_inverse(p)],
                        6: [lambda: heads_lo(p, 0)]}

            first_unit(0, U_RET)
            pair_rest(0)
            with dve.Fori(1, PAIRS) as p:
                steps.loop(p - 1, 8)
                unit(p * 6 + U_RET, pair_tail(p - 1))
                heads_lo(p - 1, 1)
                pair_rest(p)
                steps.end(PAIRS - 1)

            def weigh_tile(par, b, n, t):
                dve.wait_ge(squares_done, squares_before(1 if n == 1 else 5) + 2 * b + t + 1)
                dve.tensor_tensor(mw[:, t, NB * b:NB * (b + 1)], gemm[:, par, t, :],
                                  wpost[:, NB * b:NB * (b + 1)], ALU.mult).then_inc(drained[par], 2)

            def weigh_block(u, par, b, n):
                block_done(u)
                dve.wait_ge(wpost_full, 16 * n)
                for t in range(T):
                    weigh_tile(par, b, n, t)

            def out_projection(u0, b0, n, tail0, tail1):
                for b in range(4):
                    at = dict(tail0) if b == 0 else {0: [lambda b=b: weigh_block(u0 + 2 * b - 1, (b - 1) % 2, b - 1, n)]}
                    unit(u0 + 2 * b, at)
                    unit(u0 + 2 * b + 1, tail1 if b == 0 else {})
                block_done(u0 + 7)
                weigh_tile(1, 3, n, 0)

            out_projection(U_RET_OUT, B_RET_OUT, 1, pair_tail(3), {0: [lambda: heads_lo(3, 1)]})

            def mlp(phase, u0, b0):
                def hidden_lo(g, j):
                    for i in range(2):
                        dve.wait_ge(ht_hi_ready, (g + (phase // 2) * FF_GROUPS) * 8 + (2 * j + i + 1))
                        k = 4 * j + 2 * i
                        dve.tensor_tensor(yt_lo[:, k:k + 2, :].rearrange("p a b -> p (a b)"), zt[:, j % 2, i, :],
                                          yt_hi[:, k:k + 2, :].rearrange("p a b -> p (a b)").bitcast(F32),
                                          ALU.subtract).then_inc(ht_lo_ready, 1)

                def add_block(u, d):
                    block_done(u)
                    dve.wait_ge(acc_zero, phase // 2 + 1)
                    for t in range(T):
                        a = acc[:, t, NB * d:NB * (d + 1)]
                        dve.scalar_tensor_tensor(out=a, in0=gemm[:, d % 2, t, :], scalar=inv_ms[:, phase // 2, t:t + 1],
                                                 in1=a, op0=ALU.mult, op1=ALU.add).then_inc(drained[d % 2], 2)

                def rest(g):
                    u = g * 8 + u0
                    for j in range(1, 5):
                        unit(u + j, {3: [lambda j=j: hidden_lo(g, j - 1)]})
                    for j in range(1, 4):
                        unit(u + 4 + j, {0: [lambda j=j: add_block(u + 3 + j, j - 1)]})

                first_unit(phase, u0, late=[lambda: weigh_tile(1, 3, phase, 1)])
                with dve.Fori(0, FF_GROUPS - 1) as g:
                    rest(g)
                    unit(g * 8 + (u0 + 8), {0: [lambda: add_block(g * 8 + (u0 + 7), 3)]})
                rest(FF_GROUPS - 1)
                add_block(u0 + 31, 3)

            mlp(1, U_MLP0, B_MLP0)

            def dt_lo():
                dve.wait_ge(dtw_hi_ready, 1)
                dve.tensor_tensor(yt_lo[:, 28:32, :].rearrange("p a b -> p (a b)"), dt_raw.rearrange("p a b -> p (a b)"),
                                  yt_hi[:, 28:32, :].rearrange("p a b -> p (a b)").bitcast(F32), ALU.subtract
                                  ).then_inc(dtw_lo_ready, 1)

            def chained(make):
                n = steps.next()
                make().then_inc(dve_step, 1)
                dve.wait_ge(dve_step, n)

            def dt_input():
                f = Fill(F_DT_BACK)
                dve.wait_ge(bank_full, f.full)
                dve.wait_ge(rstd_ready, 5)
                dve.wait_ge(ssdc_full, 48)
                for t in range(T):
                    s_ = dve.scalar_tensor_tensor(out=dx[:, t, :], in0=banks[:, f.bank, SHEADS * t:SHEADS * (t + 1)],
                                                  scalar=rstd[:, 4, t:t + 1], in1=dtb_bc, op0=ALU.mult, op1=ALU.add)
                s_.then_inc(consumed[f.bank], 1)
                dve.wait_ge(consumed[f.bank], f.turn + 1)
                dve.scalar_tensor_tensor(out=de, in0=dx, scalar=-1.0, in1=dx, op0=ALU.mult, op1=ALU.max
                                         ).then_inc(dt_abs, 1)

            def dt_chain():
                dve.wait_ge(dt_exp, 1)
                dve.wait_ge(a_exp, 1)
                chained(lambda: dve.tensor_scalar(ds2, de, 2.0, None, ALU.add))
                chained(lambda: dve.reciprocal(ds2, ds2))
                chained(lambda: dve.tensor_tensor(ds_, de, ds2, ALU.mult))
                chained(lambda: dve.tensor_tensor(ds2, ds_, ds_, ALU.mult))
                chained(lambda: dve.tensor_scalar(dp, ds2, 1.0 / 15, None, ALU.mult))
                for k in (13, 11, 9, 7, 5, 3):
                    chained(lambda: dve.scalar_tensor_tensor(out=dp, in0=dp, scalar=1.0 / k, in1=ds2,
                                                             op0=ALU.add, op1=ALU.mult))
                chained(lambda: dve.scalar_tensor_tensor(out=dp, in0=dp, scalar=1.0, in1=ds_,
                                                         op0=ALU.add, op1=ALU.mult))
                chained(lambda: dve.tensor_scalar(dx, dx, 0.0, None, ALU.max))
                chained(lambda: dve.scalar_tensor_tensor(out=dt, in0=dp, scalar=2.0, in1=dx,
                                                         op0=ALU.mult, op1=ALU.add))
                for t in range(T):
                    s_ = dve.scalar_tensor_tensor(out=da[:, t, :], in0=dt[:, t, :], scalar=-1.0, in1=a_bc,
                                                  op0=ALU.mult, op1=ALU.mult)
                s_.then_inc(da_ready, 1)

            def split_da():
                dve.wait_ge(da_hi_ready, 1)
                dve.tensor_tensor(da_lo, da, da_hi.bitcast(F32), ALU.subtract
                                  ).then_inc(da_lo_ready, 1)

            def edge_weights():
                f = Fill(F_DECAY)
                dve.wait_ge(consumed[f.bank], f.turn + 1)
                dve.tensor_tensor(woff, edge[:, 0, :], dt[:, 0, :], ALU.mult).then_inc(woff_ready, 1)

            def conv_columns(k):
                chained(lambda: dve.tensor_copy(
                    gcol, cols[:, COL_CONV:NCOLS].rearrange("p (a k) -> p a k", k=CONV_KT)[:, :, bass.ds(k, 4)]))

            def load_rms_row():
                f = Fill(F_ROW2)
                dve.wait_ge(bank_full, f.full)
                dve.tensor_copy(rms_row[:, :], banks[:, f.bank, 0:SEQ]).then_inc(consumed[f.bank], 1)
                dve.wait_ge(consumed[f.bank], f.turn + 1)

            def before_conv(u, par, turn):
                block_done(u)
                for i in range(2):
                    dve.tensor_tensor(pre[:, i, :].rearrange("p (a n) -> p a n", a=2),
                                      gemm[:, par, i, :].rearrange("p (a n) -> p a n", a=2),
                                      rms_row[:, :].unsqueeze(1).to_broadcast([P, 2, SEQ]), ALU.mult
                                      ).then_inc(drained[par], 2)
                dve.wait_ge(drained[par], turn * 4 + 4)

            def convolve(i, n):
                if not isinstance(n, int) or n > 0:
                    dve.wait_ge(conv_silu, n)
                for kk in range(2):
                    k = 2 * i + kk
                    s = steps.next()
                    dve.tensor_scalar(conv[:, k, :], pre[:, i, SEQ * kk:SEQ * (kk + 1)], gcol[:, 3, k:k + 1],
                                      gcol[:, 4, k:k + 1], ALU.mult, ALU.add).then_inc(dve_step, 1)
                for back in (1, 2, 3):
                    for kk in range(2):
                        k = 2 * i + kk
                        dve.wait_ge(dve_step, s - 1 + kk)
                        i_ = dve.scalar_tensor_tensor(
                            out=conv[:, k, back:SEQ], in0=pre[:, i, SEQ * kk:SEQ * (kk + 1) - back],
                            scalar=gcol[:, 3 - back, k:k + 1], in1=conv[:, k, back:SEQ], op0=ALU.mult, op1=ALU.add)
                        if back < 3:
                            i_.then_inc(dve_step, 1)
                    if back < 3:
                        steps.next()
                        s = steps.next()
                i_.then_inc(conv_done, 1)

            def mask_cb(f):
                dve.wait_ge(bank_full, f.full)
                for i in (0, 1, 2):
                    o, v = cb[:, i, :], banks[:, f.bank, P * i:P * (i + 1)]
                    c_ = dve.tensor_copy(o, v) if i == 1 else dve.tensor_tensor(o, v, upto, ALU.mult)
                c_.then_inc(consumed[f.bank], 1)

            def weigh_scores(f, fcb, i):
                g = f + i
                dve.wait_ge(consumed[g.bank], g.turn + 1)
                if i == 0:
                    dve.wait_ge(consumed[fcb.bank], fcb.turn + 1)
                m4 = mm[:, i, :].rearrange("p (a b) -> p a b", a=4)
                dve.tensor_tensor(m4, m4, cb[:, 2 * (i // 2), :].unsqueeze(1).to_broadcast([P, 4, P]), ALU.mult
                                  ).then_inc(m_done, 1)

            def x_back(f):
                for t in range(T):
                    g = f + t
                    dve.wait_ge(bank_full, g.full)
                    dve.tensor_copy(yy[:, t, :], banks[:, g.bank, :]).then_inc(consumed[g.bank], 1)

            def gather_y(g, f):
                dve.wait_ge(x_ready, g * 5 + 5)
                for t in range(T):
                    fb = f + t
                    dve.wait_ge(bank_full, fb.full)
                    dve.tensor_tensor(yy[:, t, :], banks[:, fb.bank, :], yy[:, t, :], ALU.add
                                      ).then_inc(consumed[fb.bank], 1)
                fb = f + 2
                dve.wait_ge(bank_full, fb.full)
                dve.tensor_tensor(yoff.rearrange("p (a b) -> p a b", a=HPG),
                                  banks[:, fb.bank, :].rearrange("p (a b) -> p a b", a=HPG),
                                  edge[:, 1, bass.ds(g * HPG, HPG)].unsqueeze(2).to_broadcast([P, HPG, HD]),
                                  ALU.mult).then_inc(consumed[fb.bank], 1)

            def group_variance(g):
                dve.wait_ge(squares_done, g * 2 + 42)
                dve.tensor_scalar(group_var[:, :], group_ssq[:, :], 1.0 / NB, RMS_EPS, ALU.mult, ALU.add
                                  ).then_inc(group_var_ready, 1)

            def group_inverse(g):
                dve.wait_ge(group_std_ready, g + 1)
                dve.reciprocal(group_rstd[:, :], group_std[:, :]).then_inc(group_rstd_ready, 1)

            def group_lo(g, f):
                for i in range(2):
                    split_fill(f + i, yt_hi, yt_lo, g * 4 + 2 * i, g * 4 + (COL_SN + 2 * i),
                               yt_hi_ready, g * 2 + (16 + i + 1))

            def conv_unit(u, par, turn, k, n, c0=0, first=()):
                return {c0: list(first) + [lambda: before_conv(u, par, turn), lambda: conv_columns(k)],
                        c0 + 1: [lambda: convolve(0, n)], c0 + 3: [lambda: convolve(1, n)]}

            def bc_conv(k, c0=0, first=()):
                return conv_unit(U_SSD + k, k % 2, B_SSD + k // 2, 32 + 4 * k, 2 * k, c0, first)

            def x_conv(g):
                return conv_unit(g * 2 + (U_SSD + 4), 0, g + (B_SSD + 2), g * 4, g * 2 + 8)

            def merged(*ats):
                out_ = {}
                for at in ats:
                    for c, fs in at.items():
                        out_.setdefault(c, []).extend(fs)
                return out_

            first_unit(2, U_SSD, {0: [dt_lo]})
            spread_rms(4, rms_cols2)
            unit(U_SSD + 1, merged({1: [dt_input], 6: [dt_chain]}, bc_conv(0, 2, [load_rms_row])))
            unit(U_SSD + 2, merged({4: [split_da, edge_weights]}, bc_conv(1)))
            unit(U_SSD + 3, bc_conv(2))
            unit(U_SSD + 4, merged(bc_conv(3), {6: [lambda: mask_cb(Fill(F_G0))]}))
            f0 = Fill(F_G0 + 1)
            unit(U_SSD + 5, merged(x_conv(0), {
                0: [lambda: weigh_scores(f0, Fill(F_G0), 0), lambda: weigh_scores(f0, Fill(F_G0), 1)],
                1: [lambda: weigh_scores(f0, Fill(F_G0), 2), lambda: weigh_scores(f0, Fill(F_G0), 3)],
                7: [lambda: x_back(Fill(F_G0 + 5))]}))
            with dve.Fori(1, GROUPS) as g:
                steps.loop(g - 1, 13)

                def gf(idx):
                    return Fill(F_G1 + idx, (g - 1) * 3)
                u = g * 2 + (U_SSD + 4)
                unit(u, {3: [lambda: gather_y(g - 1, gf(0))],
                         5: [lambda: mask_cb(gf(3))]})
                unit(u + 1, merged(x_conv(g), {
                    0: [lambda: weigh_scores(gf(4), gf(3), 0),
                        lambda: weigh_scores(gf(4), gf(3), 1), lambda: group_variance(g - 1)],
                    1: [lambda: weigh_scores(gf(4), gf(3), 2), lambda: weigh_scores(gf(4), gf(3), 3),
                        lambda: group_inverse(g - 1)],
                    5: [lambda: group_lo(g - 1, gf(8))],
                    7: [lambda: x_back(gf(10))]}))
                steps.end(GROUPS - 1)
            out_projection(U_SSD_OUT, B_SSD_OUT, 3, {
                3: [lambda: gather_y(7, Fill(F_GTAIL))]},
                {0: [lambda: group_variance(7)], 1: [lambda: group_inverse(7)],
                 5: [lambda: group_lo(7, Fill(F_GTAIL + 3))]})
            mlp(3, U_MLP1, B_MLP1)
            post_norm(7)
            for j in range(8):
                residual(7, j)

        @block.gpsimd
        def _(pool):
            steps = pool_steps

            def rotate_add(p, k):
                dst = (qt, kt_)[k]
                for hh in range(2):
                    pool.wait_ge(drained[k], (p * 3 + B_RET) * 4 + 2 * (hh + 1))
                    for i in range(2):
                        pool.tensor_tensor(dst[:, hh, i, :], rot_a[:, hh, SEQ * i:SEQ * (i + 1)],
                                           rot_b[:, hh, SEQ * (1 - i):SEQ * (2 - i)], (ALU.subtract, ALU.add)[i]
                                           ).then_inc(rot_done, 1)

            def heads_scale(p):
                pool.wait_ge(head_rstd_ready, p + 1)
                for i in range(4):
                    if i % 2 == 0:
                        f = Fill(F_RET + 4 + i, p * 3)
                        pool.wait_ge(consumed[f.bank], f.turn + 1)
                        f = f + 1
                        pool.wait_ge(consumed[f.bank], f.turn + 1)
                    y = sg[:, i // 2, i % 2, :]
                    pool.tensor_tensor(y, y, head_rstd[:, i:i + 1].to_broadcast([P, NB]), ALU.mult).then_inc(y_scaled, 1)

            with pool.Fori(0, PAIRS) as p:
                rotate_add(p, 0)
                rotate_add(p, 1)
                for hh in range(2):
                    pool.wait_ge(sd_hi_ready, p * 2 + (hh + 1))
                    pool.tensor_tensor(sd_lo, sd[:, hh, :], sd_hi.bitcast(F32), ALU.subtract
                                       ).then_inc(sd_lo_ready, 1)
                heads_scale(p)

            def residual(k):
                pool.wait_ge(rstd_ready, k + 1)
                for j in range(POOL_FROM, 8):
                    residual_half(pool, k, j, 1)

            def mlp(phase, u0, b0):
                residual(2 * phase - 1)
                pool.memset(acc, 0.0).then_inc(acc_zero, 1)
                with pool.Fori(0, FF_GROUPS) as g:
                    for j in range(4):
                        for i in range(2):
                            pool.wait_ge(drained[j % 2], (g * 4 + (b0 + j // 2)) * 4 + 2 * (i + 1))
                            z = zt[:, j % 2, i, :]
                            pool.tensor_tensor(z, z, z, ALU.mult).then_inc(squared, 1)
                pool.wait_ge(wpost_full, 16 * (phase + 1))
                for d in range(4):
                    for t in range(T):
                        pool.wait_ge(drained[d % 2], (b0 + 14 + d // 2) * 4 + 2 * (t + 1))
                        c = slice(NB * d, NB * (d + 1))
                        pool.tensor_tensor(mw[:, t, c], acc[:, t, c], wpost[:, c], ALU.mult).then_inc(mw_ready, 1)

            mlp(1, U_MLP0, B_MLP0)
            residual(3)

            def copy_bc(g):
                pool.tensor_copy(bcg[:, 0, :], bt[:, g, :])
                pool.tensor_copy(bcg[:, 1, :], ct[:, g, :]).then_inc(bcg_ready, 1)

            def mask_da(g):
                for i in range(4):
                    t, q = i // 2, i % 2
                    for dst, src in ((masked_hi, da_hi), (masked_lo, da_lo)):
                        m_ = pool.tensor_tensor(
                            dst[:, i, :].rearrange("p (a b) -> p a b", a=4),
                            upto.unsqueeze(1).to_broadcast([P, 4, P]),
                            src[:, t, bass.ds(g * HPG + 4 * q, 4)].bitcast(F32).unsqueeze(2).to_broadcast([P, 4, P]),
                            ALU.mult)
                    m_.then_inc(da_masked, 1)

            def x_products(g, back):
                def per_head(v):
                    return v.rearrange("p (a b) -> p a b", a=HPG)

                def head_row(v):
                    return v[:, bass.ds(g * HPG, HPG)].unsqueeze(2).to_broadcast([P, HPG, HD])
                for t in range(T):
                    f = back + t
                    pool.wait_ge(consumed[f.bank], f.turn + 1)
                    pool.tensor_tensor(per_head(xdt[:, t, :]), per_head(yy[:, t, :]), head_row(dt[:, t, :]), ALU.mult
                                       ).then_inc(x_ready, 1)
                pool.tensor_tensor(per_head(xoff), per_head(yy[:, 0, :]), head_row(woff), ALU.mult
                                   ).then_inc(x_ready, 1)
                for t in range(T):
                    pool.tensor_tensor(per_head(yy[:, t, :]), per_head(yy[:, t, :]), head_row(d_bc), ALU.mult
                                       ).then_inc(x_ready, 1)

            def gate(g, f):
                for i in range(3):
                    pool.wait_ge(consumed[(f + i).bank], (f + i).turn + 1)
                n = steps.next()
                pool.tensor_tensor(yy[:, 1, :], yy[:, 1, :], yoff, ALU.add).then_inc(pool_step, 1)
                pool.wait_ge(drained[1], (g + (B_SSD + 2)) * 4 + 4)
                pool.tensor_tensor(yy[:, 0, :], yy[:, 0, :], sz[:, 0, :], ALU.mult).then_inc(gated, 1)
                pool.wait_ge(pool_step, n)
                pool.tensor_tensor(yy[:, 1, :], yy[:, 1, :], sz[:, 1, :], ALU.mult).then_inc(gated, 1)

            def group_scale(g):
                pool.wait_ge(group_rstd_ready, g + 1)
                for t in range(T):
                    pool.tensor_tensor(yy[:, t, :], yy[:, t, :], group_rstd[:, t:t + 1].to_broadcast([P, NB]),
                                       ALU.mult).then_inc(group_scaled, 1)

            pool.wait_ge(da_lo_ready, 1)
            mask_da(0)
            pool.wait_ge(woff_ready, 1)
            pool.wait_ge(conv_silu, 6)
            copy_bc(0)
            pool.wait_ge(conv_silu, 8)
            with pool.Fori(1, GROUPS) as g:
                def gf(idx):
                    return Fill(F_G1 + idx, (g - 1) * 3)
                pool.wait_ge(bank_full, gf(-2).full - 1)
                mask_da(g)
                x_products(g - 1, gf(-2))
                steps.loop(g - 1, 1)
                copy_bc(g)
                gate(g - 1, gf(0))
                steps.end(GROUPS - 1)
                group_scale(g - 1)
            x_products(7, Fill(F_GTAIL - 2))
            gate(7, Fill(F_GTAIL))
            group_scale(7)
            mlp(3, U_MLP1, B_MLP1)
            residual(7)


_INS = ["x", "norm_mix_pre", "norm_mix_post", "norm_ffn_pre", "norm_ffn_post", "ret_w_in", "ret_gn_w", "ret_w_out",
        "ssd_w_in", "ssd_conv_w", "ssd_conv_b", "ssd_dt_bias", "ssd_a_log", "ssd_d", "ssd_norm_w", "ssd_w_out",
        "mlp_w_up", "mlp_w_down"]
_OUTS = [((1, SEQ, D), "float32")]


def _constants():
    f32 = np.float32
    half = DK // 2
    inv_freq = (f32(10000.0) ** (-np.arange(half, dtype=f32) / f32(half))).astype(f32)
    ang = (np.arange(SEQ, dtype=f32)[:, None] * inv_freq[None, :]).astype(np.float64)
    cos, sin = np.cos(ang), np.sin(ang)
    log_gamma = np.log1p(-np.exp2(-5.0 - np.arange(HEADS)))
    n = np.arange(SEQ)
    seen = (n[:, None] // DECAY_CHUNK) <= (n[None, :] // DECAY_CHUNK)
    full = np.exp(np.abs(n[:, None] - n[None, :])[None] * log_gamma[:, None, None]) * seen * DK ** -0.5
    tiles = np.concatenate([full[:, 0:P, :], full[:, P:SEQ, P:SEQ]], axis=2)
    i = np.arange(P)
    masks = np.stack([i[:, None] == i[None, :], i[:, None] <= i[None, :], i[:, None] > i[None, :]], axis=1)
    return {
        "rot_cos": np.ascontiguousarray(cos.T).astype(f32),
        "rot_sin": np.ascontiguousarray(sin.T).astype(f32),
        "ret_decay": np.ascontiguousarray(tiles.transpose(1, 0, 2).reshape(P, -1)).astype(f32),
        "masks": np.ascontiguousarray(masks.reshape(P, -1)).astype(f32),
    }


def kernel(**inputs):
    import numpy as _np
    import concourse.bacc as _bacc
    from concourse import mybir as _mybir
    from concourse.bass_utils import run_bass_kernel_spmd as _run

    nc = _bacc.Bacc("TRN2", target_bir_lowering=False, num_devices=1, dynamic_dma_scratch_size=1024)
    arrays, args = {}, []
    named = [(name, _np.ascontiguousarray(inputs[name])) for name in _INS] + list(_constants().items())
    for name, a in named:
        arrays[f"in_{name}_dram"] = a
        args.append(nc.dram_tensor(f"in_{name}_dram", a.shape, _mybir.dt.from_np(a.dtype), kind="ExternalInput").ap())
    for i, (shape, dtype) in enumerate(_OUTS):
        dt = _mybir.dt.from_np(_np.dtype(dtype))
        args.append(nc.dram_tensor(f"out_{i}_dram", shape, dt, kind="ExternalOutput").ap())
    hybrid_trunk(nc, *args)
    r = _run(nc, [arrays], core_ids=[0])
    got = tuple(r.results[0][f"out_{i}_dram"] for i in range(len(_OUTS)))
    return got[0]
```
